# Optimizing a Trainium2 kernel written in Bass

```python
import math
import jax
import jax.numpy as jnp
from jax import lax
import numpy as np
import jax, jax.numpy as jnp

D_MODEL = 2048
BATCH = 1
SEQ = 256
DEPTH = 1

HEAD_DIM = 128
NSA_HEADS = 8
NSA_KV_HEADS = 2
CMP_LEN = 32
CMP_STRIDE = 16
CMP_HIDDEN = 2 * HEAD_DIM
SEL_BLOCK = 64
SEL_TOP_N = 16
NSA_WINDOW = 512
NSA_Q_CHUNK = 64
SWA_HEADS = 8
SWA_KV_HEADS = 2
SWA_WINDOW = 128
MOBA_HEADS = 8
MOBA_KV_HEADS = 2
MOBA_BLOCK = 256
MOBA_TOP_K = 3
MOBA_Q_CHUNK = 16
BAND_BLOCK = 128
N_BUCKETS = 32
BUCKET_MAX_DIST = 128
TOTAL_HEADS = NSA_HEADS + SWA_HEADS + MOBA_HEADS
N_BRANCHES = 3
MIX_WIDTH = NSA_HEADS * HEAD_DIM
D_FF = 4 * D_MODEL
RMS_EPS = 1e-6
NEG_INF = -1e30
FORCE_SCORE = 1e30
TINY = 1e-30

SPLIT_SIZES = (
    NSA_HEADS * HEAD_DIM,
    NSA_KV_HEADS * HEAD_DIM,
    NSA_KV_HEADS * HEAD_DIM,
    NSA_KV_HEADS * HEAD_DIM,
    NSA_KV_HEADS * HEAD_DIM,
    NSA_KV_HEADS * HEAD_DIM,
    NSA_KV_HEADS * HEAD_DIM,
    NSA_HEADS * 3,
    SWA_HEADS * HEAD_DIM,
    SWA_KV_HEADS * HEAD_DIM,
    SWA_KV_HEADS * HEAD_DIM,
    MOBA_HEADS * HEAD_DIM,
    MOBA_KV_HEADS * HEAD_DIM,
    MOBA_KV_HEADS * HEAD_DIM,
    N_BRANCHES * D_MODEL,
)
SPLIT_POINTS = tuple(int(v) for v in np.cumsum(SPLIT_SIZES)[:-1])
D_IN = sum(SPLIT_SIZES)


def rms_norm(x, gain):
    x32 = x.astype(jnp.float32)
    y = x32 * lax.rsqrt(jnp.mean(x32 * x32, axis=-1, keepdims=True) + RMS_EPS)
    return (y * gain.astype(jnp.float32)).astype(x.dtype)

def t5_bucket(dist):
    n = jnp.maximum(dist, 0)
    exact = N_BUCKETS // 2
    log_ratio = jnp.log(jnp.maximum(n, 1).astype(jnp.float32) / exact) / math.log(BUCKET_MAX_DIST / exact)
    large = jnp.minimum(exact + (log_ratio * (N_BUCKETS - exact)).astype(jnp.int32), N_BUCKETS - 1)
    return jnp.where(n < exact, n, large)

def masked_softmax(logits, mask, sink=None):
    logits = jnp.where(mask, logits, NEG_INF)
    m = jnp.max(logits, axis=-1, keepdims=True)
    if sink is not None:
        m = jnp.maximum(m, sink)
    p = jnp.where(mask, jnp.exp(logits - m), 0.0)
    denom = jnp.sum(p, axis=-1, keepdims=True)
    if sink is not None:
        denom = denom + jnp.exp(sink - m)
    return p / jnp.maximum(denom, TINY)

def split_heads(t, n_heads):
    return t.reshape(t.shape[0], t.shape[1], n_heads, HEAD_DIM)

def banded_attention(q, k, v, bias_tbl, window, sinks=None):
    b, s, h, d = q.shape
    n_kv = k.shape[2]
    g = h // n_kv
    nb = s // BAND_BLOCK
    pad = -(-(window - 1) // BAND_BLOCK) * BAND_BLOCK
    span = BAND_BLOCK + pad
    key_idx = jnp.arange(nb)[:, None] * BAND_BLOCK + jnp.arange(span)[None, :]
    padding = ((0, 0), (pad, 0), (0, 0), (0, 0))
    kp = jnp.pad(k, padding)[:, key_idx]
    vp = jnp.pad(v, padding)[:, key_idx]
    qb = q.reshape(b, nb, BAND_BLOCK, n_kv, g, d)
    logits = jnp.einsum('bnqkgd,bnlkd->bnkgql', qb, kp, preferred_element_type=jnp.float32) * (d ** -0.5)
    dist = (jnp.arange(BAND_BLOCK)[:, None] + pad) - jnp.arange(span)[None, :]
    bias = jnp.transpose(bias_tbl[t5_bucket(dist)], (2, 0, 1)).reshape(n_kv, g, BAND_BLOCK, span)
    logits = logits + bias.astype(jnp.float32)
    mask = ((dist >= 0) & (dist < window))[None] & (key_idx >= pad)[:, None, :]
    mask = mask[None, :, None, None]
    sink = None
    if sinks is not None:
        sink = sinks.astype(jnp.float32).reshape(n_kv, g, 1, 1)
    p = masked_softmax(logits, mask, sink)
    out = jnp.einsum('bnkgql,bnlkd->bnqkgd', p.astype(v.dtype), vp)
    return out.reshape(b, s, h, d)

def nsa_compress(kv, pos_emb, w1, w2):
    b, s, n_kv, d = kv.shape
    n_cmp = (s - CMP_LEN) // CMP_STRIDE + 1
    idx = jnp.arange(n_cmp)[:, None] * CMP_STRIDE + jnp.arange(CMP_LEN)[None, :]
    blocks = kv[:, idx] + pos_emb[None, None, :, None, :]
    blocks = jnp.moveaxis(blocks, 3, 2).reshape(b, n_cmp, n_kv, CMP_LEN * d)
    return jax.nn.gelu(blocks @ w1) @ w2

def selection_weights(n_cmp, n_sel):
    starts = np.arange(n_cmp)[:, None] * CMP_STRIDE
    blk = np.arange(n_sel)[None, :] * SEL_BLOCK
    shared = np.clip(np.minimum(starts + CMP_LEN, blk + SEL_BLOCK) - np.maximum(starts, blk), 0, None)
    return (shared / CMP_STRIDE).astype(np.float32)

def nsa_selected_attention(qg, k_sel, v_sel, sel_idx, bias_tbl):
    b, s, n_kv, g, d = qg.shape
    n_top = sel_idx.shape[-1]
    n_sel = s // SEL_BLOCK
    n_keys = n_top * SEL_BLOCK
    scale = d ** -0.5
    kb = jnp.moveaxis(k_sel.reshape(b, n_sel, SEL_BLOCK, n_kv, d), 3, 1)
    vb = jnp.moveaxis(v_sel.reshape(b, n_sel, SEL_BLOCK, n_kv, d), 3, 1)
    tbl = jnp.moveaxis(bias_tbl.reshape(N_BUCKETS, n_kv, g), 0, 1)
    n_chunk = s // NSA_Q_CHUNK
    q_chunks = jnp.moveaxis(qg.reshape(b, n_chunk, NSA_Q_CHUNK, n_kv, g, d), 1, 0)
    idx_chunks = jnp.moveaxis(sel_idx.reshape(b, n_kv, n_chunk, NSA_Q_CHUNK, n_top), 2, 0)
    starts = jnp.arange(n_chunk) * NSA_Q_CHUNK
    bi = jnp.arange(b)[:, None, None, None]
    kvi = jnp.arange(n_kv)[None, :, None, None]
    pos_in_blk = jnp.arange(SEL_BLOCK)

    def chunk(xs):
        q_c, idx_c, start = xs
        t_c = start + jnp.arange(NSA_Q_CHUNK)
        k_c = kb[bi, kvi, idx_c]
        v_c = vb[bi, kvi, idx_c]
        dist = t_c[:, None, None] - (idx_c[..., None] * SEL_BLOCK + pos_in_blk)
        bias = jnp.moveaxis(tbl[kvi[..., None], t5_bucket(dist)], -1, 2)
        logits = jnp.einsum('bqkgd,bkqnld->bkgqnl', q_c, k_c, preferred_element_type=jnp.float32) * scale + bias
        mask = (dist >= 0)[:, :, None]
        p = masked_softmax(logits.reshape(b, n_kv, g, NSA_Q_CHUNK, n_keys),
                           mask.reshape(b, n_kv, 1, NSA_Q_CHUNK, n_keys))
        return jnp.einsum('bkgqm,bkqmd->bqkgd', p.astype(v_sel.dtype),
                          v_c.reshape(b, n_kv, NSA_Q_CHUNK, n_keys, d))

    out = lax.map(chunk, (q_chunks, idx_chunks, starts))
    return jnp.moveaxis(out, 0, 1).reshape(b, s, n_kv * g, d)

def nsa_attention(q, k_cmp, v_cmp, k_sel, v_sel, k_win, v_win, gate_logits, cmp_pos, cmp_w1, cmp_w2, bias_tbl):
    b, s, h, d = q.shape
    n_kv = k_cmp.shape[2]
    g = h // n_kv
    scale = d ** -0.5
    qg = q.reshape(b, s, n_kv, g, d)
    t = jnp.arange(s)
    kc = nsa_compress(k_cmp, cmp_pos[0], cmp_w1[0], cmp_w2[0])
    vc = nsa_compress(v_cmp, cmp_pos[1], cmp_w1[1], cmp_w2[1])
    n_cmp = kc.shape[1]
    dist_c = t[:, None] - (jnp.arange(n_cmp) * CMP_STRIDE + CMP_LEN - 1)[None, :]
    bias_c = jnp.moveaxis(bias_tbl[t5_bucket(dist_c)], -1, 0).reshape(n_kv, g, s, n_cmp)
    logits_c = jnp.einsum('bskgd,bckd->bkgsc', qg, kc, preferred_element_type=jnp.float32) * scale + bias_c
    p_cmp = masked_softmax(logits_c, dist_c >= 0)
    o_cmp = jnp.einsum('bkgsc,bckd->bskgd', p_cmp.astype(vc.dtype), vc).reshape(b, s, h, d)
    n_sel = s // SEL_BLOCK
    n_top = min(SEL_TOP_N, n_sel)
    share = jnp.asarray(selection_weights(n_cmp, n_sel))
    importance = jnp.einsum('bkgsc,cj->bksj', p_cmp, share)
    blk = jnp.arange(n_sel)[None, :]
    cur = (t // SEL_BLOCK)[:, None]
    forced = (blk == 0) | (blk == cur) | (blk == cur - 1)
    score = jnp.where(forced, FORCE_SCORE, jnp.where(blk <= cur, importance, NEG_INF))
    _, sel_idx = lax.top_k(score, n_top)
    o_sel = nsa_selected_attention(qg, k_sel, v_sel, sel_idx, bias_tbl)
    o_win = banded_attention(q, k_win, v_win, bias_tbl, NSA_WINDOW)
    gate = jax.nn.sigmoid(gate_logits.astype(jnp.float32)).reshape(b, s, h, 3).astype(q.dtype)
    out = gate[..., 0:1] * o_cmp + gate[..., 1:2] * o_sel + gate[..., 2:3] * o_win
    return out.reshape(b, s, h * d)

def moba_attention(q, k, v, bias_tbl):
    b, s, h, d = q.shape
    n_kv = k.shape[2]
    g = h // n_kv
    scale = d ** -0.5
    n_blk = -(-s // MOBA_BLOCK)
    padding = ((0, 0), (0, n_blk * MOBA_BLOCK - s), (0, 0), (0, 0))
    kb = jnp.moveaxis(jnp.pad(k, padding).reshape(b, n_blk, MOBA_BLOCK, n_kv, d), 3, 1)
    vb = jnp.moveaxis(jnp.pad(v, padding).reshape(b, n_blk, MOBA_BLOCK, n_kv, d), 3, 1)
    qg = q.reshape(b, s, n_kv, g, d)
    tbl = jnp.transpose(bias_tbl.reshape(N_BUCKETS, n_kv, g), (1, 2, 0))
    n_top = min(MOBA_TOP_K, n_blk - 1)
    n_chunk = s // MOBA_Q_CHUNK
    q_chunks = jnp.moveaxis(qg.reshape(b, n_chunk, MOBA_Q_CHUNK, n_kv, g, d), 1, 0)
    starts = jnp.arange(n_chunk) * MOBA_Q_CHUNK
    pos_in_blk = jnp.arange(MOBA_BLOCK)
    bi = jnp.arange(b)[:, None, None, None, None]
    kvi = jnp.arange(n_kv)[None, :, None, None, None]
    gi = jnp.arange(g)[None, None, :, None, None]

    def own_block(q_c, start):
        t_c = start + jnp.arange(MOBA_Q_CHUNK)
        blk = start // MOBA_BLOCK
        k_own = lax.dynamic_index_in_dim(kb, blk, axis=2, keepdims=False)
        v_own = lax.dynamic_index_in_dim(vb, blk, axis=2, keepdims=False)
        dist = t_c[:, None] - (blk * MOBA_BLOCK + pos_in_blk)[None, :]
        logits = jnp.einsum('bqkgd,bkld->bkgql', q_c, k_own, preferred_element_type=jnp.float32) * scale
        logits = logits + tbl[:, :, t5_bucket(dist)]
        mask = jnp.broadcast_to(dist >= 0, logits.shape)
        return logits, mask, v_own, t_c

    if n_top > 0:
        t = jnp.arange(s)
        q_blk = t // MOBA_BLOCK
        k_mean = jnp.mean(kb, axis=3)
        gate = jnp.einsum('bskgd,bknd->bkgsn', qg, k_mean, preferred_element_type=jnp.float32)
        gate = jnp.where(jnp.arange(n_blk)[None, :] < q_blk[:, None], gate, NEG_INF)
        _, sel_idx = lax.top_k(gate, n_top)
        valid = sel_idx < q_blk[:, None]
        idx_chunks = jnp.moveaxis(sel_idx.reshape(b, n_kv, g, n_chunk, MOBA_Q_CHUNK, n_top), 3, 0)
        valid_chunks = jnp.moveaxis(valid.reshape(b, n_kv, g, n_chunk, MOBA_Q_CHUNK, n_top), 3, 0)
        n_sel_keys = n_top * MOBA_BLOCK

        def chunk(xs):
            q_c, start, idx_c, valid_c = xs
            logits_own, mask_own, v_own, t_c = own_block(q_c, start)
            k_sel = kb[bi, kvi, idx_c]
            v_sel = vb[bi, kvi, idx_c]
            dist = t_c[:, None, None] - (idx_c[..., None] * MOBA_BLOCK + pos_in_blk)
            bias = tbl[kvi[..., None], gi[..., None], t5_bucket(dist)]
            logits_sel = jnp.einsum('bqkgd,bkgqnld->bkgqnl', q_c, k_sel, preferred_element_type=jnp.float32) * scale + bias
            logits_sel = logits_sel.reshape(b, n_kv, g, MOBA_Q_CHUNK, n_sel_keys)
            mask_sel = jnp.broadcast_to(valid_c[..., None], dist.shape).reshape(logits_sel.shape)
            p = masked_softmax(jnp.concatenate([logits_sel, logits_own], axis=-1),
                               jnp.concatenate([mask_sel, mask_own], axis=-1)).astype(v.dtype)
            o_sel = jnp.einsum('bkgqm,bkgqmd->bqkgd', p[..., :n_sel_keys],
                               v_sel.reshape(b, n_kv, g, MOBA_Q_CHUNK, n_sel_keys, d))
            o_own = jnp.einsum('bkgql,bkld->bqkgd', p[..., n_sel_keys:], v_own)
            return o_sel + o_own

        out = lax.map(chunk, (q_chunks, starts, idx_chunks, valid_chunks))
    else:
        def chunk(xs):
            q_c, start = xs
            logits_own, mask_own, v_own, _ = own_block(q_c, start)
            p = masked_softmax(logits_own, mask_own).astype(v.dtype)
            return jnp.einsum('bkgql,bkld->bqkgd', p, v_own)

        out = lax.map(chunk, (q_chunks, starts))
    return jnp.moveaxis(out, 0, 1).reshape(b, s, h, d)

def first_inputs(seed: int = 0) -> dict:
    key = jax.random.key(seed)
    ks = jax.random.split(key, 14)

    def nrm(k, shape, scale):
        return jax.random.normal(k, shape, jnp.float32) * scale

    out_scale = (2 * DEPTH) ** -0.5
    return {
        'x': nrm(ks[0], (BATCH, SEQ, D_MODEL), 1.0),
        'w_in': nrm(ks[1], (DEPTH, D_MODEL, D_IN), D_MODEL ** -0.5),
        'cmp_pos': nrm(ks[2], (DEPTH, 2, CMP_LEN, HEAD_DIM), 0.1),
        'cmp_w1': nrm(ks[3], (DEPTH, 2, CMP_LEN * HEAD_DIM, CMP_HIDDEN), (CMP_LEN * HEAD_DIM) ** -0.5),
        'cmp_w2': nrm(ks[4], (DEPTH, 2, CMP_HIDDEN, HEAD_DIM), CMP_HIDDEN ** -0.5),
        'swa_sinks': nrm(ks[5], (DEPTH, SWA_HEADS), 1.0),
        'w_branch': nrm(ks[6], (DEPTH, N_BRANCHES, MIX_WIDTH, D_MODEL), MIX_WIDTH ** -0.5),
        'w_out': nrm(ks[7], (DEPTH, D_MODEL, D_MODEL), D_MODEL ** -0.5 * out_scale),
        'w_mlp_in': nrm(ks[8], (DEPTH, D_MODEL, D_FF), D_MODEL ** -0.5),
        'w_mlp_out': nrm(ks[9], (DEPTH, D_FF, D_MODEL), D_FF ** -0.5 * out_scale),
        'norm_mix': 1.0 + nrm(ks[10], (DEPTH, D_MODEL), 0.02),
        'norm_mlp': 1.0 + nrm(ks[11], (DEPTH, D_MODEL), 0.02),
        'norm_final': 1.0 + nrm(ks[12], (D_MODEL,), 0.02),
        'rel_bias': nrm(ks[13], (N_BUCKETS, TOTAL_HEADS), 0.5),
    }

def first_block(x, w_in, cmp_pos, cmp_w1, cmp_w2, swa_sinks, w_branch, w_out, w_mlp_in, w_mlp_out,
              norm_mix, norm_mlp, norm_final, rel_bias):
    b, s, _ = x.shape
    bias_a = rel_bias[:, :NSA_HEADS]
    bias_b = rel_bias[:, NSA_HEADS:NSA_HEADS + SWA_HEADS]
    bias_c = rel_bias[:, NSA_HEADS + SWA_HEADS:]
    for layer in range(DEPTH):
        h = rms_norm(x, norm_mix[layer])
        (a_q, a_kc, a_vc, a_ks, a_vs, a_kw, a_vw, a_gate,
         b_q, b_k, b_v, c_q, c_k, c_v, merge_gate) = jnp.split(h @ w_in[layer], SPLIT_POINTS, axis=-1)
        o_a = nsa_attention(split_heads(a_q, NSA_HEADS),
                            split_heads(a_kc, NSA_KV_HEADS), split_heads(a_vc, NSA_KV_HEADS),
                            split_heads(a_ks, NSA_KV_HEADS), split_heads(a_vs, NSA_KV_HEADS),
                            split_heads(a_kw, NSA_KV_HEADS), split_heads(a_vw, NSA_KV_HEADS),
                            a_gate, cmp_pos[layer], cmp_w1[layer], cmp_w2[layer], bias_a)
        o_b = banded_attention(split_heads(b_q, SWA_HEADS), split_heads(b_k, SWA_KV_HEADS),
                               split_heads(b_v, SWA_KV_HEADS), bias_b, SWA_WINDOW,
                               swa_sinks[layer]).reshape(b, s, MIX_WIDTH)
        o_c = moba_attention(split_heads(c_q, MOBA_HEADS), split_heads(c_k, MOBA_KV_HEADS),
                             split_heads(c_v, MOBA_KV_HEADS), bias_c).reshape(b, s, MIX_WIDTH)
        branches = jnp.stack([o_a, o_b, o_c], axis=2)
        y = jnp.einsum('bsmc,mcd->bsmd', branches, w_branch[layer])
        gate = jax.nn.sigmoid(merge_gate.reshape(b, s, N_BRANCHES, D_MODEL))
        x = x + jnp.sum(gate * y, axis=2) @ w_out[layer]
        h = rms_norm(x, norm_mlp[layer])
        x = x + jnp.square(jax.nn.relu(h @ w_mlp_in[layer])) @ w_mlp_out[layer]
    return rms_norm(x, norm_final)


DEPTH_2 = 2

CHUNK = 64
Q_BLOCK = 128
NORM_EPS = 1e-6

A_HEADS = 8
A_HEAD_DIM = 128
IDX_HEADS = 16
IDX_DIM = 64
TOPK_MAX = 256
POOL_WINDOWS = (2, 4, 8, 16)
POOL_GROUP = 256
POOL_WIDTH = POOL_GROUP * len(POOL_WINDOWS)
C_HEADS = 8
Q_LORA = 512
KV_LORA = 256
QK_NOPE = 128
QK_ROPE = 64
V_HEAD = 128
ROPE_THETA = 10000.0
LRU_WIDTH = 1024
LRU_BLOCKS = 8
LRU_CONV = 4
LRU_C = 8.0
D_FF_2 = 4096
FFN_CONV = 3

A_WIDTH = A_HEADS * A_HEAD_DIM
AB_IN = 3 * A_WIDTH + IDX_HEADS * IDX_DIM + IDX_DIM + IDX_HEADS + POOL_WIDTH
AB_OUT = A_WIDTH + POOL_WIDTH
CD_IN = Q_LORA + KV_LORA + QK_ROPE + 2 * LRU_WIDTH
CD_OUT = C_HEADS * V_HEAD + LRU_WIDTH
N_EVEN = (DEPTH_2 + 1) // 2
N_ODD = DEPTH_2 // 2


def rms_norm_2(x, g):
    xf = x.astype(jnp.float32)
    y = xf * lax.rsqrt(jnp.mean(xf * xf, axis=-1, keepdims=True) + NORM_EPS)
    return (y * g.astype(jnp.float32)).astype(x.dtype)

def causal_dwconv(x, w, b):
    K = w.shape[0]
    T = x.shape[1]
    xp = jnp.pad(x, ((0, 0), (K - 1, 0), (0, 0)))
    y = xp[:, 0:T] * w[0]
    for k in range(1, K):
        y = y + xp[:, k:k + T] * w[k]
    return y + b

def chunk_limit(q_pos):
    return (q_pos // CHUNK + 1) * CHUNK

def rope(x, pos):
    half = x.shape[-1] // 2
    freq = ROPE_THETA ** (-jnp.arange(half, dtype=jnp.float32) / half)
    ang = pos.astype(jnp.float32)[:, :, None, None] * freq
    cos, sin = jnp.cos(ang), jnp.sin(ang)
    xf = x.astype(jnp.float32)
    x1, x2 = xf[..., :half], xf[..., half:]
    return jnp.concatenate([x1 * cos - x2 * sin, x2 * cos + x1 * sin], axis=-1).astype(x.dtype)

def dsa_attention(q, k, v, q_idx, k_idx, w_idx):
    Bsz, T = q.shape[:2]
    k_top = min(TOPK_MAX, T // 4)
    n_blocks = T // Q_BLOCK
    key_pos = jnp.arange(T)
    idx_scale = (IDX_DIM ** -0.5) * (IDX_HEADS ** -0.5)
    att_scale = A_HEAD_DIM ** -0.5

    def block(i):
        start = i * Q_BLOCK
        qb = lax.dynamic_slice_in_dim(q, start, Q_BLOCK, 1)
        qib = lax.dynamic_slice_in_dim(q_idx, start, Q_BLOCK, 1)
        wb = lax.dynamic_slice_in_dim(w_idx, start, Q_BLOCK, 1)
        limit = chunk_limit(start + jnp.arange(Q_BLOCK))
        admissible = key_pos[None, :] < limit[:, None]
        logits = jnp.einsum('bqhd,bsd->bqhs', qib, k_idx, preferred_element_type=jnp.float32)
        score = jnp.einsum('bqhs,bqh->bqs', jax.nn.relu(logits), wb.astype(jnp.float32)) * idx_scale
        score = jnp.where(admissible[None], score, -jnp.inf)
        _, sel = lax.top_k(score, k_top)
        sel_ok = sel < limit[None, :, None]
        k_sel = jax.vmap(lambda kb, ib: kb[ib])(k, sel)
        v_sel = jax.vmap(lambda vb, ib: vb[ib])(v, sel)
        s = jnp.einsum('bqhd,bqkhd->bhqk', qb, k_sel, preferred_element_type=jnp.float32) * att_scale
        s = jnp.where(sel_ok[:, None], s, -jnp.inf)
        p = jax.nn.softmax(s, axis=-1)
        return jnp.einsum('bhqk,bqkhd->bqhd', p.astype(v.dtype), v_sel)

    out = lax.map(block, jnp.arange(n_blocks))
    return jnp.moveaxis(out, 0, 1).reshape(Bsz, T, A_WIDTH)

def multiscale_pool(u, w, b, scale):
    Bsz, T, _ = u.shape
    G = len(POOL_WINDOWS)
    uf = u.reshape(Bsz, T, G, POOL_GROUP).astype(jnp.float32)
    csum = jnp.cumsum(uf, axis=1)
    t = jnp.arange(T)
    outs = []
    for g, win in enumerate(POOL_WINDOWS):
        c = csum[:, :, g]
        c_prev = jnp.pad(c, ((0, 0), (win, 0), (0, 0)))[:, :T]
        count = jnp.minimum(t + 1, win).astype(jnp.float32)[None, :, None]
        outs.append((c - c_prev) / count - uf[:, :, g])
    pooled = jnp.stack(outs, axis=2).astype(u.dtype)
    mixed = jnp.einsum('btgc,gcd->btgd', pooled, w) + b
    return mixed.reshape(Bsz, T, POOL_WIDTH) * scale

def mla_attention(c_q, c_kv, k_rope_in, positions, q_norm_g, w_q_up, kv_norm_g, w_kv_up):
    Bsz, T = c_q.shape[:2]
    q = (rms_norm_2(c_q, q_norm_g) @ w_q_up).reshape(Bsz, T, C_HEADS, QK_NOPE + QK_ROPE)
    kv = (rms_norm_2(c_kv, kv_norm_g) @ w_kv_up).reshape(Bsz, T, C_HEADS, QK_NOPE + V_HEAD)
    q_nope = q[..., :QK_NOPE]
    q_rope = rope(q[..., QK_NOPE:], positions)
    k_nope = kv[..., :QK_NOPE]
    v = kv[..., QK_NOPE:]
    k_rope = rope(k_rope_in[:, :, None, :], positions)[:, :, 0]
    scale = (QK_NOPE + QK_ROPE) ** -0.5
    key_pos = jnp.arange(T)
    n_blocks = T // Q_BLOCK

    def block(i):
        start = i * Q_BLOCK
        qn = lax.dynamic_slice_in_dim(q_nope, start, Q_BLOCK, 1)
        qr = lax.dynamic_slice_in_dim(q_rope, start, Q_BLOCK, 1)
        limit = chunk_limit(start + jnp.arange(Q_BLOCK))
        admissible = key_pos[None, :] < limit[:, None]
        s = (jnp.einsum('bqhd,bshd->bhqs', qn, k_nope, preferred_element_type=jnp.float32)
             + jnp.einsum('bqhr,bsr->bhqs', qr, k_rope, preferred_element_type=jnp.float32)) * scale
        s = jnp.where(admissible[None, None], s, -jnp.inf)
        p = jax.nn.softmax(s, axis=-1)
        return jnp.einsum('bhqs,bshd->bqhd', p.astype(v.dtype), v)

    out = lax.map(block, jnp.arange(n_blocks))
    return jnp.moveaxis(out, 0, 1).reshape(Bsz, T, C_HEADS * V_HEAD)

def rg_lru_branch(x_in, y_in, conv_w, conv_b, wa, ba, wx, bx, lam):
    Bsz, T, _ = x_in.shape
    xc = causal_dwconv(x_in, conv_w, conv_b)
    xb = xc.reshape(Bsz, T, LRU_BLOCKS, LRU_WIDTH // LRU_BLOCKS)
    gate_r = jax.nn.sigmoid(jnp.einsum('btnc,ncd->btnd', xb, wa).reshape(Bsz, T, LRU_WIDTH) + ba)
    gate_i = jax.nn.sigmoid(jnp.einsum('btnc,ncd->btnd', xb, wx).reshape(Bsz, T, LRU_WIDTH) + bx)
    log_a = (-LRU_C * gate_r.astype(jnp.float32)) * jax.nn.softplus(-lam.astype(jnp.float32))
    a = jnp.exp(log_a)
    mult = jnp.sqrt(-jnp.expm1(2.0 * log_a))
    bterm = mult * (gate_i * xc).astype(jnp.float32)

    def combine(lhs, rhs):
        a_l, b_l = lhs
        a_r, b_r = rhs
        return a_l * a_r, a_r * b_l + b_r

    _, h = lax.associative_scan(combine, (a, bterm), axis=1)
    return h.astype(x_in.dtype) * jax.nn.gelu(y_in, approximate=True)

def mixer_ab(h, w_in, pool_w, pool_b, pool_scale, w_out):
    Bsz, T, _ = h.shape
    z = h @ w_in
    sizes = [A_WIDTH, A_WIDTH, A_WIDTH, IDX_HEADS * IDX_DIM, IDX_DIM, IDX_HEADS]
    cuts = [int(c) for c in np.cumsum(sizes)]
    q, k, v, qi, ki, wi, u = jnp.split(z, cuts, axis=-1)
    heads = (Bsz, T, A_HEADS, A_HEAD_DIM)
    a_out = dsa_attention(q.reshape(heads), k.reshape(heads), v.reshape(heads),
                          qi.reshape(Bsz, T, IDX_HEADS, IDX_DIM), ki, wi)
    b_out = multiscale_pool(u, pool_w, pool_b, pool_scale)
    return jnp.concatenate([a_out, b_out], axis=-1) @ w_out

def mixer_cd(h, positions, w_in, q_norm_g, w_q_up, kv_norm_g, w_kv_up,
             conv_w, conv_b, wa, ba, wx, bx, lam, w_out):
    z = h @ w_in
    sizes = [Q_LORA, KV_LORA, QK_ROPE, LRU_WIDTH]
    cuts = [int(c) for c in np.cumsum(sizes)]
    c_q, c_kv, k_rope, x_lru, y_gate = jnp.split(z, cuts, axis=-1)
    c_out = mla_attention(c_q, c_kv, k_rope, positions, q_norm_g, w_q_up, kv_norm_g, w_kv_up)
    d_out = rg_lru_branch(x_lru, y_gate, conv_w, conv_b, wa, ba, wx, bx, lam)
    return jnp.concatenate([c_out, d_out], axis=-1) @ w_out

def channel_mixer(h, up, conv_w, conv_b, down):
    hid = causal_dwconv(h @ up, conv_w, conv_b)
    gate, val = jnp.split(hid, 2, axis=-1)
    return (jax.nn.gelu(gate, approximate=True) * val) @ down

def second_inputs(seed: int = 0) -> dict:
    key = jax.random.key(seed)
    keys = iter(jax.random.split(key, 40))

    def dense(shape, fan_in):
        return jax.random.normal(next(keys), shape, jnp.float32) * (fan_in ** -0.5)

    def gain(shape):
        return 1.0 + 0.05 * jax.random.normal(next(keys), shape, jnp.float32)

    def small(shape, s=0.02):
        return s * jax.random.normal(next(keys), shape, jnp.float32)

    x = jax.random.normal(next(keys), (BATCH, SEQ, D_MODEL), jnp.float32)
    offset = jax.random.randint(next(keys), (BATCH, 1), 0, 64) * CHUNK
    positions = (offset + jnp.arange(SEQ)[None, :]).astype(jnp.int32)
    u = jax.random.uniform(next(keys), (N_ODD, LRU_WIDTH), jnp.float32, 0.9, 0.999)
    s = u ** (1.0 / LRU_C)
    lru_lambda = jnp.log(s) - jnp.log1p(-s)
    bw = LRU_WIDTH // LRU_BLOCKS
    return {
        'x': x,
        'positions': positions,
        'mix_pre_g': gain((DEPTH_2, D_MODEL)),
        'mix_post_g': gain((DEPTH_2, D_MODEL)),
        'ffn_pre_g': gain((DEPTH_2, D_MODEL)),
        'ffn_post_g': gain((DEPTH_2, D_MODEL)),
        'ffn_up': dense((DEPTH_2, D_MODEL, 2 * D_FF_2), D_MODEL),
        'ffn_conv_w': dense((DEPTH_2, FFN_CONV, 2 * D_FF_2), FFN_CONV),
        'ffn_conv_b': small((DEPTH_2, 2 * D_FF_2)),
        'ffn_down': dense((DEPTH_2, D_FF_2, D_MODEL), D_FF_2),
        'ab_w_in': dense((N_EVEN, D_MODEL, AB_IN), D_MODEL),
        'pool_w': dense((N_EVEN, len(POOL_WINDOWS), POOL_GROUP, POOL_GROUP), POOL_GROUP),
        'pool_b': small((N_EVEN, len(POOL_WINDOWS), POOL_GROUP)),
        'pool_scale': 1.0 + 0.1 * jax.random.normal(next(keys), (N_EVEN, POOL_WIDTH), jnp.float32),
        'ab_w_out': dense((N_EVEN, AB_OUT, D_MODEL), AB_OUT),
        'cd_w_in': dense((N_ODD, D_MODEL, CD_IN), D_MODEL),
        'q_norm_g': gain((N_ODD, Q_LORA)),
        'w_q_up': dense((N_ODD, Q_LORA, C_HEADS * (QK_NOPE + QK_ROPE)), Q_LORA),
        'kv_norm_g': gain((N_ODD, KV_LORA)),
        'w_kv_up': dense((N_ODD, KV_LORA, C_HEADS * (QK_NOPE + V_HEAD)), KV_LORA),
        'lru_conv_w': dense((N_ODD, LRU_CONV, LRU_WIDTH), LRU_CONV),
        'lru_conv_b': small((N_ODD, LRU_WIDTH)),
        'lru_wa': dense((N_ODD, LRU_BLOCKS, bw, bw), bw),
        'lru_ba': small((N_ODD, LRU_WIDTH), 0.1),
        'lru_wx': dense((N_ODD, LRU_BLOCKS, bw, bw), bw),
        'lru_bx': small((N_ODD, LRU_WIDTH), 0.1),
        'lru_lambda': lru_lambda,
        'cd_w_out': dense((N_ODD, CD_OUT, D_MODEL), CD_OUT),
    }

def second_block(x, positions, mix_pre_g, mix_post_g, ffn_pre_g, ffn_post_g,
              ffn_up, ffn_conv_w, ffn_conv_b, ffn_down,
              ab_w_in, pool_w, pool_b, pool_scale, ab_w_out,
              cd_w_in, q_norm_g, w_q_up, kv_norm_g, w_kv_up,
              lru_conv_w, lru_conv_b, lru_wa, lru_ba, lru_wx, lru_bx, lru_lambda, cd_w_out):
    for layer in range(DEPTH_2):
        j = layer // 2
        h = rms_norm_2(x, mix_pre_g[layer])
        if layer % 2 == 0:
            m = mixer_ab(h, ab_w_in[j], pool_w[j], pool_b[j], pool_scale[j], ab_w_out[j])
        else:
            m = mixer_cd(h, positions, cd_w_in[j], q_norm_g[j], w_q_up[j], kv_norm_g[j], w_kv_up[j],
                         lru_conv_w[j], lru_conv_b[j], lru_wa[j], lru_ba[j], lru_wx[j], lru_bx[j],
                         lru_lambda[j], cd_w_out[j])
        x = x + rms_norm_2(m, mix_post_g[layer])
        h = rms_norm_2(x, ffn_pre_g[layer])
        f = channel_mixer(h, ffn_up[layer], ffn_conv_w[layer], ffn_conv_b[layer], ffn_down[layer])
        x = x + rms_norm_2(f, ffn_post_g[layer])
    return x


def setup_inputs(seed=0):
    out = dict(first_inputs(seed))
    for name, value in second_inputs(seed + 1).items():
        if name != "x":
            out[name + "_2"] = value
    return out


def reference(
    x, w_in, cmp_pos, cmp_w1, cmp_w2, swa_sinks, w_branch, w_out, w_mlp_in, w_mlp_out, norm_mix,
    norm_mlp, norm_final, rel_bias, positions_2, mix_pre_g_2, mix_post_g_2, ffn_pre_g_2,
    ffn_post_g_2, ffn_up_2, ffn_conv_w_2, ffn_conv_b_2, ffn_down_2, ab_w_in_2, pool_w_2,
    pool_b_2, pool_scale_2, ab_w_out_2, cd_w_in_2, q_norm_g_2, w_q_up_2, kv_norm_g_2, w_kv_up_2,
    lru_conv_w_2, lru_conv_b_2, lru_wa_2, lru_ba_2, lru_wx_2, lru_bx_2, lru_lambda_2,
    cd_w_out_2,
):
    x = first_block(
        x, w_in, cmp_pos, cmp_w1, cmp_w2, swa_sinks, w_branch, w_out, w_mlp_in, w_mlp_out,
        norm_mix, norm_mlp, norm_final, rel_bias,
    )
    return second_block(
        x, positions_2, mix_pre_g_2, mix_post_g_2, ffn_pre_g_2, ffn_post_g_2, ffn_up_2,
        ffn_conv_w_2, ffn_conv_b_2, ffn_down_2, ab_w_in_2, pool_w_2, pool_b_2, pool_scale_2,
        ab_w_out_2, cd_w_in_2, q_norm_g_2, w_q_up_2, kv_norm_g_2, w_kv_up_2, lru_conv_w_2,
        lru_conv_b_2, lru_wa_2, lru_ba_2, lru_wx_2, lru_bx_2, lru_lambda_2, cd_w_out_2,
    )


_drawn_inputs = setup_inputs


def setup_inputs(seed=0):
    import zlib

    import numpy as np

    out = dict(_drawn_inputs(seed))
    spreads = {}
    factors = {'swa_sinks': 4.01,
     'norm_mix': 3.519,
     'q_norm_g_2': 8.0,
     'kv_norm_g_2': 4.335,
     'lru_ba_2': 200.0,
     'lru_bx_2': 153.408,
     'lru_conv_b_2': 64.0,
     'lru_wa_2': 35.768,
     'lru_lambda_2': 26.432,
     'lru_conv_w_2': 8.0,
     'lru_wx_2': 8.0}
    for name, (base, spread) in spreads.items():
        noise = np.random.default_rng([zlib.crc32(name.encode()), seed]).standard_normal(out[name].shape)
        drawn = base * np.exp(spread * noise) if base else spread * noise
        out[name] = jnp.asarray(drawn.astype(out[name].dtype))
    for name, factor in factors.items():
        out[name] = (out[name] * factor).astype(out[name].dtype)
    return out
```

```python
from contextlib import ExitStack

import numpy as np

import concourse.bass as bass
from concourse import mybir

F32 = mybir.dt.float32
F32R = mybir.dt.float32r
I32 = mybir.dt.int32
ALU = mybir.AluOpType
ACT = mybir.ActivationFunctionType
AX = mybir.AxisListType.X

P = 128
TOK = 256
D = 2048
KT = D // P
EPS = 1e-6
NEG = -1e30
TINY = 1e-30
LOWEST = -3.4028234663852886e38

RING = 8
SPLIT = 4
CHUNK = 1024
BW = 512
NCH = 8

HEADS, KV = 8, 2
HD = 128
A_COLS = 2560
GATE_COLS = 24
BC_COLS = 1536
MERGE0 = A_COLS + GATE_COLS + 2 * BC_COLS
N_CMP, CMP_LEN, CMP_STRIDE = 15, 32, 16
D_FF = 8192

AB_Q, AB_QI, AB_KI, AB_U = 0, 3072, 4096, 4176
IDX_HEADS, IDX_DIM, TOPK = 16, 64, 64
POOL_WINDOWS = (2, 4, 8, 16)
CD_KV, CD_X = 512, 832
ROPE = 64
LRU_T = 8
FF2 = 4096

TWO_PI = 2 * np.pi
ROUNDER = 12582912.0
PI_BELOW = 3.1415925
TURN_PARTS = (6.28125, float(np.float32(np.floor((TWO_PI - 6.28125) * 2**21) / 2**21)),)
TURN_PARTS += (float(np.float32(TWO_PI - TURN_PARTS[0] - TURN_PARTS[1])),)

SM = float(HD) ** -0.5
SM_MLA = float(HD + ROPE) ** -0.5


def bucket(dist):
    n = np.maximum(dist, 0)
    ratio = np.log(np.maximum(n, 1).astype(np.float32) / np.float32(16)) / np.float32(np.log(8.0))
    large = np.minimum(16 + (ratio * np.float32(16)).astype(np.int32), 31)
    return np.where(n < 16, n, large)


def shape_tables():
    i = np.arange(P)[:, None]
    t = {"ident": np.eye(P, dtype=np.float32)}
    m = np.arange(384)
    dist = 255 - m
    t["onehot_rev"] = ((bucket(dist)[None, :] == np.arange(32)[:, None]) & (dist >= 0)).astype(np.float32)
    causal = np.where(dist < 0, NEG, 0.0)
    window = np.where((dist < 0) | (dist >= 128), NEG, 0.0)
    t["mask_rev"] = np.stack([causal] * 8 + [window] * 8 + [causal] * 8).astype(np.float32)
    d2 = np.arange(512) - 255
    t["onehot_cmp"] = ((bucket(d2)[None, :] == np.arange(32)[:, None]) & (d2 >= 0)).astype(np.float32)
    dc = np.stack([(P * s + i - (np.arange(N_CMP) * CMP_STRIDE + CMP_LEN - 1)[None, :]) for s in (1, 0)], 1)
    cmask = np.where(dc < 0, NEG, 0.0).reshape(P, 2 * N_CMP)
    valid = (dc >= 0).any(-1).astype(np.float32)
    t["cmp_const"] = np.concatenate([cmask, valid], 1).astype(np.float32)
    k1, k0 = np.arange(256)[None, :], np.arange(128)[None, :]
    ok = np.concatenate([k1 < ((P + i) // 64 + 1) * 64, k0 < (i // 64 + 1) * 64], 1)
    t["chunk_lim"] = np.where(ok, 3e38, -3e38).astype(np.float32)
    t["chunk_mask"] = np.where(ok, 0.0, NEG).astype(np.float32)
    tok = np.arange(TOK)
    t["inv_head"] = np.stack([1.0 / np.minimum(tok[:16] + 1, w) for w in POOL_WINDOWS]).astype(np.float32).reshape(1, 64)
    t["freq"] = (10000.0 ** (-np.arange(32) / 32.0)).astype(np.float32).reshape(1, 32)
    return t


PACK = {}
_at = 0
for _name, _n in (("norm_mix", 16), ("norm_mlp", 16), ("mix_pre", 32), ("ffn_pre", 32), ("q_norm", 4), ("kv_norm", 2),
                  ("pool_b", 8), ("pool_scale", 8), ("lru_w", 32), ("lru_b", 8), ("ba", 8), ("bx", 8), ("lam", 8)):
    PACK[_name] = _at
    _at += _n
PACK_N = _at


def build_program(nc, d):
    with ExitStack() as ctx:
        def sb(name, shape, dt=F32):
            return ctx.enter_context(nc.sbuf_tensor(name, shape, dt))

        def sem(name):
            return ctx.enter_context(nc.semaphore(name))

        xres = sb("xres", [P, 2, D])
        lh = (sb("l_hi", [P, KT, TOK], F32R), sb("l_lo", [P, KT, TOK], F32R))
        mh = (sb("m_hi", [P, KT, TOK], F32R), sb("m_lo", [P, KT, TOK], F32R))
        raw = sb("raw", [P, RING, CHUNK])
        w_hi = sb("w_hi", [P, SPLIT, CHUNK], F32R)
        w_lo = sb("w_lo", [P, SPLIT, CHUNK], F32R)
        ident = sb("ident_sb", [P, P])
        pk = sb("pk_sb", [P, PACK_N])
        st = sb("stats", [P, 128])
        cx_guard = [nc.sbuf_tensor("cx_hi", [P, 8, TOK], F32R), nc.sbuf_tensor("cx_lo", [P, 8, TOK], F32R)]
        cx = tuple(g.__enter__() for g in cx_guard)
        for g in reversed(cx_guard):
            g.__exit__(None, None, None)
        late = sb("late", [P, 4096])
        main = sb("main", [P, 11136])
        ps = ctx.enter_context(nc.psum_tensor("ps", [P, 8, 512], F32))
        scr = nc.dram_tensor("bias_rows", [24, P, 384], F32, kind="Internal").ap()

        def view(tensor, off, *dims):
            n = int(np.prod(dims))
            v = tensor[:, off:off + n]
            if len(dims) == 2:
                v = v.rearrange("p (a b) -> p a b", a=dims[0])
            if len(dims) == 3:
                v = v.rearrange("p (a b c) -> p a b c", a=dims[0], b=dims[1])
            return v

        raw_in = [sem(f"raw_in{i}") for i in range(RING)]
        hi_done, lo_done, chunk_used = sem("hi_done"), sem("lo_done"), sem("chunk_used")
        acc_free = sem("acc_free")
        rows_ready = sem("rows_ready")
        tp_done, thi_done, lhs_ready = sem("tp_done"), sem("thi_done"), sem("lhs_ready")
        x_in = [sem(f"x_in{i}") for i in range(4)]
        small_in, tb_in, scr_st, gain_in = sem("small_in"), sem("tb_in"), sem("scr_st"), sem("gain_in")
        setup_pe, setup_dve = sem("setup_pe"), sem("setup_dve")
        cw_ready, cmp_gelu, cmp_pe, cmp_done = sem("cw_ready"), sem("cmp_gelu"), sem("cmp_pe"), sem("cmp_done")
        merged = sem("merged")
        dve_seq, squares_done, pool_seq, pe_seq = sem("dve_seq"), sem("squares_done"), sem("pool_seq"), sem("pe_seq")
        stat_v, stat_a = sem("stat_v"), sem("stat_a")
        at_t, at_qk, at_s, at_l, at_mx, at_e, at_r, at_p = [sem("at_" + n) for n in ("t", "qk", "s", "l", "mx", "e", "r", "p")]
        at_pt, at_ptc, at_pv, at_pvg, at_ohi, at_o = [sem("at_" + n) for n in ("pt", "ptc", "pv", "pvg", "ohi", "o")]
        out_st, out_ready = sem("out_st"), sem("out_ready")
        pool_pe, pool_dve, pool_act, lru_pe, conv_ready = [sem(n) for n in ("pool_pe", "pool_dve", "pool_act", "lru_pe", "conv_ready")]
        sp_v, sp_a = sem("sp_v"), sem("sp_a")
        ix_rows, ix_t, ix_q, ix_s, ix_r, ix_d = [sem("ix_" + n) for n in ("rows", "t", "q", "s", "r", "d")]
        conv_a, conv_m, hid_hi, hid_ready = [sem(n) for n in ("conv_a", "conv_m", "hid_hi", "hid_ready")]
        aux_in, lru_v, lru_a, lru_p, rope_v, rope_a = [sem(n) for n in ("aux_in", "lru_v", "lru_a", "lru_p", "rope_v", "rope_a")]

        ST = {n: st[:, 2 * i:2 * i + 2] for i, n in enumerate(
            ("mean", "root", "rstd", "mean2", "root2", "rstd2", "rstd12", "rq", "rkv", "tmp0", "tmp1", "tmp2"))}
        ssp = st[:, 24:32].rearrange("p (a b) -> p a b", a=2)
        ssp2 = st[:, 32:40].rearrange("p (a b) -> p a b", a=2)
        at_nmx = [st[:, 40 + 2 * j:42 + 2 * j] for j in range(3)]
        at_sum = [st[:, 46 + 2 * j:48 + 2 * j] for j in range(3)]
        at_den = [st[:, 52 + 2 * j:54 + 2 * j] for j in range(3)]
        at_rec = [st[:, 58 + 2 * j:60 + 2 * j] for j in range(3)]
        at_esk = [st[:, 64 + 2 * j:66 + 2 * j] for j in range(3)]
        sp_m, sp_e, sp_z, sp_t = [st[:, 104 + 8 * j:112 + 8 * j] if j < 3 else st[:, 88:96] for j in range(4)]
        decay = st[:, 72:80]

        tp4 = ps[:, 4:6, :].rearrange("p a (b c) -> p (a b) c", b=2)

        def acc(par, w=BW):
            return ps[:, 2 * par:2 * par + 2, 0:w]

        Z = 0
        zA = view(main, Z, 2, A_COLS)
        zB = view(main, Z, 2, BC_COLS)
        TB0 = 5120
        tb = view(main, TB0, 8, 384)
        T0 = TB0 + 3072
        qk = [main[:, T0 + 512 * j:T0 + 512 * (j + 1)] for j in range(2)]
        pp = [main[:, T0 + 1024 + 384 * j:T0 + 1024 + 384 * (j + 1)] for j in range(3)]
        pt = [main[:, T0 + 2176 + 384 * j:T0 + 2176 + 384 * (j + 1)] for j in range(2)]
        C0 = T0 + 2944
        assert C0 <= 11136
        cst = sb("cst", [P, 48 + 16 + 32 + 240 + 30 + 256 + 8])
        gsb = cst[:, 0:48].rearrange("p (s c) -> p s c", s=2)
        gcm = cst[:, 48:64].rearrange("p (s c) -> p s c", s=2)
        ccon = cst[:, 64:96]
        tbc = cst[:, 96:336].rearrange("p (h c) -> p h c", h=8)
        kct = cst[:, 336:366]
        vc = cst[:, 366:622].rearrange("p (k c) -> p k c", k=2)
        sinkb = cst[:, 622:630]
        nsink = st[:, 96:104]

        TA = {"qk": qk, "pp": pp, "pt": pt, "nsink": nsink}
        mix = view(main, 0, 2, D)
        sg = view(main, 4096, 2, BW)
        ybuf = view(main, 5120, 2, BW)
        hid = view(main, 6144, 2, BW)
        gwide = late[:, 0:D]

        rel_sb = main[0:32, TB0:TB0 + 24]
        oh_rev = main[0:32, TB0 + 24:TB0 + 408]
        oh_cmp = main[0:32, TB0 + 408:TB0 + 920]
        m_rev = main[0:24, TB0 + 920:TB0 + 1304]
        r_rows = main[0:24, TB0 + 1304:TB0 + 1688]
        w2 = view(main, TB0 + 1688, 2, 2, P)
        post = view(main, TB0 + 2200, 2, CMP_LEN)
        hg = view(main, TB0 + 2264, 2, 2, 30)
        cwin = [main[:, T0 + 480 * j:T0 + 480 * (j + 1)] for j in range(4)]
        ch = tuple(m[:, 0:8, :].rearrange("p a b -> p (a b)")[:, 0:1920].rearrange("p (s l c) -> p s l c", s=2, l=32) for m in mh)

        def wait(eng, s, v):
            if not isinstance(v, int) or v > 0:
                eng.wait_ge(s, v)

        def load_chunk(sp, q, k, src):
            n, w = src.shape[1], src.shape[2]
            wait(sp, lo_done, 8 * q + k - RING + 1)
            sp.dma_start(raw[:, k % RING, 0:n * w].rearrange("p (a b) -> p a b", a=n), src).then_inc(raw_in[k % RING], 16)

        def load_block(sp, q, w, row0, col, width=BW, nch=NCH, k0=0, kt=2):
            for c in range(nch):
                rows = w[row0 + P * kt * c:row0 + P * kt * (c + 1), :]
                src = rows[:, bass.ds(col, width)]
                load_chunk(sp, q, k0 + c, src.rearrange("(k p) n -> p k n", p=P))

        def split_hi(act, q, ks):
            for k in ks:
                wait(act, raw_in[k % RING], 16 * (q + k // RING + 1))
                wait(act, chunk_used, 8 * q + k - SPLIT + 1)
                nc.scalar.activation(w_hi[:, k % SPLIT, :], raw[:, k % RING, :], ACT.Copy).then_inc(hi_done, 1)

        def split_lo(dve, q, ks):
            for k in ks:
                dve.wait_ge(hi_done, 8 * q + k + 1)
                nc.vector.tensor_tensor(w_lo[:, k % SPLIT, :], raw[:, k % RING, :], w_hi[:, k % SPLIT, :].bitcast(F32),
                                        ALU.subtract).then_inc(lo_done, 1)

        def mm_chunk(pe, q, k, lhs, kts, out, first, last, w=BW):
            pe.wait_ge(lo_done, 8 * q + k + 1)
            hi = w_hi[:, k % SPLIT, 0:len(kts) * w].rearrange("p (a b) -> p a b", b=w)
            lo = w_lo[:, k % SPLIT, 0:len(kts) * w].rearrange("p (a b) -> p a b", b=w)
            for j, kt in enumerate(kts):
                for tt in range(2):
                    xh = lhs[0][:, kt, tt * P:(tt + 1) * P]
                    xl = lhs[1][:, kt, tt * P:(tt + 1) * P]
                    o = out[:, tt, :]
                    nc.tensor.matmul(o, xh, hi[:, j, :], start=first and j == 0, stop=False)
                    nc.tensor.matmul(o, xh, lo[:, j, :], start=False, stop=False)
                    m = nc.tensor.matmul(o, xl, hi[:, j, :], start=False, stop=last and j == len(kts) - 1)
            m.then_inc(chunk_used, 1)

        def mm_block(pe, q, u, par, lhs, k0=0, nch=NCH, kt0=0, w=BW, hook=None, need=None):
            wait(pe, acc_free, u - 1)
            for c in range(nch):
                if need is not None and c % 2 == 0:
                    pe.wait_ge(need[0], need[1] + c // 2 + 1)
                mm_chunk(pe, q, k0 + c, lhs, (kt0 + 2 * c, kt0 + 2 * c + 1), acc(par, w), c == 0, c == nch - 1, w)
                if c == 1 and hook is not None:
                    hook()

        def turn(pe, t, rows, ready, n=4):
            pe.wait_ge(*ready)
            wait(pe, lhs_ready, t)
            for j in range(n):
                for tt in range(2):
                    m = nc.tensor.transpose(tp4[:, j, tt * P:(tt + 1) * P], rows[:, tt, j * P:(j + 1) * P], ident[:])
            m.then_inc(tp_done, 1)

        def turn_hi(act, t, dst, gain=None, n=4):
            act.wait_ge(tp_done, t + 1)
            if gain is None:
                i = nc.scalar.activation(dst[0], tp4, ACT.Copy)
            else:
                for j in range(n):
                    i = nc.scalar.activation(dst[0][:, j, :], tp4[:, j, :], ACT.Copy, scale=gain[:, j:j + 1])
            i.then_inc(thi_done, 1)

        def turn_lo(dve, t, dst, gain=None, n=4):
            dve.wait_ge(thi_done, t + 1)
            if gain is None:
                i = nc.vector.tensor_tensor(dst[1], tp4, dst[0].bitcast(F32), ALU.subtract)
            else:
                for j in range(n):
                    i = nc.vector.scalar_tensor_tensor(dst[1][:, j, :], tp4[:, j, :], gain[:, j:j + 1],
                                                       dst[0][:, j, :].bitcast(F32), ALU.mult, ALU.subtract)
            i.then_inc(lhs_ready, 1)

        def tiles(lhs, kt):
            return (lhs[0][:, kt:kt + 4, :], lhs[1][:, kt:kt + 4, :])

        def gains(name, layer=0):
            a = PACK[name] + 16 * layer
            return pk[:, a:a + 16]

        class Unit:
            def __init__(self, q, k, v, bias, out, scale=SM, kt=None, gate=None, sink=None, first=True, last=True,
                         w=(256, 128), rope=None):
                self.q, self.k, self.v, self.bias, self.out, self.scale = q, k, v, bias, out, scale
                self.kt, self.gate, self.sink, self.first, self.last, self.w, self.rope = kt, gate, sink, first, last, w, rope

        def head_cols(z, c):
            return [z[:, tt, c:c + HD] for tt in range(2)]

        def units_a():
            us = []
            for h in range(HEADS):
                kv = h // 4
                q = head_cols(zA, HD * h)
                out = (mh[0][:, h, :], mh[1][:, h, :])
                for b, (kc, vcol) in enumerate(((1536, 1792), (2048, 2304))):
                    us.append(Unit(q, head_cols(zA, kc + HD * kv), head_cols(zA, vcol + HD * kv), tb[:, h, :], out,
                                   gate=gsb[:, :, 3 * h + 1 + b], first=b == 0, last=False))
                us.append(Unit(q, None, [vc[0:N_CMP, kv, :]], tbc[:, h, :], out, kt=kct[:, N_CMP * kv:N_CMP * (kv + 1)],
                               gate=gcm[:, :, h], first=False, last=True, w=(N_CMP, N_CMP)))
            return us

        def units_bc(dst, kt0, sinks):
            return [Unit(head_cols(zB, HD * h), head_cols(zB, 1024 + HD * (h // 4)), head_cols(zB, 1280 + HD * (h // 4)),
                         tb[:, h, :], (dst[0][:, kt0 + h, :], dst[1][:, kt0 + h, :]),
                         sink=sinkb[:, h:h + 1] if sinks else None) for h in range(HEADS)]

        def pe_attend(pe, us, n0, g0, T):
            for i in range(len(us) + 4):
                if i < len(us):
                    u = us[i]
                    wait(pe, at_qk, n0 + i - 1)
                    src = list(u.q) + (list(u.k) if u.k else [])
                    for j, a in enumerate(src):
                        m = nc.tensor.transpose(ps[:, (n0 + i) % 2, j * P:(j + 1) * P], a, ident[:])
                    m.then_inc(at_t, 1)
                j = i - 1
                if 0 <= j < len(us):
                    u, n = us[j], n0 + j
                    qs = T["qk"][n % 2]
                    kt = u.kt if u.kt is not None else qs[:, 256:512]
                    pe.wait_ge(at_qk, n + 1)
                    wait(pe, at_l, n - 1)
                    bank = ps[:, 2 + n % 2, :]
                    w1, w0 = u.w
                    for o, tt, w in ((bank[:, 0:w1], 1, w1), (bank[:, w1:w1 + w0], 0, w0)):
                        m = nc.tensor.matmul(o, qs[:, tt * P:(tt + 1) * P], kt[:, 0:w], start=True, stop=u.rope is None)
                        if u.rope is not None:
                            m = nc.tensor.matmul(o, u.rope[0][:, tt * P:(tt + 1) * P], u.rope[1][:, 0:w], start=False, stop=True)
                    m.then_inc(at_s, 1)
                j = i - 3
                if 0 <= j < len(us):
                    u, n = us[j], n0 + j
                    pe.wait_ge(at_p, n + 1)
                    wait(pe, at_ptc, n - 1)
                    p, bank = T["pp"][n % 3], ps[:, 4 + n % 2, :]
                    w1, w0 = u.w
                    nc.tensor.transpose(bank[0:min(w0, P), 0:P], p[:, w1:w1 + w0], ident[:])
                    m = nc.tensor.transpose(bank[0:min(w1, P), P:2 * P], p[:, 0:min(w1, P)], ident[:])
                    if w1 > P:
                        m = nc.tensor.transpose(bank[:, 2 * P:3 * P], p[:, P:2 * P], ident[:])
                    m.then_inc(at_pt, 1)
                j = i - 4
                if 0 <= j < len(us):
                    u, n = us[j], n0 + j
                    g = g0 + sum(x.last for x in us[:j])
                    pe.wait_ge(at_ptc, n + 1)
                    if u.first:
                        wait(pe, at_o, g - 1)
                    o, pts, kk = ps[:, 6 + g % 2, 0:TOK], T["pt"][n % 2], min(u.w[1], P)
                    m = nc.tensor.matmul(o, u.v[0][0:kk, :], pts[0:kk, 0:TOK], start=u.first, stop=u.last and len(u.v) == 1)
                    if len(u.v) == 2:
                        m = nc.tensor.matmul(o[:, P:TOK], u.v[1], pts[:, TOK:TOK + P], start=False, stop=u.last)
                    m.then_inc(at_pv, 1)

        def act_attend(act, us, n0, g0, T):
            ends = [j for j, u in enumerate(us) if u.last]
            for i in range(len(us) + 5):
                j = i - 2
                if 0 <= j < len(us):
                    u, n = us[j], n0 + j
                    act.wait_ge(at_mx, n + 1)
                    w1, w0 = u.w
                    p, nm, sm = T["pp"][n % 3], at_nmx[n % 3], at_sum[n % 3]
                    if u.sink is not None:
                        nc.scalar.activation(at_esk[n % 3], nm, ACT.Exp, bias=u.sink)
                    nc.scalar.activation(p[:, 0:w1], p[:, 0:w1], ACT.Exp, bias=nm[:, 0:1], accum_out=sm[:, 0:1])
                    nc.scalar.activation(p[:, w1:w1 + w0], p[:, w1:w1 + w0], ACT.Exp, bias=nm[:, 1:2],
                                         accum_out=sm[:, 1:2]).then_inc(at_e, 1)
                if i < len(us):
                    u, n = us[i], n0 + i
                    act.wait_ge(at_t, n + 1)
                    wait(act, at_s, n - 1)
                    w = 512 if u.k else 256
                    nc.scalar.activation(T["qk"][n % 2][:, 0:w], ps[:, n % 2, 0:w], ACT.Copy).then_inc(at_qk, 1)
                j = i - 5
                if 0 <= j < len(us) and us[j].last:
                    u, g = us[j], g0 + ends.index(j)
                    act.wait_ge(at_pv, n0 + j + 1)
                    nc.scalar.activation(u.out[0], ps[:, 6 + g % 2, 0:TOK], ACT.Copy).then_inc(at_ohi, 1)

        def dve_attend(dve, us, n0, g0, T, chain):
            ends = [j for j, u in enumerate(us) if u.last]
            for i in range(1, len(us) + 5):
                j = i - 1
                if 0 <= j < len(us):
                    u, n = us[j], n0 + j
                    w1, w0 = u.w
                    p, nm = T["pp"][n % 3], at_nmx[n % 3]
                    dve.wait_ge(at_s, n + 1)
                    wait(dve, at_pt, n - 2)
                    nc.vector.scalar_tensor_tensor(p[:, 0:w1 + w0], ps[:, 2 + n % 2, 0:w1 + w0], u.scale, u.bias,
                                                   ALU.mult, ALU.add).then_inc(at_l, 1)
                    dve.wait_ge(at_l, n + 1)
                    nc.vector.tensor_reduce(nm[:, 0:1], p[:, 0:w1], AX, ALU.max, negate=True)
                    m = nc.vector.tensor_reduce(nm[:, 1:2], p[:, w1:w1 + w0], AX, ALU.max, negate=True)
                    if u.sink is not None:
                        chain(m)
                        m = nc.vector.tensor_scalar(nm, nm, T["nsink"][:, j:j + 1], None, ALU.min)
                    m.then_inc(at_mx, 1)
                j = i - 2
                if 0 <= j < len(us):
                    u, n = us[j], n0 + j
                    den, rec = at_den[n % 3], at_rec[n % 3]
                    dve.wait_ge(at_e, n + 1)
                    if u.sink is not None:
                        chain(nc.vector.tensor_tensor(den, at_sum[n % 3], at_esk[n % 3], ALU.add))
                        chain(nc.vector.tensor_scalar(den, den, TINY, None, ALU.max))
                    else:
                        chain(nc.vector.tensor_scalar(den, at_sum[n % 3], TINY, None, ALU.max))
                    m = nc.vector.reciprocal(rec, den)
                    if u.gate is not None:
                        chain(m)
                        m = nc.vector.tensor_tensor(rec, rec, u.gate, ALU.mult)
                    m.then_inc(at_r, 1)
                j = i - 3
                if 0 <= j < len(us):
                    u, n = us[j], n0 + j
                    dve.wait_ge(at_pt, n + 1)
                    wait(dve, at_pv, n - 1)
                    kk = min(u.w[1], P)
                    w = 384 if u.w[0] > P else 256
                    nc.vector.tensor_copy(T["pt"][n % 2][0:kk, 0:w], ps[0:kk, 4 + n % 2, 0:w]).then_inc(at_ptc, 1)
                j = i - 5
                if 0 <= j < len(us) and us[j].last:
                    u, g = us[j], g0 + ends.index(j)
                    dve.wait_ge(at_ohi, g + 1)
                    nc.vector.tensor_tensor(u.out[1], ps[:, 6 + g % 2, 0:TOK], u.out[0].bitcast(F32),
                                            ALU.subtract).then_inc(at_o, 1)
            g = g0 + len(ends)

        def pool_attend(pool, us, n0, T):
            for j, u in enumerate(us):
                n = n0 + j
                w1, w0 = u.w
                p, rec = T["pp"][n % 3], at_rec[n % 3]
                pool.wait_ge(at_r, n + 1)
                nc.gpsimd.tensor_scalar(p[:, 0:w1], p[:, 0:w1], rec[:, 0:1], None, ALU.mult)
                nc.gpsimd.tensor_scalar(p[:, w1:w1 + w0], p[:, w1:w1 + w0], rec[:, 1:2], None, ALU.mult).then_inc(at_p, 1)


        zab = view(main, 0, 2, 5200)
        TD = {"qk": [late[:, 512 * j:512 * (j + 1)] for j in range(2)],
              "pp": [late[:, 1024 + 384 * j:1408 + 384 * j] for j in range(3)],
              "pt": [late[:, 2176 + 384 * j:2560 + 384 * j] for j in range(2)], "nsink": None}
        PAD = 16
        pu, pa, pb = [view(late, 1088 * j, 4, PAD + TOK) for j in range(3)]
        inv_head = view(late, 3264, 4, PAD)
        score = late[:, 2944:3328]
        relu_h = [late[:, 3328 + 384 * j:3712 + 384 * j] for j in range(2)]
        sel_mask, lim = main[:, 4176:4560], main[:, 4560:4944]
        ki2, kiT = view(main, 10400, 2, P), main[:, 10656:10912]
        wi_s, top1, top0 = main[:, 10912:10944], main[:, 10944:10952], main[:, 10952:10960]
        macc = view(main, 0, 2, D)
        hid2 = view(main, 4096, 2, BW)
        cg, cv = view(main, 5120, 4, TOK), view(main, 6144, 4, TOK)
        fcw, fcb = view(main, 7168, 3, 64), main[:, 7360:7424]
        gpost_ffn = main[:, 7424:7424 + D]
        gpost_mix = late[:, 0:D]
        zc = view(main, 0, 2, CD_X)
        zx, zy = view(main, 1664, 2, 1024), view(main, 3712, 2, 1024)
        rr, ii = view(main, 1664, 8, TOK), view(main, 3712, 8, TOK)
        xin, xc = view(main, 5760, 8, 3 + TOK), view(main, 7832, 8, TOK)
        mul = view(main, 5760, 8, TOK)
        decay_a, gy = view(late, 0, 8, TOK), view(late, 2048, 8, TOK)
        zq, zkv = view(main, 1664, 2, 1536), view(main, 4736, 2, 2048)
        qrow, kr2, krT = view(main, 8832, 2, 8, ROPE), view(main, 9856, 2, P), main[:, 10112:10368]
        qrT = view(late, 2944, 4, TOK)
        cmask2 = main[:, 10752:11136]
        pos_i, pos_f, freq_sb = sb("pos_i", [P, 2], I32), main[:, 10688:10690], main[:, 10690:10722]
        ang, revs, cosv, sinv, half = [view(main, 10368 + 64 * j, 2, 32) for j in range(5)]
        rq1, rq2 = view(late, 0, 2, 8, 32), view(late, 512, 2, 8, 32)

        wi = d["w_in"]
        Q_B, Q_C, Q_M, Q_O, Q_MLP = 8, 11, 14, 32, 36
        U_B, U_C, U_M, U_O, U_MLP = 6, 9, 12, 36, 40
        T_CMP, T_MIX, T_O, T_MLP = 4, 5, 9, 13
        ua = units_a()
        ub = units_bc(mh, 8, True)
        uc = units_bc(cx, 0, False)
        N_B, N_C, N_END = len(ua), len(ua) + 8, len(ua) + 16
        G_B, G_C, G_END = 8, 16, 24
        N_SMALL = 10
        O2, O4 = 2, 4
        Q_AB, Q_ABO, Q_F0, Q_CD, Q_UP, Q_CDO, Q_F1 = 68, 79, 83, 107, 113, 115, 119
        U_AB, U_ABO, U_F0, U_CD, U_UP, U_CDO, U_F1 = 72, 83, 87, 111, 117, 125, 129
        T_X1, T_PU, T_ABX, T_F0, T_FX, T_CD, T_CQ, T_QR, T_CDX, T_F1 = 29, 33, 35, 39, 55, 59, 63, 65, 67, 71

        def conv_tiles(g, j, val):
            return (FF2 * val + D * g + BW * j) // P

        ud = [Unit([zab[:, tt, HD * h:HD * (h + 1)] for tt in range(2)], [zab[:, tt, 1024 + HD * h:1024 + HD * (h + 1)] for tt in range(2)],
                   [zab[:, tt, 2048 + HD * h:2048 + HD * (h + 1)] for tt in range(2)], sel_mask, (mh[0][:, h, :], mh[1][:, h, :]))
              for h in range(HEADS)]
        um = [Unit([zq[:, tt, 192 * h:192 * h + HD] for tt in range(2)], [zkv[:, tt, 256 * h:256 * h + HD] for tt in range(2)],
                   [zkv[:, tt, 256 * h + HD:256 * h + 2 * HD] for tt in range(2)], cmask2, (mh[0][:, h, :], mh[1][:, h, :]), scale=SM_MLA,
                   rope=(qrT[ROPE * (h % 2):ROPE * (h % 2 + 1), h // 2, :], krT[ROPE * (h % 2):ROPE * (h % 2 + 1), :]))
              for h in range(HEADS)]
        X_ROWS = {T_ABX: 16, T_FX: 20, T_CDX: 24}
        N_D, N_L, N_ALL = N_END, N_END + 8, N_END + 16
        G_D, G_L, G_ALL = G_END, G_END + 8, G_END + 16

        block = ctx.enter_context(nc.Block())

        @block.sync
        def _(sp):
            for j in range(4):
                sp.dma_start(xres[:, :, BW * j:BW * (j + 1)],
                             d["x"][:, BW * j:BW * (j + 1)].rearrange("(t p) n -> p t n", p=P)).then_inc(x_in[j], 16)
            for b in range(5):
                load_block(sp, b, wi, 0, BW * b)
            load_block(sp, 5, wi, 0, A_COLS, width=GATE_COLS)
            for s in range(2):
                w1 = d["cmp_w1"][s]
                for c in range(NCH):
                    load_chunk(sp, 6 + s, c, w1[4 * P * c:4 * P * (c + 1), :].rearrange("(k p) n -> p k n", p=P))
            for b in range(6):
                load_block(sp, Q_B + b, wi, 0, A_COLS + GATE_COLS + BW * b)
            for m in range(3):
                with sp.Fori(1, 3) as i:
                    q = Q_M + 6 * m - 3 + 3 * i
                    for e in range(2):
                        load_block(sp, q, wi, 0, MERGE0 + D * m + BW * (e - 2) + 2 * BW * i, k0=12 * e)
                        load_block(sp, q, d["w_branch"][m], 0, BW * (e - 2) + 2 * BW * i, nch=4, k0=12 * e + 8)
            for b in range(4):
                load_block(sp, Q_O + b, d["w_out"], 0, BW * b)
            with sp.Fori(0, 4) as g:
                for b in range(4):
                    load_block(sp, Q_MLP + b + 8 * g, d["w_mlp_in"], 0, BW * b + D * g)
                w_down = d["w_mlp_out"][bass.ds(D * g, D), :]
                for b in range(4):
                    load_block(sp, Q_MLP + 4 + b + 8 * g, w_down, 0, BW * b)
            wab = d["ab_w_in"]
            with sp.Fori(0, 4) as i:
                for e in range(2):
                    load_block(sp, Q_AB + e + 2 * i, wab, 0, BW * e + 2 * BW * i)
            load_block(sp, Q_AB + 8, wab, 0, AB_KI, width=AB_U - AB_KI)
            for b in range(2):
                load_block(sp, Q_AB + 9 + b, wab, 0, AB_U + BW * b)
            for b in range(2):
                load_chunk(sp, Q_ABO, b, d["pool_w"][BW * b:BW * (b + 1), :].rearrange("(k p) n -> p k n", p=P))

            def load_out(q, o, w, used=None):
                for b in range(4):
                    if b == 0 and used is not None:
                        load_block(sp, q, w, 0, 0, k0=o, nch=6)
                        sp.wait_ge(*used)
                        load_block(sp, q, w, 6 * 256, 0, k0=o + 6, nch=2)
                    else:
                        load_block(sp, q + b, w, 0, BW * b, k0=o)

            def load_ffn(q, o, layer):
                up, down = d["ffn_up"][layer], d["ffn_down"][layer]
                for g in range(2):
                    with sp.Fori(0, 4) as j:
                        load_block(sp, q + 12 * g + 2 * j, up, 0, D * g + BW * j, k0=o)
                        load_block(sp, q + 12 * g + 1 + 2 * j, up, 0, FF2 + D * g + BW * j, k0=o)
                    for b in range(4):
                        load_block(sp, q + 12 * g + 8 + b, down, D * g, BW * b, k0=o)

            load_out(Q_ABO, O2, d["ab_w_out"], (pool_pe, 2))
            load_ffn(Q_F0, O2, 0)
            wcd = d["cd_w_in"]
            for b, (c, w) in enumerate(((0, 512), (512, 320), (832, 512), (1344, 512), (1856, 512), (2368, 512))):
                load_block(sp, Q_CD + b, wcd, 0, c, width=w, k0=O2)
            for b, name in enumerate(("lru_wa", "lru_wx")):
                load_chunk(sp, Q_UP, O2 + b, d[name].rearrange("(n p) c -> p n c", p=P))
            for h in range(HEADS):
                if h == 6:
                    sp.wait_ge(lru_pe, 2)
                load_chunk(sp, Q_UP, O4 + h, d["w_q_up"][:, 192 * h:192 * (h + 1)].rearrange("(k p) n -> p k n", p=P))
            for h in range(HEADS):
                load_chunk(sp, Q_UP + 1, O4 + h, d["w_kv_up"][:, 256 * h:256 * (h + 1)].rearrange("(k p) n -> p k n", p=P))
            load_out(Q_CDO, O4, d["cd_w_out"])
            load_ffn(Q_F1, O4, 1)
            for b in range(4):
                sp.wait_ge(out_ready, b + 1)
                sp.dma_start(d["out"][:, BW * b:BW * (b + 1)].rearrange("(t p) n -> p t n", p=P),
                             xres[:, :, BW * b:BW * (b + 1)]).then_inc(out_st, 16)
            sp.wait_ge(out_st, 64)

        @block.gpsimd
        def _(pool):
            pool.dma_start(ident[:], d["ident"]).then_inc(small_in, 16)
            pool.dma_start(pk[:], d["pack"]).then_inc(small_in, 16)
            pool.dma_start(rel_sb, d["rel_bias"]).then_inc(small_in, 16)
            pool.dma_start(oh_rev, d["onehot_rev"]).then_inc(small_in, 16)
            pool.dma_start(oh_cmp, d["onehot_cmp"]).then_inc(small_in, 16)
            pool.dma_start(m_rev, d["mask_rev"]).then_inc(small_in, 16)
            pool.dma_start(ccon, d["cmp_const"]).then_inc(small_in, 16)
            pool.dma_start(post.rearrange("p a b -> p (a b)"), d["cmp_pos"]).then_inc(small_in, 16)
            for s in range(2):
                pool.dma_start(w2[:, s], d["cmp_w2"][s].rearrange("(h p) n -> p h n", p=P)).then_inc(small_in, 16)
            pool.dma_start(sinkb, d["swa_sinks"].to_broadcast([P, HEADS])).then_inc(small_in, 16)

            pool.wait_ge(setup_dve, 1)
            pool.dma_start(scr, r_rows.unsqueeze(1).to_broadcast([24, P, 384])).then_inc(scr_st, 16)
            pool.wait_ge(scr_st, 16)

            def load_bias(h0):
                for a, w, at in ((0, 256, 127), (256, 128, 255)):
                    src = bass.AP(scr.tensor, P * 384 * h0 + at, [[383, P], [P * 384, HEADS], [1, w]])
                    pool.dma_start(tb[:, :, a:a + w], src).then_inc(tb_in, 16)

            pool.wait_ge(cmp_done, 1)
            load_bias(0)
            pool_attend(pool, ua, 0, TA)
            pool.wait_ge(at_l, N_B)
            load_bias(HEADS)
            pool_attend(pool, ub, N_B, TA)
            pool.wait_ge(at_l, N_C)
            load_bias(2 * HEADS)
            pool_attend(pool, uc, N_C, TA)
            pool.sem_inc(merged, 1)
            with pool.Fori(0, 2) as i:
                for e in range(2):
                    pool.wait_ge(acc_free, U_M + 8 + 2 * e + 2 + 4 * i)
                    o = mix[:, :, bass.ds(BW * e + 2 * BW * i, BW)]
                    nc.gpsimd.tensor_tensor(o, o, ybuf, ALU.add).then_inc(merged, 1)
            for n in range(4):
                pool.wait_ge(acc_free, U_M + 16 + 2 * n + 2)
                o = mix[:, :, BW * n:BW * (n + 1)]
                nc.gpsimd.tensor_tensor(o, o, ybuf, ALU.add).then_inc(merged, 1)
            pool.wait_ge(chunk_used, 8 * Q_O)
            pool.dma_start(gwide, d["norm_final"].to_broadcast([P, D])).then_inc(gain_in, 16)
            pool.wait_ge(gain_in, 16)
            for b in range(4):
                pool.wait_ge(squares_done, 16 + 4 * b + 2)
                o = xres[:, :, BW * b:BW * (b + 1)]
                g = gwide[:, BW * b:BW * (b + 1)].unsqueeze(1).to_broadcast([P, 2, BW])
                nc.gpsimd.tensor_tensor(o, o, g, ALU.mult).then_inc(merged, 1)
            def scaled_out(squares0, gwide, gains_in):
                pool.wait_ge(*gains_in)
                for b in range(4):
                    pool.wait_ge(squares_done, squares0 + 2 * b + 2)
                    o = macc[:, :, BW * b:BW * (b + 1)]
                    g = gwide[:, BW * b:BW * (b + 1)].unsqueeze(1).to_broadcast([P, 2, BW])
                    nc.gpsimd.tensor_tensor(o, o, g, ALU.mult).then_inc(merged, 1)

            def load_mixer_end(layer):
                pool.wait_ge(at_o, G_L if layer == 0 else G_ALL)
                pool.wait_ge(at_pv, N_L if layer == 0 else N_ALL)
                pool.dma_start(gpost_mix, d["mix_post"][layer:layer + 1, :].to_broadcast([P, D])).then_inc(gain_in, 16)
                pool.dma_start(gpost_ffn, d["ffn_post"][layer:layer + 1, :].to_broadcast([P, D])).then_inc(gain_in, 16)
                pool.dma_start(fcw.rearrange("p a b -> p (a b)"), d["ffn_conv_w"][layer]).then_inc(gain_in, 16)
                pool.dma_start(fcb, d["ffn_conv_b"][layer]).then_inc(gain_in, 16)

            pool.wait_ge(merged, 13)
            nc.gpsimd.memset(late[:, 0:3264], 0.0).then_inc(pool_seq, 1)
            pool.dma_start(inv_head.rearrange("p a b -> p (a b)"), d["inv_head"].to_broadcast([P, 64])).then_inc(aux_in, 16)
            pool.wait_ge(pool_dve, 4)
            pool.dma_start(lim, d["chunk_lim"]).then_inc(aux_in, 16)
            pool_attend(pool, ud, N_D, TD)
            load_mixer_end(0)
            scaled_out(32, gpost_mix, (gain_in, 16 * 5))
            scaled_out(48, gpost_ffn, (gain_in, 16 * 5))
            pool.wait_ge(lru_a, 2)
            nc.gpsimd.tensor_tensor(ii, ii, xc, ALU.mult).then_inc(lru_p, 1)
            pool.wait_ge(lru_v, 4)
            pool.dma_start(cmask2, d["chunk_mask"]).then_inc(aux_in, 16)
            pool.dma_start(pos_i[:], d["positions"]).then_inc(aux_in, 16)
            pool.dma_start(freq_sb, d["freq"].to_broadcast([P, 32])).then_inc(aux_in, 16)
            pool_attend(pool, um, N_L, TD)
            load_mixer_end(1)
            scaled_out(68, gpost_mix, (gain_in, 16 * 9))
            scaled_out(84, gpost_ffn, (gain_in, 16 * 9))

        @block.tensor
        def _(pe):
            pe.wait_ge(small_in, 16 * (N_SMALL + 1))
            nc.tensor.matmul(ps[0:24, 0, 0:384], rel_sb, oh_rev, start=True, stop=True)
            cb = ps[:, 1, 0:240].rearrange("p (h s c) -> p h s c", h=8, s=2)
            for s in range(2):
                for c in range(N_CMP):
                    a = 255 + P * (1 - s) - CMP_STRIDE * c - (CMP_LEN - 1)
                    m = nc.tensor.matmul(cb[:, :, s, c], oh_cmp[:, a:a + P], rel_sb[:, 0:HEADS], start=True, stop=True)
            m.then_inc(setup_pe, 1)
            for j in range(4):
                turn(pe, j, xres[:, :, BW * j:BW * (j + 1)], (x_in[j], 16))
            pe.wait_ge(setup_dve, 2)
            for b in range(6):
                mm_block(pe, b, b, b % 2, lh, w=BW if b < 5 else GATE_COLS, need=(lhs_ready, 0) if b == 0 else None)
            turn(pe, T_CMP, zA[:, :, 1024:1536], (acc_free, 6))
            pe.wait_ge(lhs_ready, T_CMP + 1)
            for s in range(2):
                for c in range(NCH):
                    k = 8 * s + c
                    pe.wait_ge(lo_done, 48 + k + 1)
                    whi = w_hi[:, k % SPLIT, :].rearrange("p (a h b) -> p a h b", a=4, h=2)
                    wlo = w_lo[:, k % SPLIT, :].rearrange("p (a h b) -> p a h b", a=4, h=2)
                    for j in range(4):
                        l = 4 * c + j
                        for h in range(2):
                            o = ps[:, 2 * s + h, 0:30]
                            nc.tensor.matmul(o, whi[:, j, h, :], ch[0][:, s, l, :], start=l == 0, stop=False)
                            nc.tensor.matmul(o, whi[:, j, h, :], ch[1][:, s, l, :], start=False, stop=False)
                            m = nc.tensor.matmul(o, wlo[:, j, h, :], ch[0][:, s, l, :], start=False, stop=l == CMP_LEN - 1)
                    m.then_inc(chunk_used, 1)
            pe.wait_ge(cmp_gelu, 1)
            for h in range(2):
                nc.tensor.matmul(ps[:, 4, 0:30], w2[:, 0, h, :], hg[:, 0, h, :], start=h == 0, stop=h == 1)
            for kv in range(KV):
                for h in range(2):
                    m = nc.tensor.matmul(ps[0:N_CMP, 5 + kv, 0:P], hg[:, 1, h, N_CMP * kv:N_CMP * (kv + 1)], w2[:, 1, h, :],
                                         start=h == 0, stop=h == 1)
            m.then_inc(cmp_pe, 1)
            pe.wait_ge(cmp_done, 1)
            pe_attend(pe, ua, 0, 0, TA)
            for us, q, u, n, g, nn in ((ub, Q_B, U_B, N_B, G_B, N_B), (uc, Q_C, U_C, N_C, G_C, N_C)):
                pe.wait_ge(at_qk, nn)
                pe.wait_ge(at_l, nn)
                for b in range(3):
                    mm_block(pe, q + b, u + b, (u + b) % 2, lh)
                pe.wait_ge(acc_free, u + 3)
                pe_attend(pe, us, n, g, TA)
            pe.wait_ge(at_qk, N_END)
            pe.wait_ge(at_l, N_END)
            for m in range(2):
                with pe.Fori(0, 2) as i:
                    for e in range(2):
                        q, u = Q_M + 6 * m + 3 * i, U_M + 8 * m + 2 * e + 4 * i
                        mm_block(pe, q, u, 0, lh, k0=12 * e)
                        mm_block(pe, q, u + 1, 1, mh, k0=12 * e + 8, nch=4, kt0=8 * m)
            for n in range(4):
                q, u = Q_M + 12 + 3 * (n // 2), U_M + 16 + 2 * n
                hook = None
                if n > 0:
                    def hook(n=n):
                        turn(pe, T_MIX + n - 1, mix[:, :, BW * (n - 1):BW * n], (merged, 5 + n))
                mm_block(pe, q, u, 0, lh, k0=12 * (n % 2), hook=hook)
                if n == 0:
                    pe.wait_ge(at_o, G_END)
                mm_block(pe, q, u + 1, 1, cx, k0=12 * (n % 2) + 8, nch=4)
            for b in range(4):
                def hook(b=b):
                    if b == 0:
                        turn(pe, T_MIX + 3, mix[:, :, 3 * BW:4 * BW], (merged, 9))
                    else:
                        turn(pe, T_O + b - 1, xres[:, :, BW * (b - 1):BW * b], (acc_free, U_O + b))
                mm_block(pe, Q_O + b, U_O + b, b % 2, mh, need=(lhs_ready, T_MIX) if b == 0 else None, hook=hook)

            def mlp_group(q, u, t, r, first=False, last=False):
                for b in range(4):
                    hook = None
                    if b > 0:
                        def hook(b=b):
                            turn(pe, t + b - 1, hid, (rows_ready, r + b))
                    elif first:
                        def hook():
                            turn(pe, T_O + 3, xres[:, :, 3 * BW:4 * BW], (acc_free, U_O + 4))
                    mm_block(pe, q + b, u + b, b % 2, lh, need=(lhs_ready, T_O) if first and b == 0 else None, hook=hook)
                for b in range(4):
                    hook = None
                    if b == 0:
                        def hook():
                            turn(pe, t + 3, hid, (rows_ready, r + 4))
                    elif last:
                        def hook(b=b):
                            turn(pe, t + 3 + b, xres[:, :, BW * (b - 1):BW * b], (merged, 9 + b))
                    mm_block(pe, q + 4 + b, u + 4 + b, b % 2, mh, need=(lhs_ready, t) if b == 0 else None, hook=hook)

            mlp_group(Q_MLP, U_MLP, T_MLP, 0, first=True)
            with pe.Fori(1, 3) as g:
                mlp_group(Q_MLP + 8 * g, U_MLP + 8 * g, T_MLP + 4 * g, 4 * g)
            mlp_group(Q_MLP + 24, U_MLP + 24, T_MLP + 12, 12, last=True)
            def last_turn():
                turn(pe, T_X1 + 3, xres[:, :, 3 * BW:4 * BW], (merged, 13))

            for b in range(2):
                mm_block(pe, Q_AB + b, U_AB + b, b, lh, need=(lhs_ready, T_X1) if b == 0 else None, hook=last_turn if b == 0 else None)
            with pe.Fori(1, 4) as i:
                for e in range(2):
                    mm_block(pe, Q_AB + e + 2 * i, U_AB + e + 2 * i, e, lh)
            for b in range(8, 11):
                mm_block(pe, Q_AB + b, U_AB + b, b % 2, lh, w=AB_U - AB_KI if b == 8 else BW)

            for b in range(2):
                turn(pe, T_PU + b, zab[:, :, AB_U + BW * b:AB_U + BW * (b + 1)], (acc_free, U_AB + 11))
            for b in range(2):
                pe.wait_ge(pool_dve, 1 + 3 * b)
                pe.wait_ge(raw_in[b], 16 * (Q_ABO + 1))
                pe.wait_ge(lo_done, 8 * Q_ABO + b + 1)
                pw = raw[:, b, :].rearrange("p (k c) -> p k c", k=4)
                for j in range(4):
                    o = ps[:, 2 * b:2 * b + 2, :].rearrange("p a (b c) -> p (a b) c", b=2)[:, j, :]
                    for c in range(2):
                        m = nc.tensor.matmul(o, pw[:, 2 * (j // 2) + c, P * (j % 2):P * (j % 2 + 1)],
                                             pu[:, 2 * (j // 2) + c, PAD:],
                                             start=c == 0, stop=c == 1)
                m.then_inc(pool_pe, 1)
                pe.sem_inc(chunk_used, 1)
            pe.wait_ge(ix_rows, 1)
            pe.wait_ge(pool_act, 2)
            pe.wait_ge(pool_dve, 6)
            pe.wait_ge(lhs_ready, T_PU + 2)
            for tt in range(2):
                m = nc.tensor.transpose(ps[:, 4, tt * P:(tt + 1) * P], ki2[:, tt, :], ident[:])
            m.then_inc(ix_t, 1)
            for p in range(IDX_HEADS // 2 + 1):
                if p < IDX_HEADS // 2:
                    wait(pe, ix_q, p)
                    for tt in range(2):
                        m = nc.tensor.transpose(ps[:, p % 2, tt * P:(tt + 1) * P], zab[:, tt, AB_QI + P * p:AB_QI + P * (p + 1)], ident[:])
                    m.then_inc(ix_t, 1)
                if p > 0:
                    pe.wait_ge(ix_q, p + 1)
                    for e in range(2):
                        h = 2 * (p - 1) + e
                        wait(pe, ix_r, h - 1)
                        r = slice(IDX_DIM * e, IDX_DIM * (e + 1))
                        qs = TD["qk"][(p - 1) % 2][r, :]
                        nc.tensor.matmul(ps[:, 2 + e, 0:256], qs[:, P:2 * P], kiT[r, :], start=True, stop=True)
                        nc.tensor.matmul(ps[:, 2 + e, 256:384], qs[:, 0:P], kiT[r, 0:P], start=True, stop=True).then_inc(ix_s, 1)
            pe.wait_ge(ix_r, IDX_HEADS)
            pe_attend(pe, ud, N_D, G_D, TD)

            def mixer_out(q, o, u, other, n, g, x_t):
                pe.wait_ge(at_qk, n)
                pe.wait_ge(at_l, n)
                for b in range(4):
                    if b == 0:
                        pe.wait_ge(at_ptc, n)
                        pe.wait_ge(at_o, g)
                        pe.wait_ge(*other)
                    mm_block(pe, q + b, u + b, (u + b) % 2, mh, k0=o)
                new_x(x_t)

            def new_x(x_t):
                for b in range(4):
                    turn(pe, x_t + b, xres[:, :, BW * b:BW * (b + 1)], (rows_ready, X_ROWS[x_t] + b + 1))

            def ffn(q, o, u, t, x_t, h):
                for g in range(2):
                    def pair(j, first=False):
                        def before():
                            turn(pe, t + 8 * g + 2 * j - 1, hid2, (acc_free, u + 12 * g + 2 * j))

                        def mine():
                            turn(pe, t + 8 * g + 2 * j, hid2, (acc_free, u + 12 * g + 2 * j + 1))
                        mm_block(pe, q + 12 * g + 2 * j, u + 12 * g + 2 * j, 0 if u % 2 == 0 else 1, lh, k0=o,
                                 need=(lhs_ready, x_t) if first and g == 0 else None, hook=None if first else before)
                        mm_block(pe, q + 12 * g + 2 * j + 1, u + 12 * g + 2 * j + 1, 1 if u % 2 == 0 else 0, lh, k0=o, hook=mine)
                    pair(0, first=True)
                    with pe.Fori(1, 4) as j:
                        pair(j)
                    for b in range(4):
                        def last():
                            turn(pe, t + 8 * g + 7, hid2, (acc_free, u + 12 * g + 8))
                        mm_block(pe, q + 12 * g + 8 + b, u + 12 * g + 8 + b, (u + b) % 2, mh, k0=o,
                                 need=(hid_ready, h + 4 * g) if b == 0 else None, hook=last if b == 0 else None)

            mixer_out(Q_ABO, O2, U_ABO, (pool_dve, 6), N_L, G_L, T_ABX)
            ffn(Q_F0, O2, U_F0, T_F0, T_ABX, 0)
            new_x(T_FX)
            for b in range(6):
                mm_block(pe, Q_CD + b, U_CD + b, (U_CD + b) % 2, lh, k0=O2, w=320 if b == 1 else BW, need=(lhs_ready, T_FX) if b == 0 else None)
            for b in range(4):
                z, c = (zx, BW * b) if b < 2 else (zy, BW * (b - 2))
                turn(pe, T_CD + b, z[:, :, c:c + BW], (acc_free, U_CD + 6))
            turn(pe, T_CQ, zc[:, :, 0:BW], (acc_free, U_CD + 6))
            turn(pe, T_CQ + 1, zc[:, :, BW:BW + 256], (acc_free, U_CD + 6), n=2)
            pe.wait_ge(lhs_ready, T_CQ + 2)
            pe.wait_ge(squares_done, 68)
            pe.wait_ge(lru_v, 1)
            for x in range(2):
                pe.wait_ge(raw_in[(O2 + x) % RING], 16 * (Q_UP + 1))
                pe.wait_ge(lo_done, 8 * Q_UP + O2 + x + 1)
                lw = raw[:, (O2 + x) % RING, :].rearrange("p (n c) -> p n c", n=LRU_T)
                for n in range(LRU_T):
                    m = nc.tensor.matmul(ps[:, 4 * x + n // 2, TOK * (n % 2):TOK * (n % 2 + 1)], lw[:, n, :], xc[:, n, :],
                                         start=True, stop=True)
                m.then_inc(lru_pe, 1)
                pe.sem_inc(chunk_used, 1)
            pe.wait_ge(lru_a, 2)
            for x, (kts, w) in enumerate((((0, 1, 2, 3), 192), ((4, 5), 256))):
                for h in range(HEADS):
                    u = U_UP + 4 * x + h // 2
                    if h % 2 == 0:
                        pe.wait_ge(acc_free, u - 1)
                    mm_chunk(pe, Q_UP + x, O4 + h, lh, kts, ps[:, 2 * (u % 2):2 * (u % 2) + 2, w * (h % 2):w * (h % 2 + 1)], True, True, w)
            turn(pe, T_QR, kr2, (rope_v, 2), n=1)
            turn(pe, T_QR + 1, qrow.rearrange("p t h c -> p t (h c)"), (rope_v, 3))
            pe.wait_ge(lhs_ready, T_QR + 2)
            pe.wait_ge(acc_free, U_UP + 8)
            pe_attend(pe, um, N_L, G_L, TD)
            mixer_out(Q_CDO, O4, U_CDO, (lru_v, 4), N_ALL, G_ALL, T_CDX)
            ffn(Q_F1, O4, U_F1, T_F1, T_CDX, 8)

        @block.scalar
        def _(act):
            aseq = [0]

            def squares(rows, col, sums):
                for tt in range(2):
                    wait(act, squares_done, aseq[0] - 1)
                    aseq[0] += 1
                    i = nc.scalar.activation(ps[:, 6 + tt, 0:rows.shape[2]], rows[:, tt, :], ACT.Square,
                                             accum_out=sums[:, tt, col:col + 1]).then_inc(squares_done, 1)

            def root(k, out, mean):
                act.wait_ge(stat_v, 2 * k + 1)
                nc.scalar.activation(out, mean, ACT.Sqrt).then_inc(stat_a, 1)

            def scaled(b, u, used, dst, scale, par, w=BW, func=ACT.Copy):
                act.wait_ge(chunk_used, used)
                for tt in range(2):
                    i = nc.scalar.activation(dst(tt), acc(par, w)[:, tt, :], func, scale=scale[:, tt:tt + 1])
                i.then_inc(acc_free, 1)

            split_hi(act, 0, range(0, 4))
            act.wait_ge(small_in, 16 * (N_SMALL + 1))
            act.wait_ge(sp_v, 1)
            nc.scalar.activation(sp_e, sp_t, ACT.Exp).then_inc(sp_a, 1)
            for j in range(4):
                turn_hi(act, j, tiles(lh, 4 * j), gains("norm_mix")[:, 4 * j:4 * j + 4])
                squares(xres[:, :, BW * j:BW * (j + 1)], j, ssp)
            root(0, ST["root"], ST["mean"])
            split_hi(act, 0, (4, 5))
            act.wait_ge(stat_v, 2)
            for b in range(6):
                split_hi(act, b, range(6, 12))
                if b < 5:
                    scaled(b, b, 8 * b + 8, lambda tt, b=b: zA[:, tt, BW * b:BW * (b + 1)], ST["rstd"], b % 2)
                    split_hi(act, b, (12, 13))
                else:
                    scaled(b, b, 48, lambda tt: gsb[:, 1 - tt, :], ST["rstd"], 1, w=GATE_COLS, func=ACT.Sigmoid)
            act.wait_ge(cw_ready, 1)
            for x in range(4):
                i = nc.scalar.activation(ch[0][:, x // 2, :, N_CMP * (x % 2):N_CMP * (x % 2 + 1)],
                                         cwin[x].rearrange("p (l c) -> p l c", l=CMP_LEN), ACT.Copy)
            i.then_inc(thi_done, 1)
            split_hi(act, 6, range(4, 20))
            act.wait_ge(chunk_used, 64)
            nc.scalar.activation(hg.rearrange("p a b c -> p (a b) c"), ps[:, 0:4, 0:30], ACT.Gelu_apprx_tanh).then_inc(cmp_gelu, 1)
            act_attend(act, ua, 0, 0, TA)
            for us, q, u, n, g in ((ub, Q_B, U_B, N_B, G_B), (uc, Q_C, U_C, N_C, G_C)):
                split_hi(act, q, (4, 5))
                for b in range(3):
                    split_hi(act, q + b, range(6, 12))
                    scaled(b, u + b, 8 * (q + b) + 8, lambda tt, b=b: zB[:, tt, BW * b:BW * (b + 1)], ST["rstd"], (u + b) % 2)
                    if b < 2:
                        split_hi(act, q + b, (12, 13))
                act_attend(act, us, n, g, TA)
            split_hi(act, Q_M, (4, 5))

            def gate_unit(q, e, u):
                split_hi(act, q, range(12 * e + 6, 12 * e + 12))
                act.wait_ge(acc_free, u)
                scaled(0, u, 8 * q + 12 * e + 8, lambda tt: sg[:, tt, :], ST["rstd"], 0, func=ACT.Sigmoid)
                split_hi(act, q, range(12 * e + 12, 12 * e + 18))

            for m in range(2):
                with act.Fori(0, 2) as i:
                    for e in range(2):
                        gate_unit(Q_M + 6 * m + 3 * i, e, U_M + 8 * m + 2 * e + 4 * i)
            for n in range(4):
                gate_unit(Q_M + 12 + 3 * (n // 2), n % 2, U_M + 16 + 2 * n)
                turn_hi(act, T_MIX + n, tiles(mh, 4 * n))
            for b in range(4):
                split_hi(act, Q_O + b, range(6, 12))
                act.wait_ge(acc_free, U_O + b + 1)
                squares(xres[:, :, BW * b:BW * (b + 1)], b, ssp)
                split_hi(act, Q_O + b, (12, 13))
                turn_hi(act, T_O + b, tiles(lh, 4 * b), gains("norm_mlp")[:, 4 * b:4 * b + 4])
            root(1, ST["root"], ST["mean"])
            act.wait_ge(stat_v, 4)

            def mlp_group(q, u, t, last=False):
                for b in range(4):
                    split_hi(act, q + b, range(6, 12))
                    wait(act, tp_done, t + b)
                    scaled(b, u + b, 8 * (q + b) + 8, lambda tt: hid[:, tt, :], ST["rstd"], b % 2, func=ACT.Relu)
                    split_hi(act, q + b, (12, 13))
                    turn_hi(act, t + b, tiles(mh, 4 * b))
                for b in range(4):
                    split_hi(act, q + 4 + b, range(6, 12))
                    if last:
                        act.wait_ge(acc_free, u + 5 + b)
                        squares(xres[:, :, BW * b:BW * (b + 1)], b, ssp)
                    split_hi(act, q + 4 + b, (12, 13))
                    if last:
                        turn_hi(act, t + 4 + b, tiles(lh, 4 * b), gains("mix_pre")[:, 4 * b:4 * b + 4])
                        squares(xres[:, :, BW * b:BW * (b + 1)], b, ssp2)

            with act.Fori(0, 3) as g:
                mlp_group(Q_MLP + 8 * g, U_MLP + 8 * g, T_MLP + 4 * g)
            mlp_group(Q_MLP + 24, U_MLP + 24, T_MLP + 12, last=True)
            root(2, ST["root"], ST["mean"])
            root(3, ST["root2"], ST["mean2"])
            act.wait_ge(stat_v, 8)
            with act.Fori(0, 4) as i:
                for e in range(2):
                    q = Q_AB + e + 2 * i
                    split_hi(act, q, range(6, 12))
                    scaled(0, 0, 8 * q + 8, lambda tt: zab[:, tt, bass.ds(BW * e + 2 * BW * i, BW)], ST["rstd12"], e)
                    split_hi(act, q, (12, 13))
            for b in range(8, 11):
                split_hi(act, Q_AB + b, range(6, 12))
                c, w = (AB_KI, AB_U - AB_KI) if b == 8 else (AB_U + BW * (b - 9), BW)
                scaled(b, 0, 8 * (Q_AB + b) + 8, lambda tt: zab[:, tt, c:c + w], ST["rstd12"], b % 2, w=w)
                if b < 10:
                    split_hi(act, Q_AB + b, (12, 13))
            act.wait_ge(pool_seq, 1)
            act.wait_ge(tp_done, T_PU + 1)
            nc.scalar.activation(pu[:, :, PAD:], tp4, ACT.Copy).then_inc(thi_done, 1)
            act.wait_ge(tp_done, T_PU + 2)
            act.wait_ge(pool_pe, 1)
            nc.scalar.activation(pu[:, :, PAD:], tp4, ACT.Copy).then_inc(thi_done, 1)
            for b in range(2):
                act.wait_ge(pool_dve, 2 + 3 * b)
                nc.scalar.activation(mh[0][:, 8 + 4 * b:12 + 4 * b, :], pb[:, :, PAD:], ACT.Copy).then_inc(pool_act, 1)
            act.wait_ge(ix_t, 1)
            nc.scalar.activation(kiT, ps[:, 4, 0:TOK], ACT.Copy).then_inc(ix_q, 1)
            for p in range(IDX_HEADS // 2 + 1):
                if p < IDX_HEADS // 2:
                    act.wait_ge(ix_t, p + 2)
                    wait(act, ix_s, 2 * (p - 1))
                    nc.scalar.activation(TD["qk"][p % 2][:, 0:TOK], ps[:, p % 2, 0:TOK], ACT.Copy).then_inc(ix_q, 1)
                if p > 0:
                    for e in range(2):
                        h = 2 * (p - 1) + e
                        act.wait_ge(ix_s, h + 1)
                        wait(act, ix_d, h - 1)
                        nc.scalar.activation(relu_h[e], ps[:, 2 + e, 0:384], ACT.Relu).then_inc(ix_r, 1)
            act_attend(act, ud, N_D, G_D, TD)

            def mixer_out(q, o, u, k, t, done, gain):
                split_hi(act, q, range(done, o + 6))
                for b in range(4):
                    split_hi(act, q + b, range(o + 6, o + 12))
                    act.wait_ge(acc_free, u + b + 1)
                    squares(macc[:, :, BW * b:BW * (b + 1)], b, ssp)
                    if b < 3:
                        split_hi(act, q + b, (o + 12, o + 13))
                new_x(k, t, gain)

            def new_x(k, t, gain):
                root(k, ST["root"], ST["mean"])
                for b in range(4):
                    turn_hi(act, t + b, tiles(lh, 4 * b), gain[:, 4 * b:4 * b + 4])
                    squares(xres[:, :, BW * b:BW * (b + 1)], b, ssp)
                root(k + 1, ST["root"], ST["mean"])
                act.wait_ge(stat_v, 2 * k + 4)

            def ffn(q, o, u, t, c0, layer, end):
                split_hi(act, q, range(o + 4, o + 8))
                act.wait_ge(gain_in, 16 * (5 + 4 * layer))
                for g in range(2):
                    for j in range(4):
                        for val in range(2):
                            b = 12 * g + 2 * j + val
                            tn = t + 8 * g + 2 * j + val
                            cn = c0 + 8 * g + 2 * j + val
                            split_hi(act, q + b, range(o + 8, o + 12))
                            wait(act, tp_done, tn)
                            scaled(0, 0, 8 * (q + b) + o + 8, lambda tt: hid2[:, tt, :], ST["rstd"], (u + b) % 2)
                            if val:
                                act.wait_ge(lhs_ready, tn)
                                nc.scalar.activation(cg, cg, ACT.Gelu_apprx_tanh).then_inc(conv_m, 1)
                            split_hi(act, q + b, (o + 12, o + 13))
                            act.wait_ge(tp_done, tn + 1)
                            if not val:
                                wait(act, hid_ready, 8 * layer + 4 * g + j)
                            dst = cv if val else cg
                            for x in range(4):
                                k = conv_tiles(g, j, val) + x
                                i = nc.scalar.activation(dst[:, x, :], tp4[:, x, :], ACT.Identity, scale=fcw[:, 2, k:k + 1], bias=fcb[:, k:k + 1])
                            i.then_inc(thi_done, 1)
                            split_hi(act, q + b, (o + 14, o + 15))
                            if val:
                                n = (cn + 1) // 2
                                act.wait_ge(conv_ready, n)
                                nc.scalar.activation(mh[0][:, 4 * j:4 * j + 4, :], cg, ACT.Copy).then_inc(hid_hi, 1)
                    for b in range(4):
                        x = q + 12 * g + 8 + b
                        if not (end and g == 1 and b == 3):
                            split_hi(act, x, range(o + 8, o + 12))
                        if g == 1:
                            act.wait_ge(acc_free, u + 12 * g + 9 + b)
                            squares(macc[:, :, BW * b:BW * (b + 1)], b, ssp)
                        if g == 0 or b < 3:
                            split_hi(act, x, range(o + 12, o + 16))

            mixer_out(Q_ABO, O2, U_ABO, 4, T_ABX, 4, gains("ffn_pre"))
            ffn(Q_F0, O2, U_F0, T_F0, 0, 0, False)
            new_x(6, T_FX, gains("mix_pre", 1))
            split_hi(act, Q_CD, (O2 + 4, O2 + 5))
            for b in range(6):
                split_hi(act, Q_CD + b, range(O2 + 6, O2 + 12))
                dst = (lambda tt: zc[:, tt, 0:512], lambda tt: zc[:, tt, 512:832], lambda tt: zx[:, tt, 0:512], lambda tt: zx[:, tt, 512:],
                       lambda tt: zy[:, tt, 0:512], lambda tt: zy[:, tt, 512:])[b]
                scaled(0, 0, 8 * (Q_CD + b) + O2 + 8, dst, ST["rstd"], (U_CD + b) % 2, w=320 if b == 1 else BW)
                if b < 5:
                    split_hi(act, Q_CD + b, (O2 + 12, O2 + 13))
            for b in range(2):
                act.wait_ge(tp_done, T_CD + b + 1)
                nc.scalar.activation(xin[:, 4 * b:4 * b + 4, 3:], tp4, ACT.Copy).then_inc(thi_done, 1)
            for b in range(2):
                act.wait_ge(tp_done, T_CD + b + 3)
                nc.scalar.activation(gy[:, 4 * b:4 * b + 4, :], tp4, ACT.Gelu_apprx_tanh).then_inc(thi_done, 1)
            turn_hi(act, T_CQ, tiles(lh, 0), pk[:, PACK["q_norm"]:PACK["q_norm"] + 4])
            turn_hi(act, T_CQ + 1, tiles(lh, 4), pk[:, PACK["kv_norm"]:PACK["kv_norm"] + 2], n=2)
            squares(zc[:, :, 0:512], 0, ssp)
            squares(zc[:, :, 512:768], 1, ssp)
            act.wait_ge(stat_v, 17)
            nc.scalar.activation(ST["root"], ST["mean"], ACT.Sqrt)
            nc.scalar.activation(ST["root2"], ST["mean2"], ACT.Sqrt).then_inc(stat_a, 1)
            for x, (dst, bias) in enumerate(((rr, "ba"), (ii, "bx"))):
                act.wait_ge(lru_pe, x + 1)
                for n in range(LRU_T):
                    i = nc.scalar.activation(dst[:, n, :], ps[:, 4 * x + n // 2, TOK * (n % 2):TOK * (n % 2 + 1)], ACT.Sigmoid,
                                             bias=pk[:, PACK[bias] + n:PACK[bias] + n + 1])
                i.then_inc(lru_a, 1)
            act.wait_ge(lru_a, 1)
            for n in range(LRU_T):
                i = nc.scalar.activation(decay_a[:, n, :], rr[:, n, :], ACT.Exp, scale=decay[:, n:n + 1])
            i.then_inc(lru_a, 1)
            act.wait_ge(lru_a, 3)
            for n in range(LRU_T):
                i = nc.scalar.activation(rr[:, n, :], rr[:, n, :], ACT.Tanh, scale=decay[:, n:n + 1])
            i.then_inc(lru_a, 1)
            act.wait_ge(lru_v, 2)
            nc.scalar.activation(mul, mul, ACT.Sqrt, scale=-1.0).then_inc(lru_a, 1)
            act.wait_ge(lru_v, 3)
            nc.scalar.activation(mh[0][:, 8:16, :], xc, ACT.Copy).then_inc(lru_a, 1)
            act.wait_ge(stat_v, 18)
            act.wait_ge(lru_v, 4)
            split_hi(act, Q_UP, range(O2 + 4, O4 + 6))
            for j in range(8):
                if j > 0:
                    split_hi(act, Q_UP, (O4 + 2 * j + 4, O4 + 2 * j + 5))
                x = j // 4
                w = 384 if x == 0 else 512
                z = zq if x == 0 else zkv
                scaled(0, 0, 8 * Q_UP + O4 + 2 * j + 2, lambda tt: z[:, tt, w * (j % 4):w * (j % 4 + 1)],
                       ST["rq"] if x == 0 else ST["rkv"], (U_UP + j) % 2, w=w)
            act.wait_ge(rope_v, 1)
            nc.scalar.activation(sinv, ang, ACT.Sin)
            nc.scalar.activation(half, ang, ACT.Sin, scale=0.5).then_inc(rope_a, 1)
            act.wait_ge(tp_done, T_QR + 1)
            nc.scalar.activation(krT, tp4[:, 0, :], ACT.Copy).then_inc(thi_done, 1)
            act.wait_ge(tp_done, T_QR + 2)
            nc.scalar.activation(qrT, tp4, ACT.Copy).then_inc(thi_done, 1)
            act_attend(act, um, N_L, G_L, TD)
            mixer_out(Q_CDO, O4, U_CDO, 9, T_CDX, O4 + 4, gains("ffn_pre", 1))
            ffn(Q_F1, O4, U_F1, T_F1, 16, 1, True)
            root(11, ST["root"], ST["mean"])

        @block.vector
        def _(dve):
            seq = [0]

            def chain(i):
                seq[0] += 1
                i.then_inc(dve_seq, 1)
                dve.wait_ge(dve_seq, seq[0])

            def mean_square(n, out, sums, width=D):
                dve.wait_ge(squares_done, n)
                chain(nc.vector.tensor_reduce(out, sums, AX, ALU.add))
                nc.vector.tensor_scalar(out, out, 1.0 / width, EPS, ALU.mult, ALU.add).then_inc(stat_v, 1)

            def inverse(k, out, rt):
                dve.wait_ge(stat_a, k + 1)
                nc.vector.reciprocal(out, rt).then_inc(stat_v, 1)

            dve.wait_ge(setup_pe, 1)
            nc.vector.tensor_tensor(r_rows, ps[0:24, 0, 0:384], m_rev, ALU.add).then_inc(setup_dve, 1)
            nc.vector.tensor_tensor(tbc, ps[:, 1, 0:240].rearrange("p (h c) -> p h c", h=8),
                                    ccon[:, 0:30].unsqueeze(1).to_broadcast([P, 8, 30]), ALU.add)
            nc.vector.tensor_scalar(nsink, sinkb, -1.0, None, ALU.mult).then_inc(setup_dve, 1)
            lam = pk[:, PACK["lam"]:PACK["lam"] + 8]
            nc.vector.tensor_scalar(sp_m, lam, -1.0, 0.0, ALU.mult, ALU.max)
            nc.vector.scalar_tensor_tensor(sp_t, lam, -1.0, lam, ALU.mult, ALU.min).then_inc(sp_v, 1)
            dve.wait_ge(sp_a, 1)
            chain(nc.vector.tensor_scalar(sp_t, sp_e, 2.0, None, ALU.add))
            chain(nc.vector.reciprocal(sp_z, sp_t))
            chain(nc.vector.tensor_tensor(sp_z, sp_z, sp_e, ALU.mult))
            chain(nc.vector.tensor_tensor(sp_e, sp_z, sp_z, ALU.mult))
            chain(nc.vector.tensor_scalar(sp_t, sp_e, 1.0 / 15, None, ALU.mult))
            for n in (13, 11, 9, 7, 5, 3):
                chain(nc.vector.scalar_tensor_tensor(sp_t, sp_t, 1.0 / n, sp_e, ALU.add, ALU.mult))
            chain(nc.vector.scalar_tensor_tensor(sp_t, sp_t, 1.0, sp_z, ALU.add, ALU.mult))
            chain(nc.vector.scalar_tensor_tensor(sp_t, sp_t, 2.0, sp_m, ALU.mult, ALU.add))
            nc.vector.tensor_scalar(decay, sp_t, -8.0, None, ALU.mult)
            split_lo(dve, 0, range(0, 4))
            for j in range(4):
                turn_lo(dve, j, tiles(lh, 4 * j), gains("norm_mix")[:, 4 * j:4 * j + 4])
            mean_square(8, ST["mean"], ssp)
            inverse(0, ST["rstd"], ST["root"])
            split_lo(dve, 0, (4, 5))
            for b in range(6):
                split_lo(dve, b, range(6, 14 if b < 5 else 12))
            dve.wait_ge(acc_free, 6)
            nc.vector.tensor_tensor(gcm, gsb.rearrange("p s (h b) -> p s h b", b=3)[:, :, :, 0],
                                    ccon[:, 30:32].unsqueeze(2).to_broadcast([P, 2, 8]), ALU.mult)
            dve.wait_ge(tp_done, T_CMP + 1)
            for x in range(4):
                a = tp4[:, x, 0:1]
                win = bass.AP(a.tensor, a.offset, [a.ap[0], [1, CMP_LEN], [CMP_STRIDE, N_CMP]])
                i = nc.vector.tensor_tensor(cwin[x].rearrange("p (l c) -> p l c", l=CMP_LEN), win,
                                            post[:, x // 2, :].unsqueeze(2).to_broadcast([P, CMP_LEN, N_CMP]), ALU.add)
            i.then_inc(cw_ready, 1)
            dve.wait_ge(thi_done, T_CMP + 1)
            for x in range(4):
                s = slice(N_CMP * (x % 2), N_CMP * (x % 2 + 1))
                i = nc.vector.tensor_tensor(ch[1][:, x // 2, :, s], cwin[x].rearrange("p (l c) -> p l c", l=CMP_LEN),
                                            ch[0][:, x // 2, :, s].bitcast(F32), ALU.subtract)
            i.then_inc(lhs_ready, 1)
            split_lo(dve, 6, range(4, 20))
            dve.wait_ge(cmp_pe, 1)
            nc.vector.tensor_copy(kct, ps[:, 4, 0:30])
            nc.vector.tensor_copy(vc[0:N_CMP, :, :], ps[0:N_CMP, 5:7, 0:P]).then_inc(cmp_done, 1)
            dve.wait_ge(tb_in, 32)
            dve_attend(dve, ua, 0, 0, TA, chain)
            for us, q, u, n, g, x in ((ub, Q_B, U_B, N_B, G_B, 2), (uc, Q_C, U_C, N_C, G_C, 3)):
                split_lo(dve, q, range(4, 28))
                dve.wait_ge(tb_in, 32 * x)
                dve_attend(dve, us, n, g, TA, chain)
            split_lo(dve, Q_M, (4, 5))

            def branch_unit(q, e, u, dst, merges=None):
                split_lo(dve, q, range(12 * e + 6, 12 * e + 16))
                dve.wait_ge(chunk_used, 8 * q + 12 * e + 12)
                dve.wait_ge(acc_free, u)
                if merges is not None:
                    wait(dve, merged, merges)
                nc.vector.tensor_tensor(dst, sg, acc(1), ALU.mult).then_inc(acc_free, 1)
                split_lo(dve, q, (12 * e + 16, 12 * e + 17))

            with dve.Fori(0, 2) as i:
                for e in range(2):
                    branch_unit(Q_M + 3 * i, e, U_M + 2 * e + 1 + 4 * i, mix[:, :, bass.ds(BW * e + 2 * BW * i, BW)])
            with dve.Fori(0, 2) as i:
                for e in range(2):
                    branch_unit(Q_M + 6 + 3 * i, e, U_M + 8 + 2 * e + 1 + 4 * i, ybuf, merges=2 * i + e + 1)
            for n in range(4):
                branch_unit(Q_M + 12 + 3 * (n // 2), n % 2, U_M + 16 + 2 * n + 1, ybuf, merges=5 + n)
                turn_lo(dve, T_MIX + n, tiles(mh, 4 * n))

            def add_x(q, u, b):
                dve.wait_ge(chunk_used, 8 * q + 8)
                dve.wait_ge(acc_free, u)
                o = xres[:, :, BW * b:BW * (b + 1)]
                nc.vector.tensor_tensor(o, acc(b % 2), o, ALU.add).then_inc(acc_free, 1)

            for b in range(4):
                split_lo(dve, Q_O + b, range(6, 12))
                add_x(Q_O + b, U_O + b, b)
                split_lo(dve, Q_O + b, (12, 13))
                if b == 3:
                    mean_square(16, ST["mean"], ssp)
                turn_lo(dve, T_O + b, tiles(lh, 4 * b), gains("norm_mlp")[:, 4 * b:4 * b + 4])
            inverse(1, ST["rstd"], ST["root"])

            def mlp_group(q, u, t, last=False):
                for b in range(4):
                    split_lo(dve, q + b, range(6, 12))
                    dve.wait_ge(acc_free, u + b + 1)
                    nc.vector.tensor_tensor(hid, hid, hid, ALU.mult).then_inc(rows_ready, 1)
                    split_lo(dve, q + b, (12, 13))
                    turn_lo(dve, t + b, tiles(mh, 4 * b))
                for b in range(4):
                    split_lo(dve, q + 4 + b, range(6, 12))
                    add_x(q + 4 + b, u + 4 + b, b)
                    split_lo(dve, q + 4 + b, (12, 13))
                    if last:
                        turn_lo(dve, t + 4 + b, tiles(lh, 4 * b), gains("mix_pre")[:, 4 * b:4 * b + 4])

            with dve.Fori(0, 3) as g:
                mlp_group(Q_MLP + 8 * g, U_MLP + 8 * g, T_MLP + 4 * g)
            mlp_group(Q_MLP + 24, U_MLP + 24, T_MLP + 12, last=True)
            mean_square(32, ST["mean"], ssp)
            inverse(2, ST["rstd"], ST["root"])
            dve.wait_ge(squares_done, 32)
            chain(nc.vector.tensor_reduce(ST["tmp0"], ssp2, AX, ALU.add))
            dve.wait_ge(stat_v, 6)
            chain(nc.vector.tensor_tensor(ST["tmp1"], ST["rstd"], ST["rstd"], ALU.mult))
            chain(nc.vector.tensor_tensor(ST["tmp0"], ST["tmp0"], ST["tmp1"], ALU.mult))
            nc.vector.tensor_scalar(ST["mean2"], ST["tmp0"], 1.0 / D, EPS, ALU.mult, ALU.add).then_inc(stat_v, 1)
            dve.wait_ge(stat_a, 4)
            chain(nc.vector.reciprocal(ST["rstd2"], ST["root2"]))
            nc.vector.tensor_tensor(ST["rstd12"], ST["rstd"], ST["rstd2"], ALU.mult).then_inc(stat_v, 1)
            split_lo(dve, Q_AB, range(6, 14))
            dve.wait_ge(tp_done, T_X1 + 4)
            for tt in range(2):
                nc.vector.tensor_scalar(xres[:, tt, :], xres[:, tt, :], ST["rstd"][:, tt:tt + 1], None, ALU.mult)
            for b in range(1, 11):
                split_lo(dve, Q_AB + b, range(6, 14 if b < 10 else 12))
            dve.wait_ge(acc_free, U_AB + 11)
            nc.vector.tensor_copy(ki2.rearrange("p t (a c) -> p t a c", a=2),
                                  zab[:, :, AB_KI:AB_KI + IDX_DIM].unsqueeze(2).to_broadcast([P, 2, 2, IDX_DIM]))
            nc.vector.tensor_scalar(wi_s.rearrange("p (t h) -> p t h", t=2), zab[:, :, AB_KI + IDX_DIM:AB_U],
                                    float(IDX_DIM * IDX_HEADS) ** -0.5, None, ALU.mult).then_inc(ix_rows, 1)
            dve.wait_ge(aux_in, 16)
            for b in range(2):
                dve.wait_ge(thi_done, T_PU + b + 1)
                dve.sem_inc(lhs_ready, 1)
                S = slice(PAD, PAD + TOK)

                def doubled(dst, src, n, tl):
                    chain(nc.vector.tensor_tensor(dst[:, tl:, S], src[:, tl:, S], src[:, tl:, PAD - n:PAD + TOK - n], ALU.add))

                def pooled(sums, g):
                    x = slice(2 * (g % 2), 2 * (g % 2) + 2)
                    chain(nc.vector.scalar_tensor_tensor(pu[:, x, 2 * PAD:], sums[:, x, 2 * PAD:], 1.0 / POOL_WINDOWS[g],
                                                         pu[:, x, 2 * PAD:], ALU.mult, ALU.subtract))
                    h = slice(PAD, 2 * PAD)
                    chain(nc.vector.tensor_tensor(sums[:, x, h], sums[:, x, h],
                                                  inv_head[:, g:g + 1, :].to_broadcast([P, 2, PAD]), ALU.mult))
                    return nc.vector.tensor_tensor(pu[:, x, h], sums[:, x, h], pu[:, x, h], ALU.subtract)

                doubled(pa, pu, 1, 0)
                if b == 0:
                    doubled(pb, pa, 2, 2)
                else:
                    doubled(pb, pa, 2, 0)
                    doubled(pa, pb, 4, 0)
                    doubled(pb, pa, 8, 2)
                pooled(pa, 2 * b)
                pooled(pb, 2 * b + 1).then_inc(pool_dve, 1)
                dve.wait_ge(pool_pe, b + 1)
                tp = ps[:, 2 * b:2 * b + 2, :].rearrange("p a (b c) -> p (a b) c", b=2)
                for j in range(4):
                    c = 4 * b + j
                    i = nc.vector.tensor_scalar(pb[:, j, PAD:], tp[:, j, :], pk[:, PACK["pool_b"] + c:PACK["pool_b"] + c + 1],
                                                pk[:, PACK["pool_scale"] + c:PACK["pool_scale"] + c + 1], ALU.add, ALU.mult)
                i.then_inc(pool_dve, 1)
                dve.wait_ge(pool_act, b + 1)
                nc.vector.tensor_tensor(mh[1][:, 8 + 4 * b:12 + 4 * b, :], pb[:, :, PAD:],
                                        mh[0][:, 8 + 4 * b:12 + 4 * b, :].bitcast(F32), ALU.subtract).then_inc(pool_dve, 1)
            for h in range(IDX_HEADS):
                dve.wait_ge(ix_r, h + 1)
                wait(dve, ix_d, h)
                r = relu_h[h % 2]
                for a, w, tt in ((0, 256, 1), (256, 128, 0)):
                    wc = wi_s[:, 16 * tt + h:16 * tt + h + 1]
                    if h == 0:
                        i = nc.vector.tensor_scalar(score[:, a:a + w], r[:, a:a + w], wc, None, ALU.mult)
                    else:
                        i = nc.vector.scalar_tensor_tensor(score[:, a:a + w], r[:, a:a + w], wc, score[:, a:a + w], ALU.mult, ALU.add)
                i.then_inc(ix_d, 1)
            dve.wait_ge(ix_d, IDX_HEADS)
            dve.wait_ge(aux_in, 32)
            chain(nc.vector.tensor_tensor(score, score, lim, ALU.min))
            s1, s0 = score[:, 0:256], score[:, 256:384]
            for r in range(TOPK // 8):
                nc.vector.max(top1, s1)
                chain(nc.vector.max(top0, s0))
                nc.vector.match_replace(s1, top1, s1, LOWEST)
                chain(nc.vector.match_replace(s0, top0, s0, LOWEST))
            chain(nc.vector.tensor_scalar(sel_mask, score, LOWEST, NEG, ALU.not_equal, ALU.mult))
            dve_attend(dve, ud, N_D, G_D, TD, chain)

            def store_m(used, u, par, b, add):
                dve.wait_ge(chunk_used, used)
                dve.wait_ge(acc_free, u)
                o = macc[:, :, BW * b:BW * (b + 1)]
                if add:
                    i = nc.vector.tensor_tensor(o, acc(par), o, ALU.add)
                else:
                    i = nc.vector.tensor_copy(o, acc(par))
                i.then_inc(acc_free, 1)

            def normed(k, n, m0, b, sem_, tt_last=True):
                dve.wait_ge(merged, m0 + b + 1)
                o = xres[:, :, BW * b:BW * (b + 1)]
                for tt in range(2):
                    i = nc.vector.scalar_tensor_tensor(o[:, tt, :], macc[:, tt, BW * b:BW * (b + 1)], ST["rstd"][:, tt:tt + 1],
                                                       o[:, tt, :], ALU.mult, ALU.add)
                i.then_inc(sem_, 1)

            def new_x(k, n, m0, t, gain):
                mean_square(n, ST["mean"], ssp)
                inverse(k, ST["rstd"], ST["root"])
                dve.wait_ge(stat_v, 2 * k + 2)
                for b in range(5):
                    if b < 4:
                        normed(k, n, m0, b, rows_ready)
                    if b > 0:
                        turn_lo(dve, t + b - 1, tiles(lh, 4 * b - 4), gain[:, 4 * b - 4:4 * b])
                mean_square(n + 8, ST["mean"], ssp)
                inverse(k + 1, ST["rstd"], ST["root"])

            def mixer_out(q, o, u, done):
                split_lo(dve, q, range(done, o + 6))
                for b in range(4):
                    split_lo(dve, q + b, range(o + 6, o + 12))
                    store_m(8 * (q + b) + o + 8, u + b, (u + b) % 2, b, False)
                    if b < 3:
                        split_lo(dve, q + b, (o + 12, o + 13))

            def ffn(q, o, u, t, c0, layer, end):
                split_lo(dve, q, range(o + 4, o + 8))
                dve.wait_ge(gain_in, 16 * (5 + 4 * layer))
                for g in range(2):
                    for j in range(4):
                        for val in range(2):
                            b = 12 * g + 2 * j + val
                            tn, cn = t + 8 * g + 2 * j + val, c0 + 8 * g + 2 * j + val
                            split_lo(dve, q + b, range(o + 8, o + 14))
                            dst = cv if val else cg
                            dve.wait_ge(thi_done, tn + 1)
                            for n in (1, 2):
                                for x in range(4):
                                    k = conv_tiles(g, j, val) + x
                                    i = nc.vector.scalar_tensor_tensor(dst[:, x, n:], tp4[:, x, 0:TOK - n], fcw[:, 2 - n, k:k + 1],
                                                                       dst[:, x, n:], ALU.mult, ALU.add)
                                if n == 1:
                                    i.then_inc(conv_a, 1)
                                    dve.wait_ge(conv_a, cn + 1)
                            i.then_inc(lhs_ready, 1)
                            if val:
                                n = (cn + 1) // 2
                                dve.wait_ge(conv_m, n)
                                dve.wait_ge(lhs_ready, tn + 1)
                                nc.vector.tensor_tensor(cg, cg, cv, ALU.mult).then_inc(conv_ready, 1)
                            split_lo(dve, q + b, (o + 14, o + 15))
                            if val:
                                dve.wait_ge(hid_hi, n)
                                nc.vector.tensor_tensor(mh[1][:, 4 * j:4 * j + 4, :], cg, mh[0][:, 4 * j:4 * j + 4, :].bitcast(F32),
                                                        ALU.subtract).then_inc(hid_ready, 1)
                    for b in range(4):
                        x = q + 12 * g + 8 + b
                        if not (end and g == 1 and b == 3):
                            split_lo(dve, x, range(o + 8, o + 12))
                        store_m(8 * x + o + 8, u + 12 * g + 8 + b, (u + b) % 2, b, g == 1)
                        if g == 0 or b < 3:
                            split_lo(dve, x, range(o + 12, o + 16))

            mixer_out(Q_ABO, O2, U_ABO, 4)
            new_x(4, 40, 13, T_ABX, gains("ffn_pre"))
            ffn(Q_F0, O2, U_F0, T_F0, 0, 0, False)
            new_x(6, 56, 17, T_FX, gains("mix_pre", 1))
            split_lo(dve, Q_CD, (O2 + 4, O2 + 5))
            for b in range(6):
                split_lo(dve, Q_CD + b, range(O2 + 6, O2 + (14 if b < 5 else 12)))
            nc.vector.memset(xin[:, :, 0:3], 0.0)
            for b in range(4):
                dve.wait_ge(thi_done, T_CD + b + 1)
                dve.sem_inc(lhs_ready, 1)
            turn_lo(dve, T_CQ, tiles(lh, 0), pk[:, PACK["q_norm"]:PACK["q_norm"] + 4])
            turn_lo(dve, T_CQ + 1, tiles(lh, 4), pk[:, PACK["kv_norm"]:PACK["kv_norm"] + 2], n=2)
            dve.wait_ge(squares_done, 68)
            nc.vector.tensor_scalar(ST["mean"], ssp[:, :, 0], 1.0 / 512, EPS, ALU.mult, ALU.add)
            nc.vector.tensor_scalar(ST["mean2"], ssp[:, :, 1], 1.0 / 256, EPS, ALU.mult, ALU.add).then_inc(stat_v, 1)

            def tap(c, n):
                a = PACK["lru_w"] + 8 * c + n
                return pk[:, a:a + 1]

            for n in range(LRU_T):
                a = PACK["lru_b"] + n
                i = nc.vector.tensor_scalar(xc[:, n, :], xin[:, n, 0:TOK], tap(0, n), pk[:, a:a + 1], ALU.mult, ALU.add)
            chain(i)
            for c in range(1, 4):
                for n in range(LRU_T):
                    i = nc.vector.scalar_tensor_tensor(xc[:, n, :], xin[:, n, c:c + TOK], tap(c, n), xc[:, n, :], ALU.mult, ALU.add)
                if c < 3:
                    chain(i)
            i.then_inc(lru_v, 1)
            dve.wait_ge(stat_a, 9)
            nc.vector.reciprocal(ST["rq"], ST["root"])
            nc.vector.reciprocal(ST["rkv"], ST["root2"]).then_inc(stat_v, 1)
            dve.wait_ge(lru_a, 4)
            chain(nc.vector.tensor_tensor(mul, decay_a, decay_a, ALU.mult))
            nc.vector.scalar_tensor_tensor(mul, mul, 1.0, rr, ALU.add, ALU.mult).then_inc(lru_v, 1)
            dve.wait_ge(lru_a, 5)
            dve.wait_ge(lru_p, 1)
            chain(nc.vector.tensor_tensor(ii, ii, mul, ALU.mult))
            for n in range(LRU_T):
                i = nc.vector.tensor_tensor_scan(xc[:, n, :], decay_a[:, n, :], ii[:, n, :], 0.0, ALU.mult, ALU.add)
            chain(i)
            nc.vector.tensor_tensor(xc, xc, gy, ALU.mult).then_inc(lru_v, 1)
            dve.wait_ge(lru_a, 6)
            nc.vector.tensor_tensor(mh[1][:, 8:16, :], xc, mh[0][:, 8:16, :].bitcast(F32), ALU.subtract).then_inc(lru_v, 1)
            split_lo(dve, Q_UP, range(O2 + 4, O4 + 20))
            dve.wait_ge(aux_in, 80)
            chain(nc.vector.tensor_copy(pos_f, pos_i[:]))
            for tt in range(2):
                i = nc.vector.tensor_scalar(ang[:, tt, :], freq_sb, pos_f[:, tt:tt + 1], None, ALU.mult)
            chain(i)
            chain(nc.vector.tensor_scalar(revs, ang, 1.0 / TWO_PI, ROUNDER, ALU.mult, ALU.add))
            chain(nc.vector.tensor_scalar(revs, revs, ROUNDER, None, ALU.subtract))
            for part in TURN_PARTS:
                chain(nc.vector.scalar_tensor_tensor(ang, revs, -part, ang, ALU.mult, ALU.add))
            nc.vector.tensor_scalar(ang, ang, PI_BELOW, -PI_BELOW, ALU.min, ALU.max).then_inc(rope_v, 1)
            dve.wait_ge(rope_a, 1)
            chain(nc.vector.tensor_tensor(cosv, half, half, ALU.mult))
            chain(nc.vector.tensor_scalar(cosv, cosv, -2.0, 1.0, ALU.mult, ALU.add))

            def rotate(x1, x2, c, s, t1, t2, y1, y2, done):
                nc.vector.tensor_tensor(t1, x1, c, ALU.mult)
                chain(nc.vector.tensor_tensor(t2, x2, s, ALU.mult))
                chain(y1(t1, t2, ALU.subtract))
                nc.vector.tensor_tensor(t1, x2, c, ALU.mult)
                chain(nc.vector.tensor_tensor(t2, x1, s, ALU.mult))
                y2(t1, t2, ALU.add).then_inc(done, 1)

            kd = kr2.rearrange("p t (a c) -> p t a c", a=2)
            k1, k2 = zc[:, :, 768:800], zc[:, :, 800:832]

            def twice(a):
                return a.unsqueeze(2).to_broadcast([P, 2, 2, 32])

            rotate(k1, k2, cosv, sinv, rq1[:, :, 0, :], rq2[:, :, 0, :],
                   lambda a, b, op: nc.vector.tensor_tensor(kd[:, :, :, 0:32], twice(a), twice(b), op),
                   lambda a, b, op: nc.vector.tensor_tensor(kd[:, :, :, 32:64], twice(a), twice(b), op), rope_v)
            dve.wait_ge(rope_v, 2)
            dve.wait_ge(acc_free, U_UP + 4)
            zh = zq.rearrange("p t (h c) -> p t h c", h=HEADS)

            def heads(a):
                return a.unsqueeze(2).to_broadcast([P, 2, HEADS, 32])

            rotate(zh[:, :, :, 128:160], zh[:, :, :, 160:192], heads(cosv), heads(sinv), rq1, rq2,
                   lambda a, b, op: nc.vector.tensor_tensor(qrow[:, :, :, 0:32], a, b, op),
                   lambda a, b, op: nc.vector.tensor_tensor(qrow[:, :, :, 32:64], a, b, op), rope_v)
            for n in range(2):
                dve.wait_ge(thi_done, T_QR + n + 1)
                dve.sem_inc(lhs_ready, 1)
            dve_attend(dve, um, N_L, G_L, TD, chain)
            mixer_out(Q_CDO, O4, U_CDO, O4 + 4)
            new_x(9, 76, 21, T_CDX, gains("ffn_pre", 1))
            ffn(Q_F1, O4, U_F1, T_F1, 16, 1, True)
            mean_square(92, ST["mean"], ssp)
            inverse(11, ST["rstd"], ST["root"])
            dve.wait_ge(stat_v, 24)
            for b in range(4):
                normed(11, 92, 25, b, out_ready)




def layout(inputs):
    a = {k: np.asarray(v) for k, v in inputs.items()}

    def cols(v):
        return np.ascontiguousarray(v.reshape(-1, P).T)

    t = dict(shape_tables())
    t["x"] = a["x"].reshape(TOK, D)
    t["w_in"] = a["w_in"][0]
    t["w_branch"] = a["w_branch"][0]
    t["w_out"] = a["w_out"][0]
    t["w_mlp_in"] = a["w_mlp_in"][0]
    t["w_mlp_out"] = a["w_mlp_out"][0]
    t["cmp_w1"] = a["cmp_w1"][0]
    t["cmp_w2"] = a["cmp_w2"][0]
    t["cmp_pos"] = np.ascontiguousarray(a["cmp_pos"][0].transpose(2, 0, 1).reshape(P, 64))
    t["swa_sinks"] = a["swa_sinks"]
    t["rel_bias"] = a["rel_bias"]
    t["norm_final"] = a["norm_final"].reshape(1, D)
    t["pack"] = np.concatenate([cols(v) for v in (
        a["norm_mix"], a["norm_mlp"], a["mix_pre_g_2"], a["ffn_pre_g_2"], a["q_norm_g_2"], a["kv_norm_g_2"],
        a["pool_b_2"], a["pool_scale_2"], a["lru_conv_w_2"], a["lru_conv_b_2"], a["lru_ba_2"], a["lru_bx_2"],
        a["lru_lambda_2"])], 1)
    t["mix_post"], t["ffn_post"] = a["mix_post_g_2"], a["ffn_post_g_2"]
    t["ffn_up"], t["ffn_down"] = a["ffn_up_2"], a["ffn_down_2"]
    t["ffn_conv_w"] = a["ffn_conv_w_2"].reshape(2, 3, 64, P).transpose(0, 3, 1, 2).reshape(2, P, 192)
    t["ffn_conv_b"] = a["ffn_conv_b_2"].reshape(2, 64, P).transpose(0, 2, 1)
    t["ab_w_in"], t["ab_w_out"] = a["ab_w_in_2"][0], a["ab_w_out_2"][0]
    t["pool_w"] = a["pool_w_2"].reshape(1024, 256)
    t["cd_w_in"], t["cd_w_out"] = a["cd_w_in_2"][0], a["cd_w_out_2"][0]
    t["w_q_up"], t["w_kv_up"] = a["w_q_up_2"][0], a["w_kv_up_2"][0]
    t["lru_wa"], t["lru_wx"] = a["lru_wa_2"].reshape(1024, P), a["lru_wx_2"].reshape(1024, P)
    t["positions"] = a["positions_2"].reshape(2, P).T
    return {k: np.ascontiguousarray(v) for k, v in t.items()}


def kernel(**inputs):
    import concourse.bacc as bacc
    from concourse.bass_utils import run_bass_kernel_spmd

    nc = bacc.Bacc("TRN2", target_bir_lowering=False, num_devices=1)
    arrays = layout(inputs)
    d = {n: nc.dram_tensor(n, a.shape, mybir.dt.from_np(a.dtype), kind="ExternalInput").ap() for n, a in arrays.items()}
    d["out"] = nc.dram_tensor("out", (TOK, D), F32, kind="ExternalOutput").ap()
    build_program(nc, d)
    r = run_bass_kernel_spmd(nc, [arrays], core_ids=[0])
    return r.results[0]["out"].reshape(1, TOK, D)
```

```python
from contextlib import ExitStack

import numpy as np

import concourse.bass as bass
from concourse import mybir

F32 = mybir.dt.float32
F32R = mybir.dt.float32r
I32 = mybir.dt.int32
ALU = mybir.AluOpType
ACT = mybir.ActivationFunctionType
AX = mybir.AxisListType.X

P = 128
TOK = 256
D = 2048
KT = D // P
EPS = 1e-6
NEG = -1e30
TINY = 1e-30
LOWEST = -3.4028234663852886e38

RING = 8
SPLIT = 4
CHUNK = 1024
A_TAIL = 268
AB_TAIL = 368
BW = 512
NCH = 8

HEADS, KV = 8, 2
HD = 128
A_COLS = 2560
GATE_COLS = 24
BC_COLS = 1536
MERGE0 = A_COLS + GATE_COLS + 2 * BC_COLS
N_CMP, CMP_LEN, CMP_STRIDE = 15, 32, 16
D_FF = 8192

AB_Q, AB_QI, AB_KI, AB_U = 0, 3072, 4096, 4176
IDX_HEADS, IDX_DIM, TOPK = 16, 64, 64
POOL_WINDOWS = (2, 4, 8, 16)
CD_KV, CD_X = 512, 832
ROPE = 64
LRU_T = 8
FF2 = 4096

TWO_PI = 2 * np.pi
ROUNDER = 12582912.0
PI_BELOW = 3.1415925
TURN_PARTS = (6.28125, float(np.float32(np.floor((TWO_PI - 6.28125) * 2**21) / 2**21)),)
TURN_PARTS += (float(np.float32(TWO_PI - TURN_PARTS[0] - TURN_PARTS[1])),)

SM = float(HD) ** -0.5
SM_MLA = float(HD + ROPE) ** -0.5


def bucket(dist):
    n = np.maximum(dist, 0)
    ratio = np.log(np.maximum(n, 1).astype(np.float32) / np.float32(16)) / np.float32(np.log(8.0))
    large = np.minimum(16 + (ratio * np.float32(16)).astype(np.int32), 31)
    return np.where(n < 16, n, large)


def shape_tables():
    i = np.arange(P)[:, None]
    t = {"ident": np.eye(P, dtype=np.float32)}
    m = np.arange(384)
    dist = 255 - m
    t["onehot_rev"] = ((bucket(dist)[None, :] == np.arange(32)[:, None]) & (dist >= 0)).astype(np.float32)
    causal = np.where(dist < 0, NEG, 0.0)
    window = np.where((dist < 0) | (dist >= 128), NEG, 0.0)
    t["mask_rev"] = np.stack([causal] * 8 + [window] * 8 + [causal] * 8).astype(np.float32)
    d2 = np.arange(512) - 255
    onehot = ((bucket(d2)[None, :] == np.arange(32)[:, None]) & (d2 >= 0)).astype(np.float32)
    t["onehot_cmp"] = np.concatenate([np.pad(onehot, ((0, 0), (CMP_STRIDE * g, 0)))[:, :512] for g in range(4)])
    dc = np.stack([(P * s + i - (np.arange(N_CMP) * CMP_STRIDE + CMP_LEN - 1)[None, :]) for s in (1, 0)], 1)
    cmask = np.where(dc < 0, NEG, 0.0).reshape(P, 2 * N_CMP)
    valid = (dc >= 0).any(-1).astype(np.float32)
    t["cmp_const"] = np.concatenate([cmask, valid], 1).astype(np.float32)
    k1, k0 = np.arange(256)[None, :], np.arange(128)[None, :]
    ok = np.concatenate([k1 < ((P + i) // 64 + 1) * 64, k0 < (i // 64 + 1) * 64], 1)
    t["chunk_lim"] = np.where(ok, 3e38, -3e38).astype(np.float32)
    t["chunk_mask"] = np.where(ok, 0.0, NEG).astype(np.float32)
    tok = np.arange(TOK)
    t["inv_head"] = np.stack([1.0 / np.minimum(tok[:16] + 1, w) for w in POOL_WINDOWS]).astype(np.float32).reshape(1, 64)
    t["freq"] = (10000.0 ** (-np.arange(32) / 32.0)).astype(np.float32).reshape(1, 32)
    return t


PACK = {}
_at = 0
for _name, _n in (("norm_mix", 16), ("norm_mlp", 16), ("mix_pre", 32), ("ffn_pre", 32), ("q_norm", 4), ("kv_norm", 2),
                  ("pool_b", 8), ("pool_scale", 8), ("lru_w", 32), ("lru_b", 8), ("ba", 8), ("bx", 8), ("lam", 8)):
    PACK[_name] = _at
    _at += _n
PACK_N = _at


def build_program(nc, d):
    with ExitStack() as ctx:
        def sb(name, shape, dt=F32):
            return ctx.enter_context(nc.sbuf_tensor(name, shape, dt))

        def sem(name):
            return ctx.enter_context(nc.semaphore(name))

        xres = sb("xres", [P, 2, D])
        rows_guard = [nc.sbuf_tensor("l_rows", [P, 2, KT * TOK], F32), nc.sbuf_tensor("m_rows", [P, 2, KT * TOK], F32)]
        l_rows, m_rows = [g.__enter__() for g in rows_guard]
        for g in reversed(rows_guard):
            g.__exit__(None, None, None)
        lh = (sb("l_hi", [P, KT, TOK], F32R), sb("l_lo", [P, KT, TOK], F32R))
        mh = (sb("m_hi", [P, KT, TOK], F32R), sb("m_lo", [P, KT, TOK], F32R))
        raw = sb("raw", [P, RING, CHUNK])
        w_hi = sb("w_hi", [P, SPLIT, CHUNK], F32R)
        w_lo = sb("w_lo", [P, SPLIT, CHUNK], F32R)
        ident = sb("ident_sb", [P, P])
        pk = sb("pk_sb", [P, PACK_N])
        st = sb("stats", [P, 128])
        cx_guard = [nc.sbuf_tensor("cx_hi", [P, 8, TOK], F32R), nc.sbuf_tensor("cx_lo", [P, 8, TOK], F32R)]
        cx = tuple(g.__enter__() for g in cx_guard)
        for g in reversed(cx_guard):
            g.__exit__(None, None, None)
        late = sb("late", [P, 4096])
        main = sb("main", [P, 11136])
        ps = ctx.enter_context(nc.psum_tensor("ps", [P, 8, 512], F32))
        scr = nc.dram_tensor("bias_rows", [24, P, 384], F32, kind="Internal").ap()

        def view(tensor, off, *dims):
            n = int(np.prod(dims))
            v = tensor[:, off:off + n]
            if len(dims) == 2:
                v = v.rearrange("p (a b) -> p a b", a=dims[0])
            if len(dims) == 3:
                v = v.rearrange("p (a b c) -> p a b c", a=dims[0], b=dims[1])
            return v

        raw_in = [sem(f"raw_in{i}") for i in range(RING)]
        hi_done, lo_done, chunk_used = sem("hi_done"), sem("lo_done"), sem("chunk_used")
        acc_free = sem("acc_free")
        rows_ready = sem("rows_ready")
        tp_done, thi_done, lhs_ready = sem("tp_done"), sem("thi_done"), sem("lhs_ready")
        cleared = sem("cleared")
        thi_half, lhs_half = sem("thi_half"), sem("lhs_half")
        x_in = [sem(f"x_in{i}") for i in range(4)]
        head_in, small_in, tb_in, scr_st, gain_in = sem("head_in"), sem("small_in"), sem("tb_in"), sem("scr_st"), sem("gain_in")
        setup_pe, setup_dve = sem("setup_pe"), sem("setup_dve")
        cw_ready, cmp_gelu, cmp_pe, cmp_done = sem("cw_ready"), sem("cmp_gelu"), sem("cmp_pe"), sem("cmp_done")
        merged = sem("merged")
        dve_seq, squares_done, pool_seq = sem("dve_seq"), sem("squares_done"), sem("pool_seq")
        stat_v, stat_a = sem("stat_v"), sem("stat_a")
        at_t, at_qk, at_s, at_l, at_mx, at_e, at_r, at_p = [sem("at_" + n) for n in ("t", "qk", "s", "l", "mx", "e", "r", "p")]
        at_pt, at_ptc, at_pv, at_pvg, at_ohi, at_o = [sem("at_" + n) for n in ("pt", "ptc", "pv", "pvg", "ohi", "o")]
        out_st, out_ready = sem("out_st"), sem("out_ready")
        pool_pe, pool_dve, pool_act, lru_pe, conv_ready = [sem(n) for n in ("pool_pe", "pool_dve", "pool_act", "lru_pe", "conv_ready")]
        sp_v, sp_a = sem("sp_v"), sem("sp_a")
        ix_rows, ix_t, ix_q, ix_s, ix_r, ix_d = [sem("ix_" + n) for n in ("rows", "t", "q", "s", "r", "d")]
        conv_a, conv_m, hid_hi, hid_ready = [sem(n) for n in ("conv_a", "conv_m", "hid_hi", "hid_ready")]
        aux_in, lru_v, lru_a, lru_p, rope_v, rope_a = [sem(n) for n in ("aux_in", "lru_v", "lru_a", "lru_p", "rope_v", "rope_a")]

        ST = {n: st[:, 2 * i:2 * i + 2] for i, n in enumerate(
            ("mean", "root", "rstd", "mean2", "root2", "rstd2", "rstd12", "rq", "rkv", "tmp0", "tmp1", "tmp2"))}
        ssp = st[:, 24:32].rearrange("p (a b) -> p a b", a=2)
        ssp2 = st[:, 32:40].rearrange("p (a b) -> p a b", a=2)
        at_nmx = [st[:, 40 + 2 * j:42 + 2 * j] for j in range(3)]
        at_sum = [st[:, 46 + 2 * j:48 + 2 * j] for j in range(3)]
        at_den = [st[:, 52 + 2 * j:54 + 2 * j] for j in range(3)]
        at_rec = [st[:, 58 + 2 * j:60 + 2 * j] for j in range(3)]
        at_esk = [st[:, 64 + 2 * j:66 + 2 * j] for j in range(3)]
        sp_m, sp_e, sp_z, sp_t = [st[:, 104 + 8 * j:112 + 8 * j] if j < 3 else st[:, 88:96] for j in range(4)]
        decay = st[:, 72:80]

        tp4 = ps[:, 4:6, :].rearrange("p a (b c) -> p (a b) c", b=2)

        def acc(par, w=BW):
            return ps[:, 2 * par:2 * par + 2, 0:w]

        Z = 0
        zA = view(main, Z, 2, A_COLS)
        zB, zC = view(late, 0, 2, BC_COLS), view(main, 2048, 2, BC_COLS)
        TB0 = 5120
        tb = view(main, TB0, 8, 384)
        T0 = TB0 + 3072
        qk = [main[:, T0 + 512 * j:T0 + 512 * (j + 1)] for j in range(2)]
        pp = [main[:, T0 + 1024 + 384 * j:T0 + 1024 + 384 * (j + 1)] for j in range(3)]
        pt = [main[:, T0 + 2176 + 384 * j:T0 + 2176 + 384 * (j + 1)] for j in range(2)]
        C0 = T0 + 2944
        assert C0 <= 11136
        cst = sb("cst", [P, 48 + 16 + 32 + 240 + 30 + 256 + 8])
        gsb = cst[:, 0:48].rearrange("p (s c) -> p s c", s=2)
        gcm = cst[:, 48:64].rearrange("p (s c) -> p s c", s=2)
        ccon = cst[:, 64:96]
        tbc = cst[:, 96:336].rearrange("p (h c) -> p h c", h=8)
        kct = cst[:, 336:366]
        vc = cst[:, 366:622].rearrange("p (k c) -> p k c", k=2)
        sinkb = cst[:, 622:630]
        nsink = st[:, 96:104]

        TA = {"qk": qk, "pp": pp, "pt": pt, "nsink": nsink, "bt": (2, 3), "bs": (4, 5), "bp": (6,), "bo": (7,)}
        mix = [view(main, 1024 * n, 2, BW) for n in range(4)]
        sg = view(main, 4096, 2, BW)
        ybuf = view(main, 5120, 2, BW)
        hid = view(main, 6144, 2, BW)
        gwide = late[:, 0:D]

        rel_sb = late[0:32, 0:24]
        oh_rev = late[0:32, 24:408]
        oh_cmp = late[:, 408:920]
        m_rev = late[0:24, 920:1304]
        r_rows = late[0:24, 1304:1688]
        w2 = view(late, 1688, 2, 2, P)
        post = view(late, 2200, 2, CMP_LEN)
        hg = view(late, 2264, 2, 2, 30)
        rel4 = late[:, 2384:2416]
        hgr = main[0:30, T0:T0 + 512]
        cwin = [main[:, T0 + 480 * j:T0 + 480 * (j + 1)] for j in range(4)]
        ch = tuple(m[:, 0:8, :].rearrange("p a b -> p (a b)")[:, 0:1920].rearrange("p (s l c) -> p s l c", s=2, l=32) for m in mh)

        def wait(eng, s, v):
            if not isinstance(v, int) or v > 0:
                eng.wait_ge(s, v)

        def load_chunk(sp, q, k, src):
            n, w = src.shape[1], src.shape[2]
            wait(sp, lo_done, 8 * q + k - RING + 1)
            sp.dma_start(raw[:, k % RING, 0:n * w].rearrange("p (a b) -> p a b", a=n), src).then_inc(raw_in[k % RING], 16)

        def load_block(sp, q, w, row0, col, width=BW, nch=NCH, k0=0, kt=2):
            for c in range(nch):
                rows = w[row0 + P * kt * c:row0 + P * kt * (c + 1), :]
                src = rows[:, bass.ds(col, width)]
                load_chunk(sp, q, k0 + c, src.rearrange("(k p) n -> p k n", p=P))

        def split_hi(act, q, ks):
            for k in ks:
                wait(act, raw_in[k % RING], 16 * (q + k // RING + 1))
                wait(act, chunk_used, 8 * q + k - SPLIT + 1)
                nc.scalar.activation(w_hi[:, k % SPLIT, :], raw[:, k % RING, :], ACT.Copy).then_inc(hi_done, 1)

        def split_lo(dve, q, ks):
            for k in ks:
                dve.wait_ge(hi_done, 8 * q + k + 1)
                nc.vector.tensor_tensor(w_lo[:, k % SPLIT, :], raw[:, k % RING, :], w_hi[:, k % SPLIT, :].bitcast(F32),
                                        ALU.subtract).then_inc(lo_done, 1)

        def mm_chunk(pe, q, k, lhs, kts, out, first, last, w=BW):
            pe.wait_ge(lo_done, 8 * q + k + 1)
            hi = w_hi[:, k % SPLIT, 0:len(kts) * w].rearrange("p (a b) -> p a b", b=w)
            lo = w_lo[:, k % SPLIT, 0:len(kts) * w].rearrange("p (a b) -> p a b", b=w)
            for j, kt in enumerate(kts):
                for tt in range(2):
                    xh = lhs[0][:, kt, tt * P:(tt + 1) * P]
                    xl = lhs[1][:, kt, tt * P:(tt + 1) * P]
                    o = out[:, tt, :]
                    nc.tensor.matmul(o, xh, hi[:, j, :], start=first and j == 0, stop=False)
                    nc.tensor.matmul(o, xh, lo[:, j, :], start=False, stop=False)
                    m = nc.tensor.matmul(o, xl, hi[:, j, :], start=False, stop=last and j == len(kts) - 1)
            m.then_inc(chunk_used, 1)

        def mm_block(pe, q, u, par, lhs, k0=0, nch=NCH, kt0=0, w=BW, hook=None, need=None, turns=None,
                     hook_at=1, each=None, turn_at=1):
            if turns is not None:
                turns(0)
            wait(pe, acc_free, u - 1)
            for c in range(nch):
                if turns is not None:
                    if c % 2 == 0:
                        pe.wait_ge(lhs_half, HALVES.index(need[1]) + c // 2 + 1)
                    else:
                        pe.wait_ge(lhs_ready, need[1] + c // 2 + 1)
                    if c % 2 == turn_at and c < 6:
                        turns(c // 2 + 1)
                elif need is not None and c % 2 == 0:
                    pe.wait_ge(need[0], need[1] + c // 2 + 1)
                mm_chunk(pe, q, k0 + c, lhs, (kt0 + 2 * c, kt0 + 2 * c + 1), acc(par, w), c == 0, c == nch - 1, w)
                if c == hook_at and hook is not None:
                    hook()
                if each is not None:
                    each(c)

        def turn(pe, t, rows, ready, n=4):
            pe.wait_ge(*ready)
            wait(pe, lhs_ready, t)
            for j in range(n):
                for tt in range(2):
                    m = nc.tensor.transpose(tp4[:, j, tt * P:(tt + 1) * P], rows[:, tt, j * P:(j + 1) * P], ident[:])
            m.then_inc(tp_done, 1)

        def turn_hi(act, t, dst, gain=None, n=4):
            act.wait_ge(tp_done, t + 1)
            if gain is None:
                i = nc.scalar.activation(dst[0], tp4, ACT.Copy)
            else:
                for j in range(n):
                    i = nc.scalar.activation(dst[0][:, j, :], tp4[:, j, :], ACT.Copy, scale=gain[:, j:j + 1])
                    if j == 1 and n == 4:
                        i.then_inc(thi_half, 1)
            i.then_inc(thi_done, 1)

        def turn_lo(dve, t, dst, gain=None, n=4):
            if gain is None or n < 4:
                dve.wait_ge(thi_done, t + 1)
            if gain is None:
                i = nc.vector.tensor_tensor(dst[1], tp4, dst[0].bitcast(F32), ALU.subtract)
            else:
                for j in range(n):
                    if n == 4 and j == 0:
                        dve.wait_ge(thi_half, HALVES.index(t) + 1)
                    if n == 4 and j == 2:
                        dve.wait_ge(thi_done, t + 1)
                    i = nc.vector.scalar_tensor_tensor(dst[1][:, j, :], tp4[:, j, :], gain[:, j:j + 1],
                                                       dst[0][:, j, :].bitcast(F32), ALU.mult, ALU.subtract)
                    if n == 4 and j == 1:
                        i.then_inc(lhs_half, 1)
            i.then_inc(lhs_ready, 1)

        def tiles(lhs, kt):
            return (lhs[0][:, kt:kt + 4, :], lhs[1][:, kt:kt + 4, :])

        def gains(name, layer=0):
            a = PACK[name] + 16 * layer
            return pk[:, a:a + 16]

        class Unit:
            def __init__(self, q, k, v, bias, out, qt, kt, scale=SM, new_q=True, new_k=True, gate=None, sink=None,
                         first=True, last=True, w=(256, 128), rope=None):
                self.q, self.k, self.v, self.bias, self.out, self.scale = q, k, v, bias, out, scale
                self.qt, self.kt, self.new_q, self.new_k = qt, kt, new_q, new_k
                self.gate, self.sink, self.first, self.last, self.w, self.rope = gate, sink, first, last, w, rope

        def turned_by(us, j):
            return sum(u.new_q or u.new_k for u in us[:j + 1])

        def head_cols(z, c):
            return [z[:, tt, c:c + HD] for tt in range(2)]

        def units_a():
            us = []
            for h in range(HEADS):
                kv = h // 4
                q, qt = head_cols(zA, HD * h), qk[h % 2][:, 0:TOK]
                out = (mh[0][:, h, :], mh[1][:, h, :])
                for b, (kc, vcol) in enumerate(((1536, 1792), (2048, 2304))):
                    kt = qk[b][:, TOK:2 * TOK] if kv == 0 else late[:, BC_COLS * 2 + TOK * b:BC_COLS * 2 + TOK * (b + 1)]
                    us.append(Unit(q, head_cols(zA, kc + HD * kv), head_cols(zA, vcol + HD * kv), tb[:, h, :], out,
                                   qt, kt, new_q=b == 0, new_k=h % 4 == 0, gate=gsb[:, :, 3 * h + 1 + b], first=b == 0, last=False))
                us.append(Unit(q, None, [vc[0:N_CMP, kv, :]], tbc[:, h, :], out, qt, kct[:, N_CMP * kv:N_CMP * (kv + 1)],
                               new_q=False, new_k=False,
                               gate=gcm[:, :, h], first=False, last=True, w=(N_CMP, N_CMP)))
            return us

        def units_bc(z, dst, kt0, sinks):
            return [Unit(head_cols(z, HD * h), head_cols(z, 1024 + HD * (h // 4)), head_cols(z, 1280 + HD * (h // 4)),
                         tb[:, h, :], (dst[0][:, kt0 + h, :], dst[1][:, kt0 + h, :]),
                         qk[h % 2][:, 0:TOK], qk[h // 4][:, TOK:2 * TOK], new_k=h % 4 == 0,
                         sink=sinkb[:, h:h + 1] if sinks else None) for h in range(HEADS)]

        def bank(T, kind, n):
            return T[kind][n % len(T[kind])]

        def out_lag(T):
            return 3 + len(T["bo"])

        def pe_attend(pe, us, n0, e0, g0, T, between=None):
            for i in range(len(us) + 4):
                if i < len(us) and (us[i].new_q or us[i].new_k):
                    u, e = us[i], e0 + turned_by(us, i) - 1
                    wait(pe, at_qk, e + 1 - len(T["bt"]))
                    src = [(j, a) for j, a in enumerate(u.q) if u.new_q] + [(2 + j, a) for j, a in enumerate(u.k) if u.new_k]
                    for j, a in src:
                        m = nc.tensor.transpose(ps[:, bank(T, "bt", e), j * P:(j + 1) * P], a, ident[:])
                    m.then_inc(at_t, 1)
                j = i - 1
                if 0 <= j < len(us):
                    u, n = us[j], n0 + j
                    qs, kt = u.qt, u.kt
                    pe.wait_ge(at_qk, e0 + turned_by(us, j))
                    wait(pe, at_l, n + 1 - len(T["bs"]))
                    sc = ps[:, bank(T, "bs", n), :]
                    w1, w0 = u.w
                    for o, tt, w in ((sc[:, 0:w1], 1, w1), (sc[:, w1:w1 + w0], 0, w0)):
                        m = nc.tensor.matmul(o, qs[:, tt * P:(tt + 1) * P], kt[:, 0:w], start=True, stop=u.rope is None)
                        if u.rope is not None:
                            m = nc.tensor.matmul(o, u.rope[0][:, tt * P:(tt + 1) * P], u.rope[1][:, 0:w], start=False, stop=True)
                    m.then_inc(at_s, 1)
                j = i - 3
                if 0 <= j < len(us):
                    u, n = us[j], n0 + j
                    pe.wait_ge(at_p, n + 1)
                    wait(pe, at_ptc, n + 1 - len(T["bp"]))
                    p, turned = T["pp"][n % 3], ps[:, bank(T, "bp", n), :]
                    w1, w0 = u.w
                    nc.tensor.transpose(turned[0:min(w0, P), 0:P], p[:, w1:w1 + w0], ident[:])
                    m = nc.tensor.transpose(turned[0:min(w1, P), P:2 * P], p[:, 0:min(w1, P)], ident[:])
                    if w1 > P:
                        m = nc.tensor.transpose(turned[:, 2 * P:3 * P], p[:, P:2 * P], ident[:])
                    m.then_inc(at_pt, 1)
                j = i - 4
                if 0 <= j < len(us):
                    u, n = us[j], n0 + j
                    g = g0 + sum(x.last for x in us[:j])
                    pe.wait_ge(at_ptc, n + 1)
                    if u.first:
                        wait(pe, at_o, g + 1 - len(T["bo"]))
                    o, pts, kk = ps[:, bank(T, "bo", g), 0:TOK], T["pt"][n % 2], min(u.w[1], P)
                    m = nc.tensor.matmul(o, u.v[0][0:kk, :], pts[0:kk, 0:TOK], start=u.first, stop=u.last and len(u.v) == 1)
                    if len(u.v) == 2:
                        m = nc.tensor.matmul(o[:, P:TOK], u.v[1], pts[:, TOK:TOK + P], start=False, stop=u.last)
                    m.then_inc(at_pv, 1)
                if between is not None:
                    between(i)

        def act_attend(act, us, n0, e0, g0, T, between=None):
            ends = [j for j, u in enumerate(us) if u.last]
            for i in range(len(us) + out_lag(T)):
                j = i - 2
                if 0 <= j < len(us):
                    u, n = us[j], n0 + j
                    act.wait_ge(at_mx, n + 1)
                    w1, w0 = u.w
                    p, nm, sm = T["pp"][n % 3], at_nmx[n % 3], at_sum[n % 3]
                    if u.sink is not None:
                        nc.scalar.activation(at_esk[n % 3], nm, ACT.Exp, bias=u.sink)
                    nc.scalar.activation(p[:, 0:w1], p[:, 0:w1], ACT.Exp, bias=nm[:, 0:1], accum_out=sm[:, 0:1])
                    nc.scalar.activation(p[:, w1:w1 + w0], p[:, w1:w1 + w0], ACT.Exp, bias=nm[:, 1:2],
                                         accum_out=sm[:, 1:2]).then_inc(at_e, 1)
                if between is not None:
                    between(i)
                if i < len(us) and (us[i].new_q or us[i].new_k):
                    u, e = us[i], e0 + turned_by(us, i) - 1
                    act.wait_ge(at_t, e + 1)
                    before = [j for j in range(i) if us[j].new_q]
                    wait(act, at_s, n0 + (before[-1] if before else 0))
                    copies = ([(u.qt, 0)] if u.new_q else []) + ([(u.kt, TOK)] if u.new_k else [])
                    for to, c in copies:
                        m = nc.scalar.activation(to, ps[:, bank(T, "bt", e), c:c + TOK], ACT.Copy)
                    m.then_inc(at_qk, 1)
                j = i - out_lag(T)
                if 0 <= j < len(us) and us[j].last:
                    u, g = us[j], g0 + ends.index(j)
                    act.wait_ge(at_pv, n0 + j + 1)
                    nc.scalar.activation(u.out[0], ps[:, bank(T, "bo", g), 0:TOK], ACT.Copy).then_inc(at_ohi, 1)

        def dve_attend(dve, us, n0, g0, T, chain, between=None):
            ends = [j for j, u in enumerate(us) if u.last]
            for i in range(len(us) + out_lag(T)):
                j = i - 2
                if 0 <= j < len(us):
                    u, n = us[j], n0 + j
                    den, rec = at_den[n % 3], at_rec[n % 3]
                    dve.wait_ge(at_e, n + 1)
                    if u.sink is not None:
                        chain(nc.vector.tensor_tensor(den, at_sum[n % 3], at_esk[n % 3], ALU.add))
                        chain(nc.vector.tensor_scalar(den, den, TINY, None, ALU.max))
                    else:
                        chain(nc.vector.tensor_scalar(den, at_sum[n % 3], TINY, None, ALU.max))
                    m = nc.vector.reciprocal(rec, den)
                    if u.gate is not None:
                        chain(m)
                        m = nc.vector.tensor_tensor(rec, rec, u.gate, ALU.mult)
                    m.then_inc(at_r, 1)
                j = i - 1
                if 0 <= j < len(us):
                    u, n = us[j], n0 + j
                    w1, w0 = u.w
                    p, nm = T["pp"][n % 3], at_nmx[n % 3]
                    dve.wait_ge(at_s, n + 1)
                    wait(dve, at_pt, n - 2)
                    nc.vector.scalar_tensor_tensor(p[:, 0:w1 + w0], ps[:, bank(T, "bs", n), 0:w1 + w0], u.scale, u.bias,
                                                   ALU.mult, ALU.add).then_inc(at_l, 1)
                    dve.wait_ge(at_l, n + 1)
                    nc.vector.tensor_reduce(nm[:, 0:1], p[:, 0:w1], AX, ALU.max, negate=True)
                    m = nc.vector.tensor_reduce(nm[:, 1:2], p[:, w1:w1 + w0], AX, ALU.max, negate=True)
                    if u.sink is not None:
                        chain(m)
                        m = nc.vector.tensor_scalar(nm, nm, T["nsink"][:, j:j + 1], None, ALU.min)
                    m.then_inc(at_mx, 1)
                if between is not None:
                    between(i)
                j = i - 3
                if 0 <= j < len(us):
                    u, n = us[j], n0 + j
                    dve.wait_ge(at_pt, n + 1)
                    wait(dve, at_pv, n - 1)
                    kk = min(u.w[1], P)
                    w = 384 if u.w[0] > P else 256
                    nc.vector.tensor_copy(T["pt"][n % 2][0:kk, 0:w], ps[0:kk, bank(T, "bp", n), 0:w]).then_inc(at_ptc, 1)
                j = i - out_lag(T)
                if 0 <= j < len(us) and us[j].last:
                    u, g = us[j], g0 + ends.index(j)
                    dve.wait_ge(at_ohi, g + 1)
                    nc.vector.tensor_tensor(u.out[1], ps[:, bank(T, "bo", g), 0:TOK], u.out[0].bitcast(F32),
                                            ALU.subtract).then_inc(at_o, 1)

        def pool_attend(pool, us, n0, T):
            for j, u in enumerate(us):
                n = n0 + j
                w1, w0 = u.w
                p, rec = T["pp"][n % 3], at_rec[n % 3]
                pool.wait_ge(at_r, n + 1)
                nc.gpsimd.tensor_scalar(p[:, 0:w1], p[:, 0:w1], rec[:, 0:1], None, ALU.mult)
                nc.gpsimd.tensor_scalar(p[:, w1:w1 + w0], p[:, w1:w1 + w0], rec[:, 1:2], None, ALU.mult).then_inc(at_p, 1)


        zab = view(main, 0, 2, 5200)
        TD = {"qk": [late[:, 512 * j:512 * (j + 1)] for j in range(2)],
              "pp": [late[:, 1024 + 384 * j:1408 + 384 * j] for j in range(3)],
              "pt": [late[:, 2176 + 384 * j:2560 + 384 * j] for j in range(2)], "nsink": None, "bt": (2, 3), "bs": (4, 5), "bp": (6,), "bo": (7,)}
        parts_d = [view(main, a, 2, BW) for a in (3072, 8272, 9296)]
        PAD = 16
        pu, pa, pb = [view(late, 1088 * j, 4, PAD + TOK) for j in range(3)]
        pool_out = ps[:, 6:8, :].rearrange("p a (b c) -> p (a b) c", b=2)
        inv_head = view(late, 3264, 4, PAD)
        score = late[:, 2944:3328]
        relu_h = [late[:, 3328 + 384 * j:3712 + 384 * j] for j in range(2)]
        sel_mask, lim = main[:, 4176:4560], main[:, 4560:4944]
        ki2, kiT = view(main, 10400, 2, P), main[:, 10656:10912]
        wi_s, top1, top0 = main[:, 10912:10944], main[:, 10944:10952], main[:, 10952:10960]
        macc = view(main, 0, 2, D)
        hid2 = view(main, 4096, 2, BW)
        cg, cv = view(main, 5120, 4, TOK), view(main, 6144, 4, TOK)
        fcw, fcb = view(main, 7168, 3, 64), main[:, 7360:7424]
        gpost_ffn = main[:, 7424:7424 + D]
        gpost_mix = late[:, 0:D]
        zc = view(main, 0, 2, CD_X)
        zx, zy = view(main, 1664, 2, 1024), view(main, 3712, 2, 1024)
        rr, ii = view(main, 1664, 8, TOK), view(main, 3712, 8, TOK)
        xin, xc = view(main, 5760, 8, 3 + TOK), view(main, 7832, 8, TOK)
        mul = view(main, 5760, 8, TOK)
        decay_a, gy = view(late, 0, 8, TOK), view(late, 2048, 8, TOK)
        zq, zkv = m_rows[:, :, 0:1536], l_rows[:, :, 1536:3584]
        parts_m = [macc[:, :, BW * b:BW * (b + 1)] for b in (1, 2, 3)]
        qrow, kr2, krT = view(main, 1664, 2, 8, ROPE), view(main, 2688, 2, P), main[:, 10112:10368]
        qrT = view(late, 2944, 4, TOK)
        cmask2 = main[:, 10752:11136]
        pos_i, pos_f, freq_sb = sb("pos_i", [P, 2], I32), main[:, 10688:10690], main[:, 10690:10722]
        ang, revs, cosv, sinv, half = [view(main, 10368 + 64 * j, 2, 32) for j in range(5)]
        rq1, rq2 = view(late, 0, 2, 8, 32), view(late, 512, 2, 8, 32)

        wi = d["w_in"]
        Q_B, Q_C, Q_M, Q_O, Q_MLP = 8, 11, 14, 32, 36
        U_B, U_C, U_M, U_O, U_MLP = 6, 9, 12, 36, 40
        T_CMP, T_MIX, T_O, T_MLP = 4, 5, 9, 13
        ua = units_a()
        ub = units_bc(zB, mh, 8, True)
        uc = units_bc(zC, cx, 0, False)
        N_B, N_C, N_END = len(ua), len(ua) + 8, len(ua) + 16
        E_B = turned_by(ua, len(ua) - 1)
        E_C, E_D, E_L = E_B + 8, E_B + 16, E_B + 24
        G_B, G_C, G_END = 8, 16, 24
        N_SMALL = 13
        O2, O4, O6 = 2, 4, 6
        UP_CHUNKS = (2, 4, 6, 7, 8, 9, 10)
        Q_AB, Q_ABO, Q_F0, Q_CD, Q_UP, Q_CDO, Q_F1 = 68, 79, 83, 107, 113, 114, 118
        U_AB, U_ABO, U_F0, U_CD, U_UP, U_CDO, U_F1 = 72, 83, 90, 114, 120, 127, 134
        T_X1, T_PU, T_ABX, T_F0, T_FX, T_CD, T_CQ, T_QR, T_CDX, T_F1 = 29, 33, 35, 39, 55, 59, 63, 65, 67, 71

        def conv_tiles(g, j, val):
            return (FF2 * val + D * g + BW * j) // P

        ud = [Unit([zab[:, tt, HD * h:HD * (h + 1)] for tt in range(2)], [zab[:, tt, 1024 + HD * h:1024 + HD * (h + 1)] for tt in range(2)],
                   [zab[:, tt, 2048 + HD * h:2048 + HD * (h + 1)] for tt in range(2)], sel_mask, (mh[0][:, h, :], mh[1][:, h, :]),
                   TD["qk"][h % 2][:, 0:TOK], TD["qk"][h % 2][:, TOK:2 * TOK])
              for h in range(HEADS)]
        um = [Unit([zq[:, tt, 192 * h:192 * h + HD] for tt in range(2)], [zkv[:, tt, 256 * h:256 * h + HD] for tt in range(2)],
                   [zkv[:, tt, 256 * h + HD:256 * h + 2 * HD] for tt in range(2)], cmask2, (mh[0][:, h, :], mh[1][:, h, :]),
                   TD["qk"][h % 2][:, 0:TOK], TD["qk"][h % 2][:, TOK:2 * TOK], scale=SM_MLA,
                   rope=(qrT[ROPE * (h % 2):ROPE * (h % 2 + 1), h // 2, :], krT[ROPE * (h % 2):ROPE * (h % 2 + 1), :]))
              for h in range(HEADS)]
        HALVES = [t + b for t in (0, T_O, T_X1, T_ABX, T_FX) for b in range(4)] + [T_CQ] + [T_CDX + b for b in range(4)]
        X_ROWS = {T_ABX: 16, T_FX: 20, T_CDX: 24}
        N_D, N_L, N_ALL = N_END, N_END + 8, N_END + 16
        G_D, G_L, G_ALL = G_END, G_END + 8, G_END + 16

        AB_BLOCKS = [(AB_KI + AB_TAIL * j, AB_TAIL) for j in range(3)] + [(AB_QI + BW * j, BW) for j in range(2)]
        AB_BLOCKS += [(BW * j, BW) for j in range(6)]
        AB_POOL = 5
        CD_BLOCKS = ((832, 512), (1344, 512), (1856, 512), (2368, 512), (0, 512), (512, 320))
        CD_LRU = 4
        A_BLOCKS = ((1024, BW), (0, BW), (512, BW), (1536, BW), (2048, A_TAIL), (2048 + A_TAIL, A_TAIL))

        AMID_A, AMID_B, AMID_C = (4, 1, 32), (36, 1, 48), (4, 2, 24)

        OUT_ORDER = [(b, 1) for b in (1, 2, 3)] + [(0, 1), (0, 0)] + [(b, 0) for b in (1, 2, 3)]
        OUT_PARTS, OUT_ENDS = 12, (20, 24, 28, 32)
        AMID_OUT = (0, 1, OUT_PARTS)

        def amid(plan, i):
            return min(plan[2], plan[0] + plan[1] * (i + 1))

        def split_to(plan, i):
            return amid(plan, i - 1) + SPLIT

        block = ctx.enter_context(nc.Block())

        @block.sync
        def _(sp):
            def load_x(j):
                sp.dma_start(xres[:, :, BW * j:BW * (j + 1)],
                             d["x"][:, BW * j:BW * (j + 1)].rearrange("(t p) n -> p t n", p=P)).then_inc(x_in[j], 16)

            sp.dma_start(ident[:], d["ident"]).then_inc(head_in, 16)
            load_x(0)
            sp.dma_start(pk[:], d["pack"]).then_inc(head_in, 16)
            c, w = A_BLOCKS[0]
            for k in range(NCH):
                load_block(sp, 0, wi, 2 * P * k, c, width=w, nch=1, k0=k)
                if k < 3:
                    load_x(k + 1)
            for b, (c, w) in enumerate(A_BLOCKS[1:]):
                load_block(sp, b + 1, wi, 0, c, width=w)
            for s in range(2):
                w1 = d["cmp_w1"][s]
                for c in range(NCH):
                    load_chunk(sp, 6 + s, c, w1[4 * P * c:4 * P * (c + 1), :].rearrange("(k p) n -> p k n", p=P))
            for b in range(6):
                load_block(sp, Q_B + b, wi, 0, A_COLS + GATE_COLS + BW * b)
            for m in range(3):
                with sp.Fori(1, 3) as i:
                    q = Q_M + 6 * m - 3 + 3 * i
                    for e in range(2):
                        load_block(sp, q, wi, 0, MERGE0 + D * m + BW * (e - 2) + 2 * BW * i, k0=12 * e)
                        load_block(sp, q, d["w_branch"][m], 0, BW * (e - 2) + 2 * BW * i, nch=4, k0=12 * e + 8)
            for b in range(4):
                load_block(sp, Q_O + b, d["w_out"], 0, BW * b)
            with sp.Fori(0, 4) as g:
                for b in range(4):
                    load_block(sp, Q_MLP + b + 8 * g, d["w_mlp_in"], 0, BW * b + D * g)
                w_down = d["w_mlp_out"][bass.ds(D * g, D), :]
                for b in range(4):
                    load_block(sp, Q_MLP + 4 + b + 8 * g, w_down, 0, BW * b)
            wab = d["ab_w_in"]
            for b, (c, w) in enumerate(AB_BLOCKS):
                o = 0 if b < AB_POOL else O2
                if b == AB_POOL:
                    for x in range(2):
                        load_chunk(sp, Q_AB + b, x, d["pool_w"][BW * x:BW * (x + 1), :].rearrange("(k p) n -> p k n", p=P))
                    load_block(sp, Q_AB + b, wab, 0, c, width=w, k0=o, nch=6)
                    for x in range(2):
                        sp.wait_ge(pool_pe, x + 1)
                        load_block(sp, Q_AB + b, wab, 256 * (6 + x), c, width=w, k0=o + 6 + x, nch=1)
                else:
                    load_block(sp, Q_AB + b, wab, 0, c, width=w, k0=o)

            def load_out(q, o, w):
                for n, (b, h) in enumerate(OUT_ORDER):
                    load_block(sp, q, w, 1024 * h, BW * b, k0=o + 4 * n, nch=4)

            def load_ffn(q, o, layer):
                up, down = d["ffn_up"][layer], d["ffn_down"][layer]
                for g in range(2):
                    with sp.Fori(0, 4) as j:
                        load_block(sp, q + 12 * g + 2 * j, up, 0, D * g + BW * j, k0=o)
                        load_block(sp, q + 12 * g + 1 + 2 * j, up, 0, FF2 + D * g + BW * j, k0=o)
                    for b in range(4):
                        load_block(sp, q + 12 * g + 8 + b, down, D * g, BW * b, k0=o)

            load_out(Q_ABO, O2, d["ab_w_out"])
            load_ffn(Q_F0, O2, 0)
            wcd = d["cd_w_in"]
            for b, (c, w) in enumerate(CD_BLOCKS):
                if b == CD_LRU:
                    for x, name in enumerate(("lru_wa", "lru_wx")):
                        load_chunk(sp, Q_CD + b, O2 + x, d[name].rearrange("(n p) c -> p n c", p=P))
                    load_block(sp, Q_CD + b, wcd, 0, c, width=w, k0=O4, nch=6)
                    for x in range(2):
                        sp.wait_ge(lru_pe, 2 * x + 2)
                        load_block(sp, Q_CD + b, wcd, 256 * (6 + x), c, width=w, k0=O4 + 6 + x, nch=1)
                else:
                    load_block(sp, Q_CD + b, wcd, 0, c, width=w, k0=O2 if b < CD_LRU else O4)
            for c in range(6):
                load_chunk(sp, Q_UP, O4 + c, d["w_q_up"][:, 256 * c:256 * (c + 1)].rearrange("(k p) n -> p k n", p=P))
            for c in range(4):
                load_chunk(sp, Q_UP, O4 + 6 + c, d["w_kv_up"][:, BW * c:BW * (c + 1)].rearrange("(k p) n -> p k n", p=P))
            load_out(Q_CDO, O6, d["cd_w_out"])
            load_ffn(Q_F1, O6, 1)
            for b in range(4):
                sp.wait_ge(out_ready, b + 1)
                sp.dma_start(d["out"][:, BW * b:BW * (b + 1)].rearrange("(t p) n -> p t n", p=P),
                             xres[:, :, BW * b:BW * (b + 1)]).then_inc(out_st, 16)
            sp.wait_ge(out_st, 64)

        @block.gpsimd
        def _(pool):
            nc.gpsimd.memset(rel4, 0.0).then_inc(cleared, 1)
            pool.dma_start(rel_sb, d["rel_bias"]).then_inc(small_in, 16)
            pool.dma_start(oh_rev, d["onehot_rev"]).then_inc(small_in, 16)
            pool.dma_start(oh_cmp, d["onehot_cmp"]).then_inc(small_in, 16)
            pool.dma_start(m_rev, d["mask_rev"]).then_inc(small_in, 16)
            pool.dma_start(ccon, d["cmp_const"]).then_inc(small_in, 16)
            pool.dma_start(post.rearrange("p a b -> p (a b)"), d["cmp_pos"]).then_inc(small_in, 16)
            for s in range(2):
                pool.dma_start(w2[:, s], d["cmp_w2"][s].rearrange("(h p) n -> p h n", p=P)).then_inc(small_in, 16)
            pool.dma_start(sinkb, d["swa_sinks"].to_broadcast([P, HEADS])).then_inc(small_in, 16)
            pool.wait_ge(cleared, 1)
            for g in range(4):
                pool.dma_start(rel4[32 * g:32 * (g + 1), HEADS * g:HEADS * (g + 1)], d["rel_bias"][:, 0:HEADS]).then_inc(small_in, 16)

            pool.wait_ge(setup_dve, 1)
            pool.dma_start(scr, r_rows.unsqueeze(1).to_broadcast([24, P, 384])).then_inc(scr_st, 16)
            pool.wait_ge(scr_st, 16)

            def load_bias(h0):
                for a, w, at in ((0, 256, 127), (256, 128, 255)):
                    src = bass.AP(scr.tensor, P * 384 * h0 + at, [[383, P], [P * 384, HEADS], [1, w]])
                    pool.dma_start(tb[:, :, a:a + w], src).then_inc(tb_in, 16)

            load_bias(0)
            pool_attend(pool, ua, 0, TA)
            pool.wait_ge(at_l, N_B)
            load_bias(HEADS)
            pool_attend(pool, ub, N_B, TA)
            pool.wait_ge(at_l, N_C)
            load_bias(2 * HEADS)
            pool_attend(pool, uc, N_C, TA)
            pool.sem_inc(merged, 1)
            with pool.Fori(0, 2) as i:
                for e in range(2):
                    pool.wait_ge(acc_free, U_M + 8 + 2 * e + 2 + 4 * i)
                    o = main[:, bass.ds(2 * BW * e + 4 * BW * i, 2 * BW)].rearrange("p (t c) -> p t c", t=2)
                    nc.gpsimd.tensor_tensor(o, o, ybuf, ALU.add).then_inc(merged, 1)
            for n in range(4):
                pool.wait_ge(acc_free, U_M + 16 + 2 * n + 2)
                o = mix[n]
                nc.gpsimd.tensor_tensor(o, o, ybuf, ALU.add).then_inc(merged, 1)
            pool.wait_ge(chunk_used, 8 * Q_O)
            pool.dma_start(gwide, d["norm_final"].to_broadcast([P, D])).then_inc(gain_in, 16)
            pool.wait_ge(gain_in, 16)
            for b in range(4):
                pool.wait_ge(squares_done, 16 + 4 * b + 2)
                o = xres[:, :, BW * b:BW * (b + 1)]
                g = gwide[:, BW * b:BW * (b + 1)].unsqueeze(1).to_broadcast([P, 2, BW])
                nc.gpsimd.tensor_tensor(o, o, g, ALU.mult).then_inc(merged, 1)
            def scaled_out(squares0, gwide, gains_in):
                pool.wait_ge(*gains_in)
                for b in range(4):
                    pool.wait_ge(squares_done, squares0 + 2 * b + 2)
                    o = macc[:, :, BW * b:BW * (b + 1)]
                    g = gwide[:, BW * b:BW * (b + 1)].unsqueeze(1).to_broadcast([P, 2, BW])
                    nc.gpsimd.tensor_tensor(o, o, g, ALU.mult).then_inc(merged, 1)

            def load_mixer_end(layer):
                pool.wait_ge(at_o, G_L if layer == 0 else G_ALL)
                pool.wait_ge(at_pv, N_L if layer == 0 else N_ALL)
                pool.dma_start(gpost_mix, d["mix_post"][layer:layer + 1, :].to_broadcast([P, D])).then_inc(gain_in, 16)
                pool.dma_start(fcw.rearrange("p a b -> p (a b)"), d["ffn_conv_w"][layer]).then_inc(gain_in, 16)
                pool.dma_start(fcb, d["ffn_conv_b"][layer]).then_inc(gain_in, 16)

            def load_ffn_gains(layer):
                pool.wait_ge(acc_free, (U_F0, U_F1)[layer])
                pool.dma_start(gpost_ffn, d["ffn_post"][layer:layer + 1, :].to_broadcast([P, D])).then_inc(gain_in, 16)

            pool.wait_ge(merged, 13)
            nc.gpsimd.memset(late[:, 0:3264], 0.0).then_inc(pool_seq, 1)
            pool.dma_start(inv_head.rearrange("p a b -> p (a b)"), d["inv_head"].to_broadcast([P, 64])).then_inc(aux_in, 16)
            pool.wait_ge(pool_dve, 4)
            pool.dma_start(lim, d["chunk_lim"]).then_inc(aux_in, 16)
            pool_attend(pool, ud, N_D, TD)
            load_mixer_end(0)
            scaled_out(32, gpost_mix, (gain_in, 16 * 4))
            load_ffn_gains(0)
            scaled_out(48, gpost_ffn, (gain_in, 16 * 5))
            pool.dma_start(cmask2, d["chunk_mask"]).then_inc(aux_in, 16)
            pool.dma_start(pos_i[:], d["positions"]).then_inc(aux_in, 16)
            pool.dma_start(freq_sb, d["freq"].to_broadcast([P, 32])).then_inc(aux_in, 16)
            pool.wait_ge(lru_a, 4)
            nc.gpsimd.tensor_tensor(ii, ii, xc, ALU.mult).then_inc(lru_p, 1)
            pool_attend(pool, um, N_L, TD)
            load_mixer_end(1)
            scaled_out(68, gpost_mix, (gain_in, 16 * 8))
            load_ffn_gains(1)
            scaled_out(84, gpost_ffn, (gain_in, 16 * 9))

        @block.tensor
        def _(pe):
            pe.wait_ge(head_in, 32)

            def turn_x(j):
                turn(pe, j, xres[:, :, BW * j:BW * (j + 1)], (x_in[j], 16))

            mm_block(pe, 0, 0, 0, lh, need=(lhs_ready, 0), turns=turn_x, turn_at=0)
            for b in range(1, 6):
                def hook():
                    turn(pe, T_CMP, zA[:, :, 1024:1536], (acc_free, 1))
                mm_block(pe, b, b, b % 2, lh, w=A_BLOCKS[b][1], hook=hook if b == 1 else None)
                if b == 3:
                    pe.wait_ge(small_in, 16 * N_SMALL)
                    pe.wait_ge(squares_done, 8)
                    nc.tensor.matmul(ps[0:24, 6, 0:384], rel_sb, oh_rev, start=True, stop=True)
                    for s in range(2):
                        for c in range(4):
                            a = 255 + P * (1 - s) - 4 * CMP_STRIDE * c - (CMP_LEN - 1)
                            m = nc.tensor.matmul(ps[:, 7, P * s + 32 * c:P * s + 32 * (c + 1)], oh_cmp[:, a:a + P], rel4,
                                                 start=True, stop=True)
                    m.then_inc(setup_pe, 1)
            pe.wait_ge(lhs_ready, T_CMP + 1)
            pe.wait_ge(acc_free, 6)
            for s in range(2):
                for c in range(NCH):
                    k = 8 * s + c
                    pe.wait_ge(lo_done, 48 + k + 1)
                    whi = w_hi[:, k % SPLIT, :].rearrange("p (a b) -> p a b", a=4)
                    wlo = w_lo[:, k % SPLIT, :].rearrange("p (a b) -> p a b", a=4)
                    o = ps[0:30, 2 + s, 0:256]
                    for j in range(4):
                        l = 4 * c + j
                        nc.tensor.matmul(o, ch[0][:, s, l, :], whi[:, j, :], start=l == 0, stop=False)
                        nc.tensor.matmul(o, ch[0][:, s, l, :], wlo[:, j, :], start=False, stop=False)
                        m = nc.tensor.matmul(o, ch[1][:, s, l, :], whi[:, j, :], start=False, stop=l == CMP_LEN - 1)
                    m.then_inc(chunk_used, 1)

            def bc_chunks(c0, c1):
                for c in range(c0, c1):
                    if c % 8 == 0:
                        pe.wait_ge(acc_free, U_B + c // 8)
                    mm_chunk(pe, Q_B, c, lh, (2 * (c % 8), 2 * (c % 8) + 1), acc(0), c % 8 == 0, c % 8 == 7)

            bc_chunks(0, 2)
            pe.wait_ge(cmp_gelu, 1)
            for x in range(4):
                m = nc.tensor.transpose(ps[:, 4, 30 * x:30 * (x + 1)], hgr[:, P * x:P * (x + 1)], ident[0:30, 0:30])
            m.then_inc(cmp_pe, 1)
            bc_chunks(2, 3)
            pe.wait_ge(cmp_gelu, 2)
            for h in range(2):
                nc.tensor.matmul(ps[:, 5, 0:30], w2[:, 0, h, :], hg[:, 0, h, :], start=h == 0, stop=h == 1)
            for kv in range(KV):
                for h in range(2):
                    m = nc.tensor.matmul(ps[0:N_CMP, 6 + kv, 0:P], hg[:, 1, h, N_CMP * kv:N_CMP * (kv + 1)], w2[:, 1, h, :],
                                         start=h == 0, stop=h == 1)
            m.then_inc(cmp_pe, 1)
            bc_chunks(3, AMID_A[0])
            pe.wait_ge(cmp_done, 1)
            pe_attend(pe, ua, 0, 0, 0, TA, lambda i: bc_chunks(amid(AMID_A, i - 1), amid(AMID_A, i)))
            bc_chunks(AMID_A[2], AMID_B[0])
            pe.wait_ge(acc_free, U_C)
            pe_attend(pe, ub, N_B, E_B, G_B, TA, lambda i: bc_chunks(amid(AMID_B, i - 1), amid(AMID_B, i)))

            def merge_chunks(c0, c1):
                for c in range(c0, c1):
                    n, k = c // 12, c % 12
                    if k in (0, 8):
                        pe.wait_ge(acc_free, U_M + 2 * n + k // 8)
                    j = k if k < 8 else k - 8
                    mm_chunk(pe, Q_M, c, lh if k < 8 else mh, (2 * j, 2 * j + 1), acc(0), k in (0, 8), k in (7, 11))

            merge_chunks(0, AMID_C[0])
            pe_attend(pe, uc, N_C, E_C, G_C, TA, lambda i: merge_chunks(amid(AMID_C, i - 1), amid(AMID_C, i)))
            pe.wait_ge(at_qk, E_D)
            pe.wait_ge(at_l, N_END)
            pe.wait_ge(acc_free, U_M + 4)
            for n in (2, 3):
                mm_block(pe, Q_M + 3, U_M + 2 * n, 0, lh, k0=12 * (n - 2))
                mm_block(pe, Q_M + 3, U_M + 2 * n + 1, 1, mh, k0=12 * (n - 2) + 8, nch=4)
            with pe.Fori(0, 2) as i:
                for e in range(2):
                    q, u = Q_M + 6 + 3 * i, U_M + 8 + 2 * e + 4 * i
                    mm_block(pe, q, u, 0, lh, k0=12 * e)
                    mm_block(pe, q, u + 1, 1, mh, k0=12 * e + 8, nch=4, kt0=8)
            for n in range(4):
                q, u = Q_M + 12 + 3 * (n // 2), U_M + 16 + 2 * n
                hook = None
                if n > 0:
                    def hook(n=n):
                        turn(pe, T_MIX + n - 1, mix[n - 1], (merged, 5 + n))
                mm_block(pe, q, u, 0, lh, k0=12 * (n % 2), hook=hook)
                if n == 0:
                    pe.wait_ge(at_o, G_END)
                mm_block(pe, q, u + 1, 1, cx, k0=12 * (n % 2) + 8, nch=4)
            for b in range(4):
                def hook(b=b):
                    if b == 0:
                        turn(pe, T_MIX + 3, mix[3], (merged, 9))
                    else:
                        turn(pe, T_O + b - 1, xres[:, :, BW * (b - 1):BW * b], (acc_free, U_O + b))
                mm_block(pe, Q_O + b, U_O + b, b % 2, mh, need=(lhs_ready, T_MIX) if b == 0 else None, hook=hook)

            def mlp_group(q, u, t, r, first=False, last=False):
                for b in range(4):
                    hook = None
                    if b > 0:
                        def hook(b=b):
                            turn(pe, t + b - 1, hid, (rows_ready, r + b))
                    elif first:
                        def hook():
                            turn(pe, T_O + 3, xres[:, :, 3 * BW:4 * BW], (acc_free, U_O + 4))
                    mm_block(pe, q + b, u + b, b % 2, lh, need=(lhs_ready, T_O) if first and b == 0 else None, hook=hook)
                for b in range(4):
                    hook = None
                    if b == 0:
                        def hook():
                            turn(pe, t + 3, hid, (rows_ready, r + 4))
                    elif last:
                        def hook(b=b):
                            turn(pe, t + 3 + b, xres[:, :, BW * (b - 1):BW * b], (merged, 9 + b))
                    mm_block(pe, q + 4 + b, u + 4 + b, b % 2, mh, need=(lhs_ready, t) if b == 0 else None, hook=hook,
                             hook_at=3 if last and b > 0 else 1)

            mlp_group(Q_MLP, U_MLP, T_MLP, 0, first=True)
            with pe.Fori(1, 3) as g:
                mlp_group(Q_MLP + 8 * g, U_MLP + 8 * g, T_MLP + 4 * g, 4 * g)
            mlp_group(Q_MLP + 24, U_MLP + 24, T_MLP + 12, 12, last=True)
            def pool_product(b):
                pe.wait_ge(pool_dve, 1 + 3 * b)
                pe.wait_ge(raw_in[b], 16 * (Q_AB + AB_POOL + 1))
                if b == 1:
                    pe.wait_ge(pool_dve, 2)
                pw = raw[:, b, :].rearrange("p (k c) -> p k c", k=4)
                for j in range(4):
                    o = pool_out[:, j, :]
                    for c in range(2):
                        m = nc.tensor.matmul(o, pw[:, 2 * (j // 2) + c, P * (j % 2):P * (j % 2 + 1)],
                                             pu[:, 2 * (j // 2) + c, PAD:],
                                             start=c == 0, stop=c == 1)
                    if (b, j) == (0, 0):
                        m.then_inc(chunk_used, 2)
                m.then_inc(pool_pe, 1)

            def index_step(p):
                if p == 0:
                    pe.wait_ge(ix_rows, 1)
                    pe.wait_ge(pool_dve, 6)
                    pe.wait_ge(lhs_ready, T_PU + 2)
                    for tt in range(2):
                        m = nc.tensor.transpose(ps[:, 5, tt * P:(tt + 1) * P], ki2[:, tt, :], ident[:])
                    m.then_inc(ix_t, 1)
                if p < IDX_HEADS // 2:
                    wait(pe, ix_q, p)
                    for tt in range(2):
                        m = nc.tensor.transpose(ps[:, 4 + p % 2, tt * P:(tt + 1) * P], zab[:, tt, AB_QI + P * p:AB_QI + P * (p + 1)], ident[:])
                    m.then_inc(ix_t, 1)
                if p > 0:
                    pe.wait_ge(ix_q, p + 1)
                    for e in range(2):
                        h = 2 * (p - 1) + e
                        wait(pe, ix_r, h - 1)
                        r = slice(IDX_DIM * e, IDX_DIM * (e + 1))
                        qs = TD["qk"][(p - 1) % 2][r, :]
                        nc.tensor.matmul(ps[:, 6 + e, 0:256], qs[:, P:2 * P], kiT[r, :], start=True, stop=True)
                        nc.tensor.matmul(ps[:, 6 + e, 256:384], qs[:, 0:P], kiT[r, 0:P], start=True, stop=True).then_inc(ix_s, 1)

            for b, (c, w) in enumerate(AB_BLOCKS):
                def each(c, b=b):
                    if (b, c) == (0, 1):
                        turn(pe, T_X1 + 3, xres[:, :, 3 * BW:4 * BW], (merged, 13))
                    if (b, c) == (3, 3):
                        turn(pe, T_PU, zab[:, :, AB_U:AB_U + BW], (acc_free, U_AB + 3))
                    if (b, c) == (4, 3):
                        turn(pe, T_PU + 1, zab[:, :, AB_U + BW:AB_U + 2 * BW], (acc_free, U_AB + 3))
                    if (b, c) == (AB_POOL, 4):
                        pool_product(1)
                    p = 8 * (b - AB_POOL - 1) + c - 1
                    if 0 <= p <= IDX_HEADS // 2:
                        index_step(p)

                if b == AB_POOL:
                    pe.wait_ge(lo_done, 8 * (Q_AB + b) + 2)
                    pool_product(0)
                mm_block(pe, Q_AB + b, U_AB + b, b % 2, lh, w=w, k0=0 if b < AB_POOL else O2,
                         need=(lhs_ready, T_X1) if b == 0 else None, each=each)
            pe.wait_ge(ix_r, IDX_HEADS)
            pe.wait_ge(acc_free, U_AB + 11)

            def out_chunks(q, o, u, c0, c1):
                for c in range(c0, c1):
                    n = c // 4 if c < OUT_ENDS[0] - 4 else c // 4 - 1
                    first = c % 4 == 0 and c != OUT_ENDS[0] - 4
                    last = c % 4 == 3 and c != OUT_ENDS[0] - 5
                    if first and n != 3:
                        pe.wait_ge(acc_free, u + n if n < 3 else u + n - 1)
                    kt = 8 * OUT_ORDER[c // 4][1] + 2 * (c % 4)
                    mm_chunk(pe, q, o + c, mh, (kt, kt + 1), acc(n % 2 if n > 2 else 0), first, last)

            def mixer_out(q, o, u, other, us, n, e, g):
                pe.wait_ge(*other)
                pe_attend(pe, us, n, e, g, TD, lambda i: out_chunks(q, o, u, amid(AMID_OUT, i - 1), amid(AMID_OUT, i)))
                pe.wait_ge(at_qk, e + HEADS)
                out_chunks(q, o, u, OUT_PARTS, OUT_ENDS[0] - 4)
                pe.wait_ge(at_l, n + HEADS)
                pe.wait_ge(at_ptc, n + HEADS)
                pe.wait_ge(at_o, g + HEADS)
                out_chunks(q, o, u, OUT_ENDS[0] - 4, OUT_ENDS[3])

            def new_x(x_t):
                return lambda b: turn(pe, x_t + b, xres[:, :, BW * b:BW * (b + 1)], (rows_ready, X_ROWS[x_t] + b + 1))

            def ffn(q, o, u, t, x_t, h):
                for g in range(2):
                    def pair(j, first=False):
                        def before():
                            turn(pe, t + 8 * g + 2 * j - 1, hid2, (acc_free, u + 12 * g + 2 * j))

                        def mine():
                            turn(pe, t + 8 * g + 2 * j, hid2, (acc_free, u + 12 * g + 2 * j + 1))
                        mm_block(pe, q + 12 * g + 2 * j, u + 12 * g + 2 * j, 0 if u % 2 == 0 else 1, lh, k0=o,
                                 need=(lhs_ready, x_t) if first and g == 0 else None, hook=None if first else before,
                                 turns=new_x(x_t) if first and g == 0 else None)
                        mm_block(pe, q + 12 * g + 2 * j + 1, u + 12 * g + 2 * j + 1, 1 if u % 2 == 0 else 0, lh, k0=o, hook=mine)
                    pair(0, first=True)
                    with pe.Fori(1, 4) as j:
                        pair(j)
                    for b in range(4):
                        def last():
                            turn(pe, t + 8 * g + 7, hid2, (acc_free, u + 12 * g + 8))
                        mm_block(pe, q + 12 * g + 8 + b, u + 12 * g + 8 + b, (u + b) % 2, mh, k0=o,
                                 need=(hid_ready, h + 4 * g) if b == 0 else None, hook=last if b == 0 else None)

            mixer_out(Q_ABO, O2, U_ABO, (pool_dve, 6), ud, N_D, E_D, G_D)
            ffn(Q_F0, O2, U_F0, T_F0, T_ABX, 0)
            def lru_round(n):
                if n == 0:
                    pe.wait_ge(lo_done, 8 * (Q_CD + CD_LRU) + O2 + 2)
                    pe.wait_ge(squares_done, 64)
                    pe.wait_ge(lru_v, 1)
                else:
                    pe.wait_ge(lru_a, n)
                x = n // 2
                pe.wait_ge(raw_in[O2 + x], 16 * (Q_CD + CD_LRU + 1))
                lw = raw[:, O2 + x, :].rearrange("p (n c) -> p n c", n=LRU_T)
                for j in range(4):
                    t = 4 * (n % 2) + j
                    m = nc.tensor.matmul(pool_out[:, j, :], lw[:, t, :], xc[:, t, :], start=True, stop=True)
                    if (n, j) == (0, 0):
                        m.then_inc(chunk_used, 2)
                m.then_inc(lru_pe, 1)

            for b, (c, w) in enumerate(CD_BLOCKS):
                def each(c, b=b):
                    if (b, c) == (CD_LRU, 0):
                        lru_round(1)
                    if c == 3 and 0 < b < 5:
                        z = zx if b < 3 else zy
                        turn(pe, T_CD + b - 1, z[:, :, BW * ((b - 1) % 2):BW * ((b - 1) % 2 + 1)], (acc_free, U_CD + b))
                    if b == CD_LRU and c in (3, 4):
                        lru_round(c - 1)
                    if (b, c) == (5, 3):
                        turn(pe, T_CQ, zc[:, :, 0:BW], (acc_free, U_CD + 5))

                if b == CD_LRU:
                    lru_round(0)
                mm_block(pe, Q_CD + b, U_CD + b, (U_CD + b) % 2, lh, k0=O2 if b < CD_LRU else O4, w=w,
                         need=(lhs_ready, T_FX) if b == 0 else None, turns=new_x(T_FX) if b == 0 else None, each=each)
            turn(pe, T_CQ + 1, zc[:, :, BW:BW + 256], (acc_free, U_CD + 6), n=2)
            pe.wait_ge(lhs_ready, T_CQ + 2)
            for c in range(6):
                u = U_UP + c // 2
                pe.wait_ge(acc_free, u - 1)
                mm_chunk(pe, Q_UP, O4 + c, mh, (8, 9, 10, 11), ps[:, 2 * (u % 2):2 * (u % 2) + 2, 256 * (c % 2):256 * (c % 2 + 1)], True, True, 256)
            for c in range(4):
                u = U_UP + 3 + c
                pe.wait_ge(acc_free, u - 1)
                mm_chunk(pe, Q_UP, O4 + 6 + c, mh, (12, 13), acc(u % 2), True, True)
            turn(pe, T_QR, kr2, (rope_v, 2), n=1)
            turn(pe, T_QR + 1, qrow.rearrange("p t h c -> p t (h c)"), (rope_v, 3))
            pe.wait_ge(lhs_ready, T_QR + 2)
            pe.wait_ge(acc_free, U_UP + 7)
            pe.wait_ge(squares_done, 68)
            mixer_out(Q_CDO, O6, U_CDO, (lru_v, 4), um, N_L, E_L, G_L)
            ffn(Q_F1, O6, U_F1, T_F1, T_CDX, 8)

        @block.scalar
        def _(act):
            aseq = [0]

            def squares(rows, col, sums):
                for tt in range(2):
                    wait(act, squares_done, aseq[0] - 1)
                    aseq[0] += 1
                    i = nc.scalar.activation(ps[:, 6 + tt, 0:rows.shape[2]], rows[:, tt, :], ACT.Square,
                                             accum_out=sums[:, tt, col:col + 1]).then_inc(squares_done, 1)

            def root(k, out, mean):
                act.wait_ge(stat_v, 2 * k + 1)
                nc.scalar.activation(out, mean, ACT.Sqrt).then_inc(stat_a, 1)

            def scaled(b, u, used, dst, scale, par, w=BW, func=ACT.Copy):
                act.wait_ge(chunk_used, used)
                for tt in range(2):
                    i = nc.scalar.activation(dst(tt), acc(par, w)[:, tt, :], func, scale=scale[:, tt:tt + 1])
                i.then_inc(acc_free, 1)

            act.wait_ge(head_in, 32)
            for j in range(4):
                turn_hi(act, j, tiles(lh, 4 * j), gains("norm_mix")[:, 4 * j:4 * j + 4])
                split_hi(act, 0, (2 * j, 2 * j + 1))
                if j == 1:
                    squares(xres[:, :, 0:BW], 0, ssp)
                if j > 0:
                    squares(xres[:, :, BW * j:BW * (j + 1)], j, ssp)
            root(0, ST["root"], ST["mean"])
            act.wait_ge(stat_v, 2)
            for b, (c, w) in enumerate(A_BLOCKS):
                split_hi(act, b, range(8 if b == 0 else 6, 12))
                if b < 5:
                    scaled(b, b, 8 * b + 8, lambda tt, c=c, w=w: zA[:, tt, c:c + w], ST["rstd"], b % 2, w=w)
                    split_hi(act, b, (12, 13))
                    if b == 1:
                        act.wait_ge(cw_ready, 1)
                        for x in range(4):
                            i = nc.scalar.activation(ch[0][:, x // 2, :, N_CMP * (x % 2):N_CMP * (x % 2 + 1)],
                                                     cwin[x].rearrange("p (l c) -> p l c", l=CMP_LEN), ACT.Copy)
                        i.then_inc(thi_done, 1)
                else:
                    act.wait_ge(sp_v, 1)
                    nc.scalar.activation(sp_e, sp_t, ACT.Exp).then_inc(sp_a, 1)
                    act.wait_ge(chunk_used, 48)
                    n = A_TAIL - GATE_COLS
                    for tt in range(2):
                        nc.scalar.activation(zA[:, tt, A_COLS - n:A_COLS], acc(1, n)[:, tt, :], ACT.Copy, scale=ST["rstd"][:, tt:tt + 1])
                    for tt in range(2):
                        i = nc.scalar.activation(gsb[:, 1 - tt, :], ps[:, 2 + tt, n:A_TAIL], ACT.Sigmoid, scale=ST["rstd"][:, tt:tt + 1])
                    i.then_inc(acc_free, 1)
            split_hi(act, 6, range(4, 20))
            act.wait_ge(chunk_used, 64)
            nc.scalar.activation(hgr.rearrange("p (s h) -> p s h", s=2), ps[0:30, 2:4, 0:256], ACT.Gelu_apprx_tanh).then_inc(cmp_gelu, 1)
            act.wait_ge(cmp_pe, 1)
            nc.scalar.activation(hg.rearrange("p a b c -> p (a b c)"), ps[:, 4, 0:120], ACT.Copy).then_inc(cmp_gelu, 1)

            def bc_amid(plan, i):
                done, before = amid(plan, i - 1), amid(plan, i - 2)
                if i > 0 and done // 8 > before // 8:
                    b = before // 8
                    z, c = (zB, BW * b) if b < 3 else (zC, BW * (b - 3))
                    scaled(b, U_B + b, 8 * (Q_B + b) + 8, lambda tt: z[:, tt, c:c + BW], ST["rstd"], 0)
                split_hi(act, Q_B, range(SPLIT if i == 0 else split_to(plan, i - 1), split_to(plan, i)))

            act_attend(act, ua, 0, 0, 0, TA, lambda i: bc_amid(AMID_A, i))
            scaled(0, U_C, 8 * Q_C + 8, lambda tt: zC[:, tt, 0:BW], ST["rstd"], 0)
            split_hi(act, Q_B, range(split_to(AMID_A, len(ua) + 3), AMID_B[0] + SPLIT))
            act_attend(act, ub, N_B, E_B, G_B, TA, lambda i: bc_amid(AMID_B, i) if i > 0 else None)
            bc_amid(AMID_B, len(ub) + 4)

            def gate_block(n):
                scaled(0, U_M + 2 * n, 8 * Q_M + 12 * n + 8, lambda tt: mix[n][:, tt, :], ST["rstd"], 0, func=ACT.Sigmoid)

            def merge_amid(i):
                done, before = amid(AMID_C, i - 1), amid(AMID_C, i - 2) if i > 0 else 0
                for n in range(2):
                    if before < 12 * n + 8 <= done:
                        gate_block(n)
                split_hi(act, Q_M, range(SPLIT if i == 0 else split_to(AMID_C, i - 1), split_to(AMID_C, i)))

            act_attend(act, uc, N_C, E_C, G_C, TA, merge_amid)
            split_hi(act, Q_M, (28, 29))

            def gate_unit(q, e, u):
                split_hi(act, q, range(12 * e + 6, 12 * e + 12))
                act.wait_ge(acc_free, u)
                scaled(0, u, 8 * q + 12 * e + 8, lambda tt: sg[:, tt, :], ST["rstd"], 0, func=ACT.Sigmoid)
                split_hi(act, q, range(12 * e + 12, 12 * e + 18))

            for n in (2, 3):
                split_hi(act, Q_M, range(12 * n + 6, 12 * n + 12))
                gate_block(n)
                split_hi(act, Q_M, range(12 * n + 12, 12 * n + 18))
            with act.Fori(0, 2) as i:
                for e in range(2):
                    gate_unit(Q_M + 6 + 3 * i, e, U_M + 8 + 2 * e + 4 * i)
            for n in range(4):
                gate_unit(Q_M + 12 + 3 * (n // 2), n % 2, U_M + 16 + 2 * n)
                turn_hi(act, T_MIX + n, tiles(mh, 4 * n))
            for b in range(4):
                split_hi(act, Q_O + b, range(6, 12))
                act.wait_ge(acc_free, U_O + b + 1)
                squares(xres[:, :, BW * b:BW * (b + 1)], b, ssp)
                split_hi(act, Q_O + b, (12, 13))
                turn_hi(act, T_O + b, tiles(lh, 4 * b), gains("norm_mlp")[:, 4 * b:4 * b + 4])
            root(1, ST["root"], ST["mean"])
            act.wait_ge(stat_v, 4)

            def mlp_group(q, u, t, last=False):
                for b in range(4):
                    split_hi(act, q + b, range(6, 12))
                    wait(act, tp_done, t + b)
                    scaled(b, u + b, 8 * (q + b) + 8, lambda tt: hid[:, tt, :], ST["rstd"], b % 2, func=ACT.Relu)
                    split_hi(act, q + b, (12, 13))
                    turn_hi(act, t + b, tiles(mh, 4 * b))
                for b in range(4):
                    split_hi(act, q + 4 + b, range(6, 12))
                    if last:
                        act.wait_ge(acc_free, u + 5 + b)
                        squares(xres[:, :, BW * b:BW * (b + 1)], b, ssp)
                    split_hi(act, q + 4 + b, (12, 13))
                    if last:
                        turn_hi(act, t + 4 + b, tiles(lh, 4 * b), gains("mix_pre")[:, 4 * b:4 * b + 4])
                        squares(xres[:, :, BW * b:BW * (b + 1)], b, ssp2)

            with act.Fori(0, 3) as g:
                mlp_group(Q_MLP + 8 * g, U_MLP + 8 * g, T_MLP + 4 * g)
            mlp_group(Q_MLP + 24, U_MLP + 24, T_MLP + 12, last=True)
            root(2, ST["root"], ST["mean"])
            root(3, ST["root2"], ST["mean2"])
            act.wait_ge(stat_v, 8)
            def pool_in(b):
                act.wait_ge(pool_seq, 1)
                act.wait_ge(tp_done, T_PU + b + 1)
                wait(act, pool_pe, b)
                nc.scalar.activation(pu[:, :, PAD:], tp4, ACT.Copy).then_inc(thi_done, 1)

            def pool_hi(b):
                act.wait_ge(pool_dve, 2 + 3 * b)
                nc.scalar.activation(mh[0][:, 8 + 4 * b:12 + 4 * b, :], pb[:, :, PAD:], ACT.Copy).then_inc(pool_act, 1)

            def index_step(p):
                if p == 0:
                    act.wait_ge(ix_t, 1)
                    nc.scalar.activation(kiT, ps[:, 5, 0:TOK], ACT.Copy).then_inc(ix_q, 1)
                if p < IDX_HEADS // 2:
                    act.wait_ge(ix_t, p + 2)
                    wait(act, ix_s, 2 * (p - 1))
                    nc.scalar.activation(TD["qk"][p % 2][:, 0:TOK], ps[:, 4 + p % 2, 0:TOK], ACT.Copy).then_inc(ix_q, 1)
                if p > 0:
                    for e in range(2):
                        h = 2 * (p - 1) + e
                        act.wait_ge(ix_s, h + 1)
                        wait(act, ix_d, h - 1)
                        nc.scalar.activation(relu_h[e], ps[:, 6 + e, 0:384], ACT.Relu).then_inc(ix_r, 1)

            for b, (c, w) in enumerate(AB_BLOCKS):
                o, q = (0 if b < AB_POOL else O2), Q_AB + b
                if b == AB_POOL:
                    pool_in(1)
                    pool_hi(0)
                    split_hi(act, q, (6, 7))
                if b == AB_POOL + 2:
                    index_step(8)
                for x in range(6):
                    if b == AB_POOL + 1:
                        if x == 0:
                            pool_hi(1)
                        index_step(x)
                    split_hi(act, q, (o + 6 + x,))
                scaled(0, 0, 8 * q + o + 8, lambda tt: zab[:, tt, c:c + w], ST["rstd12"], b % 2, w=w)
                if b < 10:
                    for x in range(2):
                        if b == AB_POOL + 1:
                            index_step(6 + x)
                        split_hi(act, q, (o + 12 + x,))
                if b == 3:
                    pool_in(0)

            def mixer_out(q, o, u, us, n, e, g, k, t, gain):
                act_attend(act, us, n, e, g, TD, lambda i: split_hi(
                    act, q, range(o + (SPLIT if i == 0 else split_to(AMID_OUT, i - 1)), o + split_to(AMID_OUT, i))))
                at = split_to(AMID_OUT, HEADS + 3)
                for b, end in enumerate(OUT_ENDS):
                    split_hi(act, q, range(o + at, o + end + SPLIT))
                    at = end + SPLIT
                    act.wait_ge(acc_free, u + 3 + b + 1)
                    squares(macc[:, :, BW * b:BW * (b + 1)], b, ssp)
                new_x(q + 4, o, k, t, gain)

            def new_x(q, o, k, t, gain):
                root(k, ST["root"], ST["mean"])
                for b in range(4):
                    turn_hi(act, t + b, tiles(lh, 4 * b), gain[:, 4 * b:4 * b + 4])
                    squares(xres[:, :, BW * b:BW * (b + 1)], b, ssp)
                    if 0 < b < 3:
                        split_hi(act, q, (o + 2 * b + 2, o + 2 * b + 3))
                root(k + 1, ST["root"], ST["mean"])
                act.wait_ge(stat_v, 2 * k + 4)

            def ffn(q, o, u, t, c0, layer, end):
                act.wait_ge(gain_in, 16 * (4 + 4 * layer))
                for g in range(2):
                    for j in range(4):
                        for val in range(2):
                            b = 12 * g + 2 * j + val
                            tn = t + 8 * g + 2 * j + val
                            cn = c0 + 8 * g + 2 * j + val
                            split_hi(act, q + b, range(o + 8, o + 12))
                            wait(act, tp_done, tn)
                            scaled(0, 0, 8 * (q + b) + o + 8, lambda tt: hid2[:, tt, :], ST["rstd"], (u + b) % 2)
                            if val:
                                act.wait_ge(lhs_ready, tn)
                                nc.scalar.activation(cg, cg, ACT.Gelu_apprx_tanh).then_inc(conv_m, 1)
                            split_hi(act, q + b, (o + 12, o + 13))
                            act.wait_ge(tp_done, tn + 1)
                            if not val:
                                wait(act, hid_ready, 8 * layer + 4 * g + j)
                            dst = cv if val else cg
                            for x in range(4):
                                k = conv_tiles(g, j, val) + x
                                i = nc.scalar.activation(dst[:, x, :], tp4[:, x, :], ACT.Identity, scale=fcw[:, 2, k:k + 1], bias=fcb[:, k:k + 1])
                            i.then_inc(thi_done, 1)
                            split_hi(act, q + b, (o + 14, o + 15))
                            if val:
                                n = (cn + 1) // 2
                                act.wait_ge(conv_ready, n)
                                nc.scalar.activation(mh[0][:, 4 * j:4 * j + 4, :], cg, ACT.Copy).then_inc(hid_hi, 1)
                    for b in range(4):
                        x = q + 12 * g + 8 + b
                        if not (end and g == 1 and b == 3):
                            split_hi(act, x, range(o + 8, o + 12))
                        if g == 1:
                            act.wait_ge(acc_free, u + 12 * g + 9 + b)
                            squares(macc[:, :, BW * b:BW * (b + 1)], b, ssp)
                        if g == 0 or b < 3:
                            split_hi(act, x, range(o + 12, o + 16))

            mixer_out(Q_ABO, O2, U_ABO, ud, N_D, E_D, G_D, 4, T_ABX, gains("ffn_pre"))
            ffn(Q_F0, O2, U_F0, T_F0, 0, 0, False)
            new_x(Q_CD, O2, 6, T_FX, gains("mix_pre", 1))
            def lru_gates(n):
                dst, bias = (rr, "ba") if n < 2 else (ii, "bx")
                act.wait_ge(lru_pe, n + 1)
                for j in range(4):
                    t = 4 * (n % 2) + j
                    i = nc.scalar.activation(dst[:, t, :], pool_out[:, j, :], ACT.Sigmoid, bias=pk[:, PACK[bias] + t:PACK[bias] + t + 1])
                i.then_inc(lru_a, 1)

            def lru_exp():
                act.wait_ge(lru_a, 2)
                for n in range(LRU_T):
                    i = nc.scalar.activation(decay_a[:, n, :], rr[:, n, :], ACT.Exp, scale=decay[:, n:n + 1])
                i.then_inc(lru_a, 1)

            def lru_tanh():
                act.wait_ge(lru_a, 5)
                for n in range(LRU_T):
                    i = nc.scalar.activation(rr[:, n, :], rr[:, n, :], ACT.Tanh, scale=decay[:, n:n + 1])
                i.then_inc(lru_a, 1)

            def turned_in(b):
                act.wait_ge(tp_done, T_CD + b + 1)
                if b < 2:
                    nc.scalar.activation(xin[:, 4 * b:4 * b + 4, 3:], tp4, ACT.Copy).then_inc(thi_done, 1)
                else:
                    nc.scalar.activation(gy[:, 4 * b - 8:4 * b - 4, :], tp4, ACT.Gelu_apprx_tanh).then_inc(thi_done, 1)

            for b, (c, w) in enumerate(CD_BLOCKS):
                q, o = Q_CD + b, O2 if b < CD_LRU else O4
                if b == CD_LRU:
                    for x in range(2):
                        lru_gates(x)
                        split_hi(act, q, (o + 4 + x,))
                for x in range(2 if b == 0 else 0, 6):
                    if b == CD_LRU and x == 1:
                        lru_gates(2)
                        turned_in(b - 1)
                        lru_gates(3)
                    if b == CD_LRU and x == 4:
                        lru_exp()
                    if b == CD_LRU + 1 and x == 0:
                        lru_tanh()
                    if b == CD_LRU + 1 and x == 5:
                        act.wait_ge(rope_v, 1)
                        nc.scalar.activation(sinv, ang, ACT.Sin)
                        nc.scalar.activation(half, ang, ACT.Sin, scale=0.5).then_inc(rope_a, 1)
                    split_hi(act, q, (o + 6 + x,))
                    if x == 2 and 0 < b < CD_LRU:
                        turned_in(b - 1)
                    if x == 2 and b == 5:
                        turn_hi(act, T_CQ, tiles(mh, 8), pk[:, PACK["q_norm"]:PACK["q_norm"] + 4])
                dst = [lambda tt, z=z, a=a: z[:, tt, a:a + BW] for z in (zx, zy) for a in (0, BW)]
                dst += [lambda tt: zc[:, tt, 0:512], lambda tt: zc[:, tt, 512:832]]
                scaled(0, 0, 8 * q + o + 8, dst[b], ST["rstd"], (U_CD + b) % 2, w=w)
                if b < 5:
                    split_hi(act, q, (o + 12, o + 13))
            turn_hi(act, T_CQ + 1, tiles(mh, 12), pk[:, PACK["kv_norm"]:PACK["kv_norm"] + 2], n=2)
            squares(zc[:, :, 0:512], 0, ssp)
            squares(zc[:, :, 512:768], 1, ssp)
            act.wait_ge(stat_v, 17)
            nc.scalar.activation(ST["root"], ST["mean"], ACT.Sqrt)
            nc.scalar.activation(ST["root2"], ST["mean2"], ACT.Sqrt).then_inc(stat_a, 1)
            act.wait_ge(lru_v, 2)
            nc.scalar.activation(mul, mul, ACT.Sqrt, scale=-1.0).then_inc(lru_a, 1)
            act.wait_ge(stat_v, 18)
            for j, n in enumerate(UP_CHUNKS):
                split_hi(act, Q_UP, range(O4 + 4 + (UP_CHUNKS[j - 1] if j else 0), O4 + 4 + n))
                z, c = (zq, BW * j) if j < 3 else (zkv, BW * (j - 3))
                scaled(0, 0, 8 * Q_UP + O4 + n, lambda tt: z[:, tt, c:c + BW], ST["rq"] if j < 3 else ST["rkv"], (U_UP + j) % 2)
            act.wait_ge(lru_v, 3)
            nc.scalar.activation(mh[0][:, 8:16, :], xc, ACT.Copy).then_inc(lru_a, 1)
            act.wait_ge(tp_done, T_QR + 1)
            nc.scalar.activation(krT, tp4[:, 0, :], ACT.Copy).then_inc(thi_done, 1)
            act.wait_ge(tp_done, T_QR + 2)
            nc.scalar.activation(qrT, tp4, ACT.Copy).then_inc(thi_done, 1)
            mixer_out(Q_CDO, O6, U_CDO, um, N_L, E_L, G_L, 9, T_CDX, gains("ffn_pre", 1))
            ffn(Q_F1, O6, U_F1, T_F1, 16, 1, True)
            root(11, ST["root"], ST["mean"])

        @block.vector
        def _(dve):
            seq = [0]

            def chain(i):
                seq[0] += 1
                i.then_inc(dve_seq, 1)
                dve.wait_ge(dve_seq, seq[0])

            def mean_square(n, out, sums, width=D):
                dve.wait_ge(squares_done, n)
                chain(nc.vector.tensor_reduce(out, sums, AX, ALU.add))
                nc.vector.tensor_scalar(out, out, 1.0 / width, EPS, ALU.mult, ALU.add).then_inc(stat_v, 1)

            def inverse(k, out, rt):
                dve.wait_ge(stat_a, k + 1)
                nc.vector.reciprocal(out, rt).then_inc(stat_v, 1)

            def bias_rows():
                dve.wait_ge(setup_pe, 1)
                nc.vector.tensor_tensor(r_rows, ps[0:24, 6, 0:384], m_rev, ALU.add).then_inc(setup_dve, 1)
                nc.vector.tensor_tensor(tbc.rearrange("p h (s c) -> p h s c", s=2),
                                        ps[:, 7, 0:256].rearrange("p (s c h) -> p h s c", s=2, h=HEADS)[:, :, :, 0:N_CMP],
                                        ccon[:, 0:30].rearrange("p (s c) -> p s c", s=2).unsqueeze(1).to_broadcast([P, HEADS, 2, N_CMP]), ALU.add)
                nc.vector.tensor_scalar(nsink, sinkb, -1.0, None, ALU.mult).then_inc(setup_dve, 1)
                lam = pk[:, PACK["lam"]:PACK["lam"] + 8]
                nc.vector.tensor_scalar(sp_m, lam, -1.0, 0.0, ALU.mult, ALU.max)
                nc.vector.scalar_tensor_tensor(sp_t, lam, -1.0, lam, ALU.mult, ALU.min).then_inc(sp_v, 1)

            def windows():
                dve.wait_ge(tp_done, T_CMP + 1)
                for x in range(4):
                    a = tp4[:, x, 0:1]
                    win = bass.AP(a.tensor, a.offset, [a.ap[0], [1, CMP_LEN], [CMP_STRIDE, N_CMP]])
                    i = nc.vector.tensor_tensor(cwin[x].rearrange("p (l c) -> p l c", l=CMP_LEN), win,
                                                post[:, x // 2, :].unsqueeze(2).to_broadcast([P, CMP_LEN, N_CMP]), ALU.add)
                i.then_inc(cw_ready, 1)
                dve.wait_ge(thi_done, T_CMP + 1)
                for x in range(4):
                    s = slice(N_CMP * (x % 2), N_CMP * (x % 2 + 1))
                    i = nc.vector.tensor_tensor(ch[1][:, x // 2, :, s], cwin[x].rearrange("p (l c) -> p l c", l=CMP_LEN),
                                                ch[0][:, x // 2, :, s].bitcast(F32), ALU.subtract)
                i.then_inc(lhs_ready, 1)

            dve.wait_ge(head_in, 32)
            for j in range(4):
                turn_lo(dve, j, tiles(lh, 4 * j), gains("norm_mix")[:, 4 * j:4 * j + 4])
                split_lo(dve, 0, (2 * j, 2 * j + 1))
            mean_square(8, ST["mean"], ssp)
            inverse(0, ST["rstd"], ST["root"])
            split_lo(dve, 0, range(8, 14))
            for b in range(1, 6):
                split_lo(dve, b, range(6, 14 if b < 5 else 12))
                if b == 1:
                    dve.wait_ge(small_in, 16 * N_SMALL)
                    windows()
                if b == 4:
                    bias_rows()
            dve.wait_ge(sp_a, 1)
            chain(nc.vector.tensor_scalar(sp_t, sp_e, 2.0, None, ALU.add))
            chain(nc.vector.reciprocal(sp_z, sp_t))
            chain(nc.vector.tensor_tensor(sp_z, sp_z, sp_e, ALU.mult))
            chain(nc.vector.tensor_tensor(sp_e, sp_z, sp_z, ALU.mult))
            chain(nc.vector.tensor_scalar(sp_t, sp_e, 1.0 / 15, None, ALU.mult))
            for n in (13, 11, 9, 7, 5, 3):
                chain(nc.vector.scalar_tensor_tensor(sp_t, sp_t, 1.0 / n, sp_e, ALU.add, ALU.mult))
            chain(nc.vector.scalar_tensor_tensor(sp_t, sp_t, 1.0, sp_z, ALU.add, ALU.mult))
            chain(nc.vector.scalar_tensor_tensor(sp_t, sp_t, 2.0, sp_m, ALU.mult, ALU.add))
            nc.vector.tensor_scalar(decay, sp_t, -8.0, None, ALU.mult)
            dve.wait_ge(acc_free, 6)
            nc.vector.tensor_tensor(gcm, gsb.rearrange("p s (h b) -> p s h b", b=3)[:, :, :, 0],
                                    ccon[:, 30:32].unsqueeze(2).to_broadcast([P, 2, 8]), ALU.mult)
            split_lo(dve, 6, range(4, 20))
            dve.wait_ge(cmp_pe, 2)
            nc.vector.tensor_copy(kct, ps[:, 5, 0:30])
            nc.vector.tensor_copy(vc[0:N_CMP, :, :], ps[0:N_CMP, 6:8, 0:P]).then_inc(cmp_done, 1)
            dve.wait_ge(tb_in, 32)

            def bc_amid(plan, i):
                split_lo(dve, Q_B, range(SPLIT if i == 0 else split_to(plan, i - 1), split_to(plan, i)))

            dve_attend(dve, ua, 0, 0, TA, chain, lambda i: bc_amid(AMID_A, i))
            split_lo(dve, Q_B, range(split_to(AMID_A, len(ua) + 3), AMID_B[0] + SPLIT))
            dve.wait_ge(tb_in, 64)
            dve_attend(dve, ub, N_B, G_B, TA, chain, lambda i: bc_amid(AMID_B, i) if i > 0 else None)
            bc_amid(AMID_B, len(ub) + 4)
            dve.wait_ge(tb_in, 96)

            def branch_block(n):
                dve.wait_ge(chunk_used, 8 * Q_M + 12 * n + 12)
                dve.wait_ge(acc_free, U_M + 2 * n + 1)
                nc.vector.tensor_tensor(mix[n], mix[n], acc(0 if n < 2 else 1), ALU.mult).then_inc(acc_free, 1)

            def merge_amid(i):
                done, before = amid(AMID_C, i - 1), amid(AMID_C, i - 2) if i > 0 else 0
                for n in range(2):
                    if before < 12 * n + 12 <= done:
                        branch_block(n)
                split_lo(dve, Q_M, range(SPLIT if i == 0 else split_to(AMID_C, i - 1), split_to(AMID_C, i)))

            dve_attend(dve, uc, N_C, G_C, TA, chain, merge_amid)
            split_lo(dve, Q_M, (28, 29))
            for n in (2, 3):
                split_lo(dve, Q_M, range(12 * n + 6, 12 * n + 16))
                branch_block(n)
                split_lo(dve, Q_M, (12 * n + 16, 12 * n + 17))

            def branch_unit(q, e, u, dst, merges=None):
                split_lo(dve, q, range(12 * e + 6, 12 * e + 16))
                dve.wait_ge(chunk_used, 8 * q + 12 * e + 12)
                dve.wait_ge(acc_free, u)
                if merges is not None:
                    wait(dve, merged, merges)
                nc.vector.tensor_tensor(dst, sg, acc(1), ALU.mult).then_inc(acc_free, 1)
                split_lo(dve, q, (12 * e + 16, 12 * e + 17))

            with dve.Fori(0, 2) as i:
                for e in range(2):
                    branch_unit(Q_M + 6 + 3 * i, e, U_M + 8 + 2 * e + 1 + 4 * i, ybuf, merges=2 * i + e + 1)
            for n in range(4):
                branch_unit(Q_M + 12 + 3 * (n // 2), n % 2, U_M + 16 + 2 * n + 1, ybuf, merges=5 + n)
                turn_lo(dve, T_MIX + n, tiles(mh, 4 * n))

            def add_x(q, u, b):
                dve.wait_ge(chunk_used, 8 * q + 8)
                dve.wait_ge(acc_free, u)
                o = xres[:, :, BW * b:BW * (b + 1)]
                nc.vector.tensor_tensor(o, acc(b % 2), o, ALU.add).then_inc(acc_free, 1)

            for b in range(4):
                split_lo(dve, Q_O + b, range(6, 12))
                add_x(Q_O + b, U_O + b, b)
                split_lo(dve, Q_O + b, (12, 13))
                if b == 3:
                    mean_square(16, ST["mean"], ssp)
                turn_lo(dve, T_O + b, tiles(lh, 4 * b), gains("norm_mlp")[:, 4 * b:4 * b + 4])
            inverse(1, ST["rstd"], ST["root"])

            def mlp_group(q, u, t, last=False):
                for b in range(4):
                    split_lo(dve, q + b, range(6, 12))
                    dve.wait_ge(acc_free, u + b + 1)
                    nc.vector.tensor_tensor(hid, hid, hid, ALU.mult).then_inc(rows_ready, 1)
                    split_lo(dve, q + b, (12, 13))
                    turn_lo(dve, t + b, tiles(mh, 4 * b))
                for b in range(4):
                    split_lo(dve, q + 4 + b, range(6, 12))
                    add_x(q + 4 + b, u + 4 + b, b)
                    split_lo(dve, q + 4 + b, (12, 13))
                    if last:
                        turn_lo(dve, t + 4 + b, tiles(lh, 4 * b), gains("mix_pre")[:, 4 * b:4 * b + 4])

            with dve.Fori(0, 3) as g:
                mlp_group(Q_MLP + 8 * g, U_MLP + 8 * g, T_MLP + 4 * g)
            mlp_group(Q_MLP + 24, U_MLP + 24, T_MLP + 12, last=True)
            mean_square(32, ST["mean"], ssp)
            inverse(2, ST["rstd"], ST["root"])
            dve.wait_ge(squares_done, 32)
            chain(nc.vector.tensor_reduce(ST["tmp0"], ssp2, AX, ALU.add))
            dve.wait_ge(stat_v, 6)
            chain(nc.vector.tensor_tensor(ST["tmp1"], ST["rstd"], ST["rstd"], ALU.mult))
            chain(nc.vector.tensor_tensor(ST["tmp0"], ST["tmp0"], ST["tmp1"], ALU.mult))
            nc.vector.tensor_scalar(ST["mean2"], ST["tmp0"], 1.0 / D, EPS, ALU.mult, ALU.add).then_inc(stat_v, 1)
            dve.wait_ge(stat_a, 4)
            chain(nc.vector.reciprocal(ST["rstd2"], ST["root2"]))
            nc.vector.tensor_tensor(ST["rstd12"], ST["rstd"], ST["rstd2"], ALU.mult).then_inc(stat_v, 1)
            split_lo(dve, Q_AB, range(6, 14))
            dve.wait_ge(tp_done, T_X1 + 4)
            for tt in range(2):
                nc.vector.tensor_scalar(xres[:, tt, :], xres[:, tt, :], ST["rstd"][:, tt:tt + 1], None, ALU.mult)
            def index_rows():
                dve.wait_ge(acc_free, U_AB + 3)
                nc.vector.tensor_copy(ki2.rearrange("p t (a c) -> p t a c", a=2),
                                      zab[:, :, AB_KI:AB_KI + IDX_DIM].unsqueeze(2).to_broadcast([P, 2, 2, IDX_DIM]))
                nc.vector.tensor_scalar(wi_s.rearrange("p (t h) -> p t h", t=2), zab[:, :, AB_KI + IDX_DIM:AB_U],
                                        float(IDX_DIM * IDX_HEADS) ** -0.5, None, ALU.mult).then_inc(ix_rows, 1)

            S = slice(PAD, PAD + TOK)

            def doubled(dst, src, n, tl):
                chain(nc.vector.tensor_tensor(dst[:, tl:, S], src[:, tl:, S], src[:, tl:, PAD - n:PAD + TOK - n], ALU.add))

            def pooled(sums, g):
                x = slice(2 * (g % 2), 2 * (g % 2) + 2)
                chain(nc.vector.scalar_tensor_tensor(pu[:, x, 2 * PAD:], sums[:, x, 2 * PAD:], 1.0 / POOL_WINDOWS[g],
                                                     pu[:, x, 2 * PAD:], ALU.mult, ALU.subtract))
                h = slice(PAD, 2 * PAD)
                chain(nc.vector.tensor_tensor(sums[:, x, h], sums[:, x, h],
                                              inv_head[:, g:g + 1, :].to_broadcast([P, 2, PAD]), ALU.mult))
                return nc.vector.tensor_tensor(pu[:, x, h], sums[:, x, h], pu[:, x, h], ALU.subtract)

            def pool_sums(b):
                dve.wait_ge(aux_in, 16)
                dve.wait_ge(thi_done, T_PU + b + 1)
                dve.sem_inc(lhs_ready, 1)
                doubled(pa, pu, 1, 0)
                if b == 0:
                    doubled(pb, pa, 2, 2)
                else:
                    doubled(pb, pa, 2, 0)
                    doubled(pa, pb, 4, 0)

            def pool_means(b):
                if b == 1:
                    doubled(pb, pa, 8, 2)
                pooled(pa, 2 * b)
                pooled(pb, 2 * b + 1).then_inc(pool_dve, 1)

            def pool_scaled(b):
                dve.wait_ge(pool_pe, b + 1)
                for j in range(4):
                    c = 4 * b + j
                    i = nc.vector.tensor_scalar(pb[:, j, PAD:], pool_out[:, j, :], pk[:, PACK["pool_b"] + c:PACK["pool_b"] + c + 1],
                                                pk[:, PACK["pool_scale"] + c:PACK["pool_scale"] + c + 1], ALU.add, ALU.mult)
                i.then_inc(pool_dve, 1)

            def pool_lo(b):
                dve.wait_ge(pool_act, b + 1)
                nc.vector.tensor_tensor(mh[1][:, 8 + 4 * b:12 + 4 * b, :], pb[:, :, PAD:],
                                        mh[0][:, 8 + 4 * b:12 + 4 * b, :].bitcast(F32), ALU.subtract).then_inc(pool_dve, 1)

            def index_step(p):
                for h in range(max(2 * p - 2, 0), 2 * p):
                    dve.wait_ge(ix_r, h + 1)
                    wait(dve, ix_d, h)
                    r = relu_h[h % 2]
                    for a, w, tt in ((0, 256, 1), (256, 128, 0)):
                        wc = wi_s[:, 16 * tt + h:16 * tt + h + 1]
                        if h == 0:
                            i = nc.vector.tensor_scalar(score[:, a:a + w], r[:, a:a + w], wc, None, ALU.mult)
                        else:
                            i = nc.vector.scalar_tensor_tensor(score[:, a:a + w], r[:, a:a + w], wc, score[:, a:a + w], ALU.mult, ALU.add)
                    i.then_inc(ix_d, 1)

            def select(rnd):
                s1, s0 = score[:, 0:256], score[:, 256:384]
                if rnd == 0:
                    dve.wait_ge(ix_d, IDX_HEADS)
                    dve.wait_ge(aux_in, 32)
                    chain(nc.vector.tensor_tensor(score, score, lim, ALU.min))
                nc.vector.max(top1, s1)
                chain(nc.vector.max(top0, s0))
                nc.vector.match_replace(s1, top1, s1, LOWEST)
                chain(nc.vector.match_replace(s0, top0, s0, LOWEST))
                if rnd == TOPK // 8 - 1:
                    chain(nc.vector.tensor_scalar(sel_mask, score, LOWEST, NEG, ALU.not_equal, ALU.mult))

            for b in range(1, 11):
                o, q = (0 if b < AB_POOL else O2), Q_AB + b
                if b == AB_POOL:
                    pool_scaled(0)
                    pool_lo(0)
                    split_lo(dve, q, (6,))
                    pool_sums(1)
                    split_lo(dve, q, (7,))
                    pool_means(1)
                if b == AB_POOL + 1:
                    pool_scaled(1)
                    pool_lo(1)
                if b == AB_POOL + 2:
                    index_step(8)
                for x in range(8 if b < 10 else 6):
                    if b == AB_POOL + 1:
                        index_step(x)
                    split_lo(dve, q, (o + 6 + x,))
                    if b == AB_POOL + 3:
                        select(x)
                if b == 3:
                    index_rows()
                    pool_sums(0)
                    pool_means(0)

            def store_m(used, u, par, b, add):
                dve.wait_ge(chunk_used, used)
                dve.wait_ge(acc_free, u)
                o = macc[:, :, BW * b:BW * (b + 1)]
                if add:
                    i = nc.vector.tensor_tensor(o, acc(par), o, ALU.add)
                else:
                    i = nc.vector.tensor_copy(o, acc(par))
                i.then_inc(acc_free, 1)

            def normed(k, n, m0, b, sem_, tt_last=True):
                dve.wait_ge(merged, m0 + b + 1)
                o = xres[:, :, BW * b:BW * (b + 1)]
                for tt in range(2):
                    i = nc.vector.scalar_tensor_tensor(o[:, tt, :], macc[:, tt, BW * b:BW * (b + 1)], ST["rstd"][:, tt:tt + 1],
                                                       o[:, tt, :], ALU.mult, ALU.add)
                i.then_inc(sem_, 1)

            def new_x(q, o, k, n, m0, t, gain):
                mean_square(n, ST["mean"], ssp)
                inverse(k, ST["rstd"], ST["root"])
                dve.wait_ge(stat_v, 2 * k + 2)
                for b in range(5):
                    if b < 4:
                        normed(k, n, m0, b, rows_ready)
                    if b > 0:
                        turn_lo(dve, t + b - 1, tiles(lh, 4 * b - 4), gain[:, 4 * b - 4:4 * b])
                    if 1 < b < 4:
                        split_lo(dve, q, (o + 2 * b, o + 2 * b + 1))
                mean_square(n + 8, ST["mean"], ssp)
                inverse(k + 1, ST["rstd"], ST["root"])

            def mixer_out(q, o, u, us, n, g, parts):
                def out_amid(i):
                    done = amid(AMID_OUT, i - 1)
                    if i > 0 and done % 4 == 0 and done > amid(AMID_OUT, i - 2):
                        dve.wait_ge(chunk_used, 8 * q + o + done)
                        nc.vector.tensor_copy(parts[done // 4 - 1], acc(0)).then_inc(acc_free, 1)
                    split_lo(dve, q, range(o + (SPLIT if i == 0 else split_to(AMID_OUT, i - 1)), o + split_to(AMID_OUT, i)))

                dve_attend(dve, us, n, g, TD, chain, out_amid)
                out_amid(HEADS + 4)
                at = split_to(AMID_OUT, HEADS + 4)
                for b, end in enumerate(OUT_ENDS):
                    split_lo(dve, q, range(o + at, o + end + SPLIT))
                    at = end + SPLIT
                    dve.wait_ge(chunk_used, 8 * q + o + end)
                    dve.wait_ge(acc_free, u + 3 + b)
                    to, a = macc[:, :, BW * b:BW * (b + 1)], acc((3 + b) % 2)
                    if b == 0:
                        nc.vector.tensor_copy(to, a).then_inc(acc_free, 1)
                    else:
                        nc.vector.tensor_tensor(to, a, parts[b - 1], ALU.add).then_inc(acc_free, 1)

            def ffn(q, o, u, t, c0, layer, end):
                dve.wait_ge(gain_in, 16 * (4 + 4 * layer))
                for g in range(2):
                    for j in range(4):
                        for val in range(2):
                            b = 12 * g + 2 * j + val
                            tn, cn = t + 8 * g + 2 * j + val, c0 + 8 * g + 2 * j + val
                            split_lo(dve, q + b, range(o + 8, o + 14))
                            dst = cv if val else cg
                            dve.wait_ge(thi_done, tn + 1)
                            for n in (1, 2):
                                for x in range(4):
                                    k = conv_tiles(g, j, val) + x
                                    i = nc.vector.scalar_tensor_tensor(dst[:, x, n:], tp4[:, x, 0:TOK - n], fcw[:, 2 - n, k:k + 1],
                                                                       dst[:, x, n:], ALU.mult, ALU.add)
                                if n == 1:
                                    i.then_inc(conv_a, 1)
                                    dve.wait_ge(conv_a, cn + 1)
                            i.then_inc(lhs_ready, 1)
                            if val:
                                n = (cn + 1) // 2
                                dve.wait_ge(conv_m, n)
                                dve.wait_ge(lhs_ready, tn + 1)
                                nc.vector.tensor_tensor(cg, cg, cv, ALU.mult).then_inc(conv_ready, 1)
                            split_lo(dve, q + b, (o + 14, o + 15))
                            if val:
                                dve.wait_ge(hid_hi, n)
                                nc.vector.tensor_tensor(mh[1][:, 4 * j:4 * j + 4, :], cg, mh[0][:, 4 * j:4 * j + 4, :].bitcast(F32),
                                                        ALU.subtract).then_inc(hid_ready, 1)
                    for b in range(4):
                        x = q + 12 * g + 8 + b
                        if not (end and g == 1 and b == 3):
                            split_lo(dve, x, range(o + 8, o + 12))
                        store_m(8 * x + o + 8, u + 12 * g + 8 + b, (u + b) % 2, b, g == 1)
                        if g == 0 or b < 3:
                            split_lo(dve, x, range(o + 12, o + 16))

            mixer_out(Q_ABO, O2, U_ABO, ud, N_D, G_D, parts_d)
            new_x(Q_F0, O2, 4, 40, 13, T_ABX, gains("ffn_pre"))
            ffn(Q_F0, O2, U_F0, T_F0, 0, 0, False)
            new_x(Q_CD, O2, 6, 56, 17, T_FX, gains("mix_pre", 1))
            def tap(c, n):
                a = PACK["lru_w"] + 8 * c + n
                return pk[:, a:a + 1]

            def conv(g, c):
                for n in range(4 * g, 4 * g + 4):
                    if c == 0:
                        a = PACK["lru_b"] + n
                        i = nc.vector.tensor_scalar(xc[:, n, :], xin[:, n, 0:TOK], tap(0, n), pk[:, a:a + 1], ALU.mult, ALU.add)
                    else:
                        i = nc.vector.scalar_tensor_tensor(xc[:, n, :], xin[:, n, c:c + TOK], tap(c, n), xc[:, n, :], ALU.mult, ALU.add)
                if c < 3:
                    chain(i)
                elif g == 1:
                    i.then_inc(lru_v, 1)

            def angles():
                dve.wait_ge(aux_in, 80)
                chain(nc.vector.tensor_copy(pos_f, pos_i[:]))
                for tt in range(2):
                    i = nc.vector.tensor_scalar(ang[:, tt, :], freq_sb, pos_f[:, tt:tt + 1], None, ALU.mult)
                chain(i)
                chain(nc.vector.tensor_scalar(revs, ang, 1.0 / TWO_PI, ROUNDER, ALU.mult, ALU.add))
                chain(nc.vector.tensor_scalar(revs, revs, ROUNDER, None, ALU.subtract))
                for part in TURN_PARTS:
                    chain(nc.vector.scalar_tensor_tensor(ang, revs, -part, ang, ALU.mult, ALU.add))
                nc.vector.tensor_scalar(ang, ang, PI_BELOW, -PI_BELOW, ALU.min, ALU.max).then_inc(rope_v, 1)

            nc.vector.memset(xin[:, :, 0:3], 0.0)
            for b in range(6):
                q, o = Q_CD + b, O2 if b < CD_LRU else O4
                if b == CD_LRU:
                    split_lo(dve, q, (o + 4, o + 5))
                for x in range(2 if b == 0 else 0, 8 if b < 5 else 6):
                    split_lo(dve, q, (o + 6 + x,))
                    if x == 2 and 0 < b < 5:
                        dve.wait_ge(thi_done, T_CD + b)
                        dve.sem_inc(lhs_ready, 1)
                    if x == 2 and b == 5:
                        turn_lo(dve, T_CQ, tiles(mh, 8), pk[:, PACK["q_norm"]:PACK["q_norm"] + 4])
                    if x >= 4 and b in (1, 2):
                        conv(b - 1, x - 4)
                    if (b, x) == (CD_LRU, 7):
                        angles()
                    if b == 5 and x == 3:
                        dve.wait_ge(lru_a, 6)
                        chain(nc.vector.tensor_tensor(mul, decay_a, decay_a, ALU.mult))
                    if b == 5 and x == 4:
                        nc.vector.scalar_tensor_tensor(mul, mul, 1.0, rr, ALU.add, ALU.mult).then_inc(lru_v, 1)
            turn_lo(dve, T_CQ + 1, tiles(mh, 12), pk[:, PACK["kv_norm"]:PACK["kv_norm"] + 2], n=2)
            dve.wait_ge(squares_done, 68)
            nc.vector.tensor_scalar(ST["mean"], ssp[:, :, 0], 1.0 / 512, EPS, ALU.mult, ALU.add)
            nc.vector.tensor_scalar(ST["mean2"], ssp[:, :, 1], 1.0 / 256, EPS, ALU.mult, ALU.add).then_inc(stat_v, 1)
            dve.wait_ge(stat_a, 9)
            nc.vector.reciprocal(ST["rq"], ST["root"])
            nc.vector.reciprocal(ST["rkv"], ST["root2"]).then_inc(stat_v, 1)
            split_lo(dve, Q_UP, (O4 + 4,))
            dve.wait_ge(lru_a, 7)
            dve.wait_ge(lru_p, 1)
            chain(nc.vector.tensor_tensor(ii, ii, mul, ALU.mult))
            for n in range(LRU_T):
                if n % 2 == 0:
                    split_lo(dve, Q_UP, (O4 + 5 + n // 2,))
                i = nc.vector.tensor_tensor_scan(xc[:, n, :], decay_a[:, n, :], ii[:, n, :], 0.0, ALU.mult, ALU.add)
            chain(i)
            split_lo(dve, Q_UP, (O4 + 9,))
            nc.vector.tensor_tensor(xc, xc, gy, ALU.mult).then_inc(lru_v, 1)
            split_lo(dve, Q_UP, range(O4 + 10, O4 + 14))
            dve.wait_ge(rope_a, 1)
            chain(nc.vector.tensor_tensor(cosv, half, half, ALU.mult))
            chain(nc.vector.tensor_scalar(cosv, cosv, -2.0, 1.0, ALU.mult, ALU.add))

            def rotate(x1, x2, c, s, t1, t2, y1, y2, done):
                nc.vector.tensor_tensor(t1, x1, c, ALU.mult)
                chain(nc.vector.tensor_tensor(t2, x2, s, ALU.mult))
                chain(y1(t1, t2, ALU.subtract))
                nc.vector.tensor_tensor(t1, x2, c, ALU.mult)
                chain(nc.vector.tensor_tensor(t2, x1, s, ALU.mult))
                y2(t1, t2, ALU.add).then_inc(done, 1)

            kd = kr2.rearrange("p t (a c) -> p t a c", a=2)
            k1, k2 = zc[:, :, 768:800], zc[:, :, 800:832]

            def twice(a):
                return a.unsqueeze(2).to_broadcast([P, 2, 2, 32])

            rotate(k1, k2, cosv, sinv, rq1[:, :, 0, :], rq2[:, :, 0, :],
                   lambda a, b, op: nc.vector.tensor_tensor(kd[:, :, :, 0:32], twice(a), twice(b), op),
                   lambda a, b, op: nc.vector.tensor_tensor(kd[:, :, :, 32:64], twice(a), twice(b), op), rope_v)
            dve.wait_ge(rope_v, 2)
            dve.wait_ge(acc_free, U_UP + 3)
            zh = zq.rearrange("p t (h c) -> p t h c", h=HEADS)

            def heads(a):
                return a.unsqueeze(2).to_broadcast([P, 2, HEADS, 32])

            rotate(zh[:, :, :, 128:160], zh[:, :, :, 160:192], heads(cosv), heads(sinv), rq1, rq2,
                   lambda a, b, op: nc.vector.tensor_tensor(qrow[:, :, :, 0:32], a, b, op),
                   lambda a, b, op: nc.vector.tensor_tensor(qrow[:, :, :, 32:64], a, b, op), rope_v)
            dve.wait_ge(lru_a, 8)
            nc.vector.tensor_tensor(mh[1][:, 8:16, :], xc, mh[0][:, 8:16, :].bitcast(F32), ALU.subtract).then_inc(lru_v, 1)
            for n in range(2):
                dve.wait_ge(thi_done, T_QR + n + 1)
                dve.sem_inc(lhs_ready, 1)
            mixer_out(Q_CDO, O6, U_CDO, um, N_L, G_L, parts_m)
            new_x(Q_F1, O6, 9, 76, 21, T_CDX, gains("ffn_pre", 1))
            ffn(Q_F1, O6, U_F1, T_F1, 16, 1, True)
            mean_square(92, ST["mean"], ssp)
            inverse(11, ST["rstd"], ST["root"])
            dve.wait_ge(stat_v, 24)
            for b in range(4):
                normed(11, 92, 25, b, out_ready)




def layout(inputs):
    a = {k: np.asarray(v) for k, v in inputs.items()}

    def cols(v):
        return np.ascontiguousarray(v.reshape(-1, P).T)

    t = dict(shape_tables())
    t["x"] = a["x"].reshape(TOK, D)
    t["w_in"] = a["w_in"][0]
    t["w_branch"] = a["w_branch"][0]
    t["w_out"] = a["w_out"][0]
    t["w_mlp_in"] = a["w_mlp_in"][0]
    t["w_mlp_out"] = a["w_mlp_out"][0]
    t["cmp_w1"] = a["cmp_w1"][0]
    t["cmp_w2"] = a["cmp_w2"][0]
    t["cmp_pos"] = np.ascontiguousarray(a["cmp_pos"][0].transpose(2, 0, 1).reshape(P, 64))
    t["swa_sinks"] = a["swa_sinks"]
    t["rel_bias"] = a["rel_bias"]
    t["norm_final"] = a["norm_final"].reshape(1, D)
    t["pack"] = np.concatenate([cols(v) for v in (
        a["norm_mix"], a["norm_mlp"], a["mix_pre_g_2"], a["ffn_pre_g_2"], a["q_norm_g_2"], a["kv_norm_g_2"],
        a["pool_b_2"], a["pool_scale_2"], a["lru_conv_w_2"], a["lru_conv_b_2"], a["lru_ba_2"], a["lru_bx_2"],
        a["lru_lambda_2"])], 1)
    t["mix_post"], t["ffn_post"] = a["mix_post_g_2"], a["ffn_post_g_2"]
    t["ffn_up"], t["ffn_down"] = a["ffn_up_2"], a["ffn_down_2"]
    t["ffn_conv_w"] = a["ffn_conv_w_2"].reshape(2, 3, 64, P).transpose(0, 3, 1, 2).reshape(2, P, 192)
    t["ffn_conv_b"] = a["ffn_conv_b_2"].reshape(2, 64, P).transpose(0, 2, 1)
    t["ab_w_in"], t["ab_w_out"] = a["ab_w_in_2"][0], a["ab_w_out_2"][0]
    t["pool_w"] = a["pool_w_2"].reshape(1024, 256)
    t["cd_w_in"], t["cd_w_out"] = a["cd_w_in_2"][0], a["cd_w_out_2"][0]
    t["w_q_up"], t["w_kv_up"] = a["w_q_up_2"][0], a["w_kv_up_2"][0]
    t["lru_wa"], t["lru_wx"] = a["lru_wa_2"].reshape(1024, P), a["lru_wx_2"].reshape(1024, P)
    t["positions"] = a["positions_2"].reshape(2, P).T
    return {k: np.ascontiguousarray(v) for k, v in t.items()}


def kernel(**inputs):
    import concourse.bacc as bacc
    from concourse.bass_utils import run_bass_kernel_spmd

    nc = bacc.Bacc("TRN2", target_bir_lowering=False, num_devices=1)
    arrays = layout(inputs)
    d = {n: nc.dram_tensor(n, a.shape, mybir.dt.from_np(a.dtype), kind="ExternalInput").ap() for n, a in arrays.items()}
    d["out"] = nc.dram_tensor("out", (TOK, D), F32, kind="ExternalOutput").ap()
    build_program(nc, d)
    r = run_bass_kernel_spmd(nc, [arrays], core_ids=[0])
    return r.results[0]["out"].reshape(1, TOK, D)
```
